# Optimizing a Trainium2 kernel written in Bass

```python
import math
import jax, jax.numpy as jnp
from jax import lax
import numpy as np

D_MODEL = 1024
BATCH = 1
SEQ = 512
DEPTH = 2

CTX_LEN = 256
GRID_W = 64
EPS = 1e-6

A_HEADS = 4
A_QK_DIM = 64
A_V_DIM = 2 * A_QK_DIM
A_WIDTH = A_HEADS * A_V_DIM
ROPE_FREQS = A_QK_DIM // 4
ROPE_BASE = 10000.0
Q_BLOCK = 128

B_WIDTH = D_MODEL - A_WIDTH
B_GROUPS = 4
B_GROUP_CH = B_WIDTH // B_GROUPS
B_CHUNK = 128

EV_IN = 3 * A_WIDTH + 2 * B_WIDTH
EV_SPLITS = [A_WIDTH, 2 * A_WIDTH, 3 * A_WIDTH, 3 * A_WIDTH + B_WIDTH]

CONV_WIDTH = 31

N_KEYS = 128
N_EXPERTS = N_KEYS * N_KEYS
PEER_HEADS = 8
PEER_KEY_DIM = 128
PEER_TOPK = 16
PEER_TOKEN_BLOCK = 128

N_EVEN = (DEPTH + 1) // 2
N_ODD = DEPTH // 2

kernel_name = "hybrid_diffattn_gmlp_conformer_peer_dit"

def rms_norm(x):
    xf = x.astype(jnp.float32)
    return (xf * lax.rsqrt(jnp.mean(xf * xf, axis=-1, keepdims=True) + EPS)).astype(x.dtype)

def layer_norm(x, g, b):
    xf = x.astype(jnp.float32)
    mu = jnp.mean(xf, axis=-1, keepdims=True)
    var = jnp.mean(jnp.square(xf - mu), axis=-1, keepdims=True)
    return ((xf - mu) * lax.rsqrt(var + EPS)).astype(x.dtype) * g + b

def modulate(h, shift, scale):
    return rms_norm(h) * (1.0 + scale) + shift

def axial_rope(n_tokens):
    rows = n_tokens // GRID_W
    r = jnp.repeat(jnp.arange(rows, dtype=jnp.float32), GRID_W)
    col = jnp.tile(jnp.arange(GRID_W, dtype=jnp.float32), rows)
    inv = ROPE_BASE ** (-jnp.arange(ROPE_FREQS, dtype=jnp.float32) / ROPE_FREQS)
    ang = jnp.stack([r[:, None] * inv, col[:, None] * inv], axis=1)
    return jnp.cos(ang), jnp.sin(ang)

def apply_rope(x, cos, sin):
    xr = x.reshape(x.shape[:-1] + (2, 2, ROPE_FREQS))
    x1, x2 = xr[..., 0, :], xr[..., 1, :]
    cs = cos[None, :, None, None].astype(x.dtype)
    sn = sin[None, :, None, None].astype(x.dtype)
    out = jnp.stack([x1 * cs - x2 * sn, x1 * sn + x2 * cs], axis=-2)
    return out.reshape(x.shape)

def diff_attend(q, k, v, lam):
    s = jnp.einsum('bqhcd,bkhcd->bhcqk', q, k).astype(jnp.float32) * (A_QK_DIM ** -0.5)
    p = jax.nn.softmax(s, axis=-1)
    w = (p[:, :, 0] - lam * p[:, :, 1]).astype(v.dtype)
    return jnp.einsum('bhqk,bkhe->bqhe', w, v)

def spatial_gating(u, v, vn_g, vn_b, sgu_w, sgu_b):
    bsz, n, _ = v.shape
    v = layer_norm(v, vn_g, vn_b).reshape(bsz, n // B_CHUNK, B_CHUNK, B_GROUPS, B_GROUP_CH)
    mixed = jnp.einsum('gpq,bnqgc->bnpgc', sgu_w, v) + sgu_b.T[:, :, None]
    return u * mixed.reshape(bsz, n, B_WIDTH)

def even_mixer(h_lat, h_ctx, ctx_full, lam_init, w_in, w_out, q_gain, k_gain, lam_p, subln_g,
               vn_g, vn_b, sgu_w, sgu_b, cos, sin):
    bsz, n_lat, _ = h_lat.shape
    n_ctx = h_ctx.shape[1]
    lam_f = lam_p.astype(jnp.float32)
    lam = jnp.exp(jnp.sum(lam_f[0] * lam_f[1])) - jnp.exp(jnp.sum(lam_f[2] * lam_f[3])) + lam_init

    def heads(t, n):
        return t.reshape(bsz, n, A_HEADS, 2, A_QK_DIM)

    q, k, v, u, vg = jnp.split(h_lat @ w_in, EV_SPLITS, axis=-1)
    q = apply_rope(rms_norm(heads(q, n_lat)) * q_gain, cos, sin)
    k = apply_rope(rms_norm(heads(k, n_lat)) * k_gain, cos, sin)
    v = v.reshape(bsz, n_lat, A_HEADS, A_V_DIM)
    if ctx_full:
        qc, kc, vc, uc, vgc = jnp.split(h_ctx @ w_in, EV_SPLITS, axis=-1)
    else:
        kc, vc = jnp.split(h_ctx @ w_in[:, A_WIDTH:3 * A_WIDTH], 2, axis=-1)
    kc = rms_norm(heads(kc, n_ctx)) * k_gain
    vc = vc.reshape(bsz, n_ctx, A_HEADS, A_V_DIM)
    k_all = jnp.concatenate([kc, k], axis=1)
    v_all = jnp.concatenate([vc, v], axis=1)

    qb = q.reshape(bsz, n_lat // Q_BLOCK, Q_BLOCK, A_HEADS, 2, A_QK_DIM).swapaxes(0, 1)
    o = lax.map(lambda qi: diff_attend(qi, k_all, v_all, lam), qb)
    o = o.swapaxes(0, 1).reshape(bsz, n_lat, A_HEADS, A_V_DIM)

    def finish(o_att, u_, vg_, n):
        a = (rms_norm(o_att) * subln_g * (1.0 - lam_init)).reshape(bsz, n, A_WIDTH)
        g = spatial_gating(u_, vg_, vn_g, vn_b, sgu_w, sgu_b)
        return jnp.concatenate([a, g], axis=-1) @ w_out

    y_lat = finish(o, u, vg, n_lat)
    y_ctx = None
    if ctx_full:
        qc = rms_norm(heads(qc, n_ctx)) * q_gain
        y_ctx = finish(diff_attend(qc, kc, vc, lam), uc, vgc, n_ctx)
    return y_lat, y_ctx

def conformer_conv(h, pw1_w, pw1_b, dw_w, dw_b, ln_g, ln_b, pw2_w, pw2_b):
    a, g = jnp.split(h @ pw1_w + pw1_b, 2, axis=-1)
    z = a * jax.nn.sigmoid(g)
    pad = CONV_WIDTH // 2
    z = lax.conv_general_dilated(z, dw_w[:, None, :], window_strides=(1,), padding=[(pad, pad)],
                                 dimension_numbers=('NWC', 'WIO', 'NWC'),
                                 feature_group_count=D_MODEL) + dw_b
    z = jax.nn.silu(layer_norm(z, ln_g, ln_b))
    return z @ pw2_w + pw2_b

def peer_ffn(h, wq, keys, w_down, w_up):
    shape = h.shape
    hb = h.reshape(-1, PEER_TOKEN_BLOCK, D_MODEL)

    def block(xb):
        n = xb.shape[0]
        q = (xb @ wq).reshape(n, PEER_HEADS, 2, PEER_KEY_DIM)
        s = jnp.einsum('nhpd,hpkd->nhpk', q, keys).astype(jnp.float32)
        v1, i1 = lax.top_k(s[:, :, 0], PEER_TOPK)
        v2, i2 = lax.top_k(s[:, :, 1], PEER_TOPK)
        cand = (v1[..., :, None] + v2[..., None, :]).reshape(n, PEER_HEADS, PEER_TOPK * PEER_TOPK)
        cidx = (i1[..., :, None] * N_KEYS + i2[..., None, :]).reshape(n, PEER_HEADS, PEER_TOPK * PEER_TOPK)
        top_s, pos = lax.top_k(cand, PEER_TOPK)
        idx = jnp.take_along_axis(cidx, pos, axis=-1)
        g = jax.nn.softmax(top_s, axis=-1).astype(xb.dtype)
        act = jax.nn.gelu(jnp.einsum('nhkd,nd->nhk', w_down[idx], xb), approximate=False)
        return jnp.einsum('nhk,nhkd->nd', g * act, w_up[idx])

    return lax.map(block, hb).reshape(shape)

def setup_inputs(seed: int = 0) -> dict:
    key = jax.random.key(seed)
    ks = iter(jax.random.split(key, 32))

    def nrm(shape, scale):
        return jax.random.normal(next(ks), shape, jnp.float32) * scale

    D = D_MODEL
    return {
        'x': nrm((BATCH, SEQ, D), 1.0),
        'c': nrm((BATCH, D), 1.0),
        'ctx': nrm((BATCH, CTX_LEN, D), 1.0),
        'c_ctx': nrm((D,), 1.0),
        'ada_w': nrm((DEPTH, D, 6 * D), D ** -0.5),
        'ada_b': nrm((DEPTH, 6 * D), 0.02),
        'ev_w_in': nrm((N_EVEN, D, EV_IN), D ** -0.5),
        'ev_w_out': nrm((N_EVEN, A_WIDTH + B_WIDTH, D), (A_WIDTH + B_WIDTH) ** -0.5),
        'ev_q_gain': 1.0 + nrm((N_EVEN, A_QK_DIM), 0.05),
        'ev_k_gain': 1.0 + nrm((N_EVEN, A_QK_DIM), 0.05),
        'ev_lam': nrm((N_EVEN, 4, A_QK_DIM), 0.1),
        'ev_subln_g': 1.0 + nrm((N_EVEN, A_V_DIM), 0.05),
        'ev_vnorm_g': 1.0 + nrm((N_EVEN, B_WIDTH), 0.05),
        'ev_vnorm_b': nrm((N_EVEN, B_WIDTH), 0.02),
        'ev_sgu_w': nrm((N_EVEN, B_GROUPS, B_CHUNK, B_CHUNK), B_CHUNK ** -0.5),
        'ev_sgu_b': 1.0 + nrm((N_EVEN, B_GROUPS, B_CHUNK), 0.05),
        'od_pw1_w': nrm((N_ODD, D, 2 * D), D ** -0.5),
        'od_pw1_b': nrm((N_ODD, 2 * D), 0.02),
        'od_dw_w': nrm((N_ODD, CONV_WIDTH, D), CONV_WIDTH ** -0.5),
        'od_dw_b': nrm((N_ODD, D), 0.02),
        'od_ln_g': 1.0 + nrm((N_ODD, D), 0.05),
        'od_ln_b': nrm((N_ODD, D), 0.02),
        'od_pw2_w': nrm((N_ODD, D, D), D ** -0.5),
        'od_pw2_b': nrm((N_ODD, D), 0.02),
        'peer_wq': nrm((DEPTH, D, PEER_HEADS * 2 * PEER_KEY_DIM), D ** -0.5),
        'peer_keys': nrm((DEPTH, PEER_HEADS, 2, N_KEYS, PEER_KEY_DIM), PEER_KEY_DIM ** -0.5),
        'peer_down': nrm((DEPTH, N_EXPERTS, D), D ** -0.5),
        'peer_up': nrm((DEPTH, N_EXPERTS, D), PEER_HEADS ** -0.5),
    }

def reference(x, c, ctx, c_ctx, ada_w, ada_b, ev_w_in, ev_w_out, ev_q_gain, ev_k_gain, ev_lam,
              ev_subln_g, ev_vnorm_g, ev_vnorm_b, ev_sgu_w, ev_sgu_b, od_pw1_w, od_pw1_b, od_dw_w,
              od_dw_b, od_ln_g, od_ln_b, od_pw2_w, od_pw2_b, peer_wq, peer_keys, peer_down, peer_up):
    cos, sin = axial_rope(x.shape[1])
    last_read = 2 * (N_EVEN - 1)
    silu_c = jax.nn.silu(c)
    silu_cc = jax.nn.silu(c_ctx)
    for l in range(DEPTH):
        sh1, sc1, g1, sh2, sc2, g2 = jnp.split((silu_c @ ada_w[l] + ada_b[l])[:, None, :], 6, axis=-1)
        ctx_live = l < last_read
        if ctx_live:
            csh1, csc1, cg1, csh2, csc2, cg2 = jnp.split(silu_cc @ ada_w[l] + ada_b[l], 6, axis=-1)
        elif l == last_read:
            csh1, csc1 = jnp.split(silu_cc @ ada_w[l, :, :2 * D_MODEL] + ada_b[l, :2 * D_MODEL], 2, axis=-1)
        h = modulate(x, sh1, sc1)
        if l % 2 == 0:
            e = l // 2
            lam_init = 0.8 - 0.6 * math.exp(-0.3 * l)
            y, y_c = even_mixer(h, modulate(ctx, csh1, csc1), ctx_live, lam_init, ev_w_in[e], ev_w_out[e],
                                ev_q_gain[e], ev_k_gain[e], ev_lam[e], ev_subln_g[e], ev_vnorm_g[e],
                                ev_vnorm_b[e], ev_sgu_w[e], ev_sgu_b[e], cos, sin)
        else:
            o = l // 2
            conv_p = (od_pw1_w[o], od_pw1_b[o], od_dw_w[o], od_dw_b[o], od_ln_g[o], od_ln_b[o],
                      od_pw2_w[o], od_pw2_b[o])
            y = conformer_conv(h, *conv_p)
            y_c = conformer_conv(modulate(ctx, csh1, csc1), *conv_p) if ctx_live else None
        x = x + g1 * y
        x = x + g2 * peer_ffn(modulate(x, sh2, sc2), peer_wq[l], peer_keys[l], peer_down[l], peer_up[l])
        if ctx_live:
            ctx = ctx + cg1 * y_c
            ctx = ctx + cg2 * peer_ffn(modulate(ctx, csh2, csc2), peer_wq[l], peer_keys[l],
                                       peer_down[l], peer_up[l])
    return x


_drawn_inputs = setup_inputs


def setup_inputs(seed=0):
    import zlib

    import numpy as np

    out = dict(_drawn_inputs(seed))
    spreads = {}
    factors = {'ev_q_gain': 4.748,
     'ev_k_gain': 4.454,
     'ev_vnorm_b': 3.445,
     'od_pw1_b': 6.762,
     'od_dw_b': 4.88,
     'od_ln_g': 3.077,
     'od_ln_b': 6.589,
     'od_pw2_b': 4.6}
    for name, (base, spread) in spreads.items():
        noise = np.random.default_rng([zlib.crc32(name.encode()), seed]).standard_normal(out[name].shape)
        drawn = base * np.exp(spread * noise) if base else spread * noise
        out[name] = __import__('jax').numpy.asarray(drawn.astype(out[name].dtype))
    for name, factor in factors.items():
        out[name] = (out[name] * factor).astype(out[name].dtype)
    return out
```

```python
from contextlib import ExitStack

import numpy as np

import concourse.bass as bass
from concourse import mybir

F32 = mybir.dt.float32
U32 = mybir.dt.uint32
ALU = mybir.AluOpType
ACT = mybir.ActivationFunctionType
AX = mybir.AxisListType

P = 128
D = 1024
KD = D // P
SEQ = 512
CTX = 256
NB = SEQ // P
NT = (SEQ + CTX) // P
LAYERS = 2
EPS = 1e-6
COLS = 512

HEADS = 4
QK = 64
VD = 128
KEYS = SEQ + CTX
LAM_INIT = 0.8 - 0.6
SCALE = QK ** -0.5
GROUPS = 4

TAPS = 31
PAD = TAPS // 2

N_KEYS = 128
PH = 8
TOPK = 16
SLOTS_PER_BLOCK = PH * TOPK
N_EXPERTS = N_KEYS * N_KEYS
LOW = -3.0e38

RING = 8
GROUP = 2
NG = RING // GROUP
ITERS = SLOTS_PER_BLOCK // RING

ADA_CH = [0, 12]
Q_CH, K_CH, V_CH, U_CH, VG_CH = 24, 25, 26, 27, 28
OUT_CH = 29
PW1_CH = 31
PW2_CH = 35
WQ_CH = [37, 41]
KEY_CH = 45
N_CHUNKS = 46
ADA_BIAS = [0, 12]
PW1_BIAS = 24
PW2_BIAS = 28
N_BIAS = 30

SH1, SC1, G1, SH2, SC2, G2 = range(6)


class Tile:

    def __init__(self, bank, frees_before, full_after):
        self.bank, self.frees_before, self.full_after = bank, frees_before, full_after


class Chunk:

    def __init__(self, source, buf, landed, bias):
        self.source, self.buf, self.landed, self.bias, self.last_use = source, buf, landed, bias, None


class Stage:

    def __init__(self, kind, layer=None, b=None, name=None, tiles=None, which=None, src=None, dest=None, out_t=None,
                 mods=None, parts=None):
        self.kind, self.layer, self.b, self.name, self.tiles, self.which = kind, layer, b, name, tiles, which
        self.src, self.dest, self.out_t, self.mods, self.parts = src, dest, out_t, mods, parts


class Plan:

    DUOS = 3
    BUFS = 2

    def __init__(self):
        self.uses = [0] * self.DUOS
        self.fulls = [0] * self.DUOS
        self.n = 0
        self.chunks = []
        self.landed = [0] * self.BUFS
        self.counts = {}
        self.stages = []

    def tile(self, parts=1):
        d = self.n % self.DUOS
        self.n += 1
        t = Tile(d, self.uses[d], [self.fulls[d] + i + 1 for i in range(parts)])
        self.uses[d] += 1
        self.fulls[d] += parts
        return t

    def chunk(self, source, bias=None):
        b = len(self.chunks) % self.BUFS
        self.landed[b] += 16 if bias is None else 32
        c = Chunk(source, b, self.landed[b], bias)
        self.chunks.append(c)
        return c

    def used(self, chunk, tile, part):
        chunk.last_use = (tile.bank, tile.full_after[part])

    def take(self, name, k=1):
        before = self.counts.get(name, 0)
        self.counts[name] = before + k
        return before

    def so_far(self, name):
        return self.counts.get(name, 0)

    def norm(self, src, dest, out_t, mods, final=None):
        s = Stage(kind="norm", src=src, dest=dest, out_t=out_t, mods=mods)
        s.x_updates = self.so_far("x_updated")
        s.topk_before = self.so_far("topk_ready")
        s.std = self.take("std_ready")
        s.h = self.take("h_ready")
        s.ht = self.take("ht_ready")
        s.tile = self.tile()
        return s

    def ada(self, layer):
        s = Stage(kind="ada", layer=layer, parts=[])
        s.cond = self.take("cond_ready")
        s.x_updates = self.so_far("x_updated")
        for j in range(12):
            both = layer == 0 and j < 4
            c = self.chunk(ADA_CH[layer] + j, ADA_BIAS[layer] + j)
            t = self.tile(2 if both else 1)
            self.used(c, t, -1)
            s.parts.append((j, c, t, both))
        s.mod = self.take("mod_ready")
        return s

    def heads(self, name, tiles, source):
        s = Stage(kind="heads", name=name, tiles=tiles)
        s.ht = self.so_far("ht_ready")
        s.chunk = self.chunk(source)
        s.proj, s.turn = [None] * len(tiles), [None] * len(tiles)
        for n in range(len(tiles) + 1):
            if n < len(tiles):
                s.proj[n] = self.tile()
            if n:
                s.turn[n - 1] = self.tile()
        self.used(s.chunk, s.proj[-1], 0)
        s.copied = self.take("qk_copied", len(tiles))
        s.summed = self.take("qk_summed", len(tiles))
        s.std = self.take("std_ready", len(tiles))
        s.turned = self.take("qk_rotated", len(tiles))
        s.done = self.take("qkt_ready", len(tiles))
        return s

    def values(self, tiles):
        s = Stage(kind="values", tiles=tiles)
        s.ht = self.so_far("ht_ready")
        s.chunk = self.chunk(V_CH)
        s.proj = [self.tile() for _ in tiles]
        self.used(s.chunk, s.proj[-1], 0)
        s.done = self.take("v_ready")
        return s

    def gating(self, b):
        s = Stage(kind="gating", b=b)
        s.ht = self.so_far("ht_ready")
        s.u, s.vg = self.chunk(U_CH), self.chunk(VG_CH)
        s.ut, s.vt, s.mt = self.tile(), self.tile(), self.tile()
        self.used(s.u, s.ut, 0)
        self.used(s.vg, s.vt, 0)
        s.u_ready = self.take("u_ready")
        s.var = self.take("var_ready")
        s.std = self.take("std_ready")
        s.vn = self.take("vn_ready")
        return s

    def attend(self, b):
        s = Stage(kind="attend", b=b)
        s.qkt, s.v = self.so_far("qkt_ready"), self.so_far("v_ready")
        s.score, s.turn, s.out = [None] * HEADS, [None] * HEADS, [None] * HEADS
        s.score[0] = [self.tile(2), self.tile(2)]
        for h in range(HEADS):
            if h + 1 < HEADS:
                s.score[h + 1] = [self.tile(2), self.tile(2)]
            s.turn[h], s.out[h] = self.tile(), self.tile()
        s.max = self.take("max_ready", 2 * HEADS)
        s.exp = self.take("exp_ready", 2 * HEADS)
        s.mix = self.take("probs_ready", HEADS)
        s.pt = self.take("probst_ready", HEADS)
        s.o = self.take("o_ready", HEADS)
        s.ss = self.take("o_summed")
        s.std = self.take("std_ready")
        s.cat = self.take("cat_ready")
        return s

    def project(self, b, which):
        s = Stage(kind="project", b=b, which=which)
        if which == "even":
            s.cat = self.so_far("cat_ready")
            s.turn = self.tile()
            s.chunks = [self.chunk(OUT_CH + j) for j in range(2)]
        else:
            s.chunks = [self.chunk(PW2_CH + j, PW2_BIAS + j) for j in range(2)]
        s.left_before = self.so_far("left_ready")
        s.left = self.take("left_ready") if which == "even" else None
        s.tile = self.tile(2)
        for j in range(2):
            self.used(s.chunks[j], s.tile, j)
        s.x = self.take("x_updated")
        return s

    def conv_in(self, b):
        s = Stage(kind="conv_in", b=b)
        s.ht = self.so_far("ht_ready")
        order = [2, 3, 0, 1]
        s.chunks = [self.chunk(PW1_CH + j, PW1_BIAS + j) for j in order]
        s.gate, s.val, s.turn = self.tile(2), self.tile(2), self.tile()
        for j in range(4):
            self.used(s.chunks[j], s.gate if j < 2 else s.val, j % 2)
        s.sig = self.take("sig_ready")
        s.z = self.take("z_ready")
        s.zt = self.take("zt_ready")
        return s

    def conv(self, b):
        s = Stage(kind="conv", b=b)
        s.zt = self.so_far("zt_ready")
        s.there, s.back = self.tile(), self.tile()
        s.conv = self.take("conv_done")
        s.var = self.take("var_ready")
        s.std = self.take("std_ready")
        s.cn = self.take("cn_ready")
        s.left = self.take("left_ready")
        s.steps = self.take("tap_done", KD)
        return s

    def select(self, layer, b):
        s = Stage(kind="select", layer=layer, b=b)
        s.ht = self.so_far("ht_ready")
        s.chunks = [self.chunk(WQ_CH[layer] + j) for j in range(4)]
        s.q = [self.tile(2), self.tile(2)]
        for j in range(4):
            self.used(s.chunks[j], s.q[j // 2], j % 2)
        s.keys = self.chunk(KEY_CH)
        s.s = [self.tile(2), self.tile(2)]
        self.used(s.keys, s.s[1], 1)
        s.qt = self.take("pq_ready", 2)
        s.sc = self.take("scores_ready", 2)
        s.top = self.take("cand_ready")
        s.exp = self.take("gate_exp")
        s.done = self.take("topk_ready")
        return s

    def gather(self, layer, b):
        s = Stage(kind="gather", layer=layer, b=b)
        s.topk = self.so_far("topk_ready")
        s.index = layer * NB + b
        s.x = self.take("x_updated")
        return s


def make_plan():
    p = Plan()
    order = [p.ada(0)]
    for t in range(NT):
        ctx = t < CTX // P
        order.append(p.norm(("ctx", t) if ctx else ("x", t - CTX // P), "h", ("all", t), "ctx" if ctx else "mix"))
    order.append(p.heads("k", list(range(NT)), K_CH))
    order.append(p.values(list(range(NT))))
    for b in range(NB):
        order.append(p.norm(("x", b), "h", ("one", 0), "mix"))
        order.append(p.heads("q", [b + CTX // P], Q_CH))
        order.append(p.gating(b))
        order.append(p.attend(b))
        order.append(p.project(b, "even"))
        order.append(p.norm(("x", b), ("h2", b), ("one", 0), "ffn"))
        order.append(p.select(0, b))
    for b in range(NB):
        order.append(p.gather(0, b))
    order.append(p.ada(1))
    for b in range(NB):
        order.append(p.norm(("x", b), "h", ("one", 0), "mix"))
        order.append(p.conv_in(b))
    for b in range(NB):
        order.append(p.conv(b))
        order.append(p.project(b, "odd"))
        order.append(p.norm(("x", b), ("h2", b), ("one", 0), "ffn"))
        order.append(p.select(1, b))
    for b in range(NB):
        order.append(p.gather(1, b))
    p.stages = order
    return p


def trunk_kernel(nc, A, out):
    plan = make_plan()
    with ExitStack() as ctx:
        def sb(name, shape, dt=F32):
            return ctx.enter_context(nc.sbuf_tensor(name, shape, dt))

        def sem(name):
            return ctx.enter_context(nc.semaphore(name))

        x = sb("x", [P, NB, D])
        mod = sb("mod", [P, 6, D])
        ring = sb("ring", [P, RING, 2 * D])
        h2 = sb("h2", [P, NB, D])
        weights = sb("weights", [P, Plan.BUFS, KD + 1, COLS])
        arena = sb("arena", [P, 8192])
        ident = sb("ident", [P, P])
        ones_row = sb("ones_row", [1, P])
        zero_row = sb("zero_row", [1, P])
        eps = sb("eps", [P, 1])
        iota16 = sb("iota16", [P, TOPK])
        cond = sb("cond", [P, 2, KD])
        cond_silu = sb("cond_silu", [P, 2, KD])
        rope_cos = sb("rope_cos", [P, NB, QK])
        rope_sin = sb("rope_sin", [P, NB, QK])
        gains = sb("gains", [P, 2, QK])
        subln = sb("subln", [P, VD])
        sgu_t = sb("sgu_t", [P, GROUPS, P])
        sgu_bias = sb("sgu_bias", [P, GROUPS])
        taps = sb("taps", [P, KD, TAPS])
        conv_par = sb("conv_par", [P, 3, KD])
        neg_lam = sb("neg_lam", [P, 1])
        sumsq = sb("sumsq", [P, 8])
        std = sb("std", [P, 8])
        rstd = sb("rstd", [P, 8])
        stats = sb("stats", [P, 2, 6])
        meanvar = sb("meanvar", [P, 2])
        peak = sb("peak", [P, 2, 2])
        neg_peak = sb("neg_peak", [P, 2, 2])
        expsum = sb("expsum", [P, 2, 2])
        inv_sum = sb("inv_sum", [P, 2, 2])
        top_v = sb("top_v", [P, 2 * PH, TOPK])
        top_i = sb("top_i", [P, 2 * PH, TOPK], U32)
        best_v = sb("best_v", [P, PH, TOPK])
        best_p = sb("best_p", [P, PH, TOPK], U32)
        gate_sum = sb("gate_sum", [P, PH])
        expert = sb("expert", [P, NB, SLOTS_PER_BLOCK], U32)
        gate = sb("gate", [P, NB, SLOTS_PER_BLOCK])
        staged = sb("staged", [P, RING], U32)
        dots = sb("dots", [P, RING])
        acts = sb("acts", [P, RING])
        diag = sb("diag", [P, RING, P])
        psum = ctx.enter_context(nc.psum_tensor("psum", [P, 4, 2 * COLS], F32))
        ffn_out = psum[:, 3, :]

        store = ring[:].rearrange("p s n -> p (s n)")
        k_t = store[:, 0:3072].rearrange("p (h t) -> p h t", h=HEADS)
        v_all = store[:, 3072:6144].rearrange("p (t n) -> p t n", t=NT)
        ht_all = store[:, 6144:12288].rearrange("p (t k n) -> p t k n", t=NT, k=KD)
        ctx_mod = store[:, 12288:14336].rearrange("p (s n) -> p s n", s=2)
        cond_b = store[:, 14336:16384].rearrange("p (s k n) -> p s k n", s=2, k=KD)
        ctx_x = h2[:, 0:2, :]
        vn_gain = h2[:, 3, :].rearrange("p (a n) -> p a n", a=2)
        ZW = SEQ + 2 * PAD
        z_t = store[:, 0:KD * ZW].rearrange("p (k t) -> p k t", k=KD)

        def at(start, n):
            return arena[:, start:start + n]

        h_tile = at(0, 1024)
        h_t = at(1024, 1024).rearrange("p (k n) -> p k n", k=KD)
        q_t = at(2048, 512).rearrange("p (h n) -> p h n", h=HEADS)
        qk_raw, qk_sq, qk_rot = at(2560, 512), at(3072, 512), at(3584, 512)
        u_tile, vn_tile = at(4096, 512), at(4608, 512)
        o_tile, o_sq = at(5120, 512), at(3584, 512)
        cat = at(5632, 1024)
        probs = [[at(0, KEYS), at(1024, KEYS)], [at(4096, KEYS), at(6656, KEYS)]]
        lam_in = at(2048, 4 * QK).rearrange("p (a n) -> p a n", a=4)
        probs_t = at(2560, 768).rearrange("p (t n) -> p t n", t=NT)
        pq_t = at(2048, 2048).rearrange("p (g n) -> p g n", g=2 * PH)
        scores = at(4096, 2048).rearrange("p (g n) -> p g n", g=2 * PH)
        cand = at(6144, 2048).rearrange("p (h n) -> p h n", h=PH)
        onehot = at(2048, 2048).rearrange("p (s n) -> p s n", n=TOPK)
        top_f = at(4096, 256).rearrange("p (g n) -> p g n", n=TOPK)
        part_u = at(4352, 256).bitcast(U32).rearrange("p (a n) -> p a n", a=2)
        part_f = at(4608, 256).rearrange("p (a n) -> p a n", a=2)
        sig, z_tile = at(2048, 1024), at(3072, 1024)
        acc = [at(4096, 1024).rearrange("p (k n) -> p k n", k=KD), at(5120, 1024).rearrange("p (k n) -> p k n", k=KD)]
        cn_tile = at(6144, 1024)
        cn_t = at(7168, 1024).rearrange("p (k n) -> p k n", k=KD)

        params = sem("params_landed")
        x_landed = sem("x_landed")
        consts = sem("consts_ready")
        landed = [sem(f"chunk_landed{i}") for i in range(Plan.BUFS)]
        full = [sem(f"psum_full{i}") for i in range(Plan.DUOS)]
        free = [sem(f"psum_free{i}") for i in range(Plan.DUOS)]
        act_step, dve_step = sem("act_step"), sem("dve_step")
        S = {n: sem(n) for n in (
            "std_ready", "h_ready", "ht_ready", "cond_ready", "mod_ready", "qk_copied", "qk_summed", "qk_rotated",
            "qkt_ready", "v_ready", "u_ready", "var_ready", "vn_ready", "max_ready", "exp_ready",
            "probs_ready", "probst_ready", "o_ready", "o_summed", "cat_ready", "left_ready", "x_updated", "sig_ready",
            "z_ready", "zt_ready", "conv_done", "cn_ready", "tap_done", "pq_ready", "scores_ready", "cand_ready",
            "gate_exp", "topk_ready")}
        lam_sum, lam_exp, cond_act = sem("lam_sum"), sem("lam_exp"), sem("cond_act")
        slot_landed = [sem(f"slot_landed{i}") for i in range(RING)]
        staged_ready, staged_seen = sem("staged_ready"), sem("staged_seen")
        dots_ready, acts_ready, diag_ready = sem("dots_ready"), sem("acts_ready"), sem("diag_ready")
        slots_free = sem("slots_free")
        tap_a, tap_b = sem("tap_a"), sem("tap_b")
        stored = sem("stored")

        N_PARAMS = 14
        block = ctx.enter_context(nc.Block())

        @block.sync
        def _(sp):
            sp.dma_start(cond[:], A["cond"]).then_inc(params, 16)
            sp.dma_start(ident[:], A["ident"]).then_inc(params, 16)

            def load_chunk(n):
                c = plan.chunks[n]
                if n >= Plan.BUFS:
                    sp.wait_ge(full[plan.chunks[n - Plan.BUFS].last_use[0]], plan.chunks[n - Plan.BUFS].last_use[1])
                sp.dma_start(weights[:, c.buf, 0:KD, :].rearrange("p k n -> p (k n)"), A["chunks"][c.source]).then_inc(
                    landed[c.buf], 16)
                if c.bias is not None:
                    sp.dma_start(weights[0:1, c.buf, KD, :], A["biases"][c.bias:c.bias + 1, :]).then_inc(
                        landed[c.buf], 16)

            load_chunk(0)
            load_chunk(1)
            sp.dma_start(iota16[:], A["iota16"]).then_inc(params, 16)
            sp.dma_start(rope_cos[:], A["rope_cos"]).then_inc(params, 16)
            sp.dma_start(rope_sin[:], A["rope_sin"]).then_inc(params, 16)
            sp.dma_start(gains[:], A["gains"].partition_broadcast(P)).then_inc(params, 16)
            sp.dma_start(lam_in[:], A["lam"].partition_broadcast(P)).then_inc(params, 16)
            sp.dma_start(subln[:], A["subln"].partition_broadcast(P)).then_inc(params, 16)
            sp.dma_start(vn_gain[:], A["vn_gain"].partition_broadcast(P)).then_inc(params, 16)
            sp.dma_start(sgu_t[:], A["sgu_t"]).then_inc(params, 16)
            sp.dma_start(sgu_bias[:], A["sgu_bias"]).then_inc(params, 16)
            sp.dma_start(taps[:], A["taps"]).then_inc(params, 16)
            sp.dma_start(conv_par[:], A["conv_par"]).then_inc(params, 16)
            sp.dma_start(ctx_x, A["ctx"].rearrange("(t p) n -> p t n", p=P)).then_inc(params, 16)
            sp.dma_start(x[:], A["x"].rearrange("(t p) n -> p t n", p=P)).then_inc(x_landed, 16)
            for n in range(2, len(plan.chunks)):
                load_chunk(n)
            n_out = 0
            for s in plan.stages:
                if s.kind == "gather" and s.layer == LAYERS - 1:
                    sp.wait_ge(S["x_updated"], s.x + 1)
                    sp.dma_start(out[s.b * P:(s.b + 1) * P, :], x[:, s.b, :]).then_inc(stored, 16)
                    n_out += 1
            sp.wait_ge(stored, 16 * n_out)

        @block.gpsimd
        def _(pool):
            table = A["experts"]
            for s in plan.stages:
                if s.kind != "gather":
                    continue
                base = s.index * ITERS * NG
                pool.wait_ge(S["topk_ready"], s.topk)
                with pool.Fori(0, ITERS) as i:
                    for g in range(NG):
                        pool.wait_ge(slots_free, i * NG + (base + g + 1))
                        pool.tensor_copy(staged[:, g * GROUP:(g + 1) * GROUP],
                                         expert[:, s.b, bass.ds(i * RING + g * GROUP, GROUP)]).then_inc(staged_ready, 1)
                        pool.wait_ge(staged_ready, i * NG + (base + g + 1))
                        pool.sem_inc(staged_seen, 1)
                        for k in range(g * GROUP, (g + 1) * GROUP):
                            pool.indirect_dma_start(
                                out=ring[:, k, :], out_offset=None, in_=table,
                                in_offset=bass.IndirectOffsetOnAxis(ap=staged[:, k:k + 1], axis=0),
                            ).then_inc(slot_landed[k], 16)

        @block.scalar
        def _(act):
            steps = [0]

            def step(ins):
                steps[0] += 1
                ins.then_inc(act_step, 1)
                act.wait_ge(act_step, steps[0])

            def tile_ap(t, n):
                return psum[:, t.bank, 0:n]

            def evacuate(dst, t, n, signal=None):
                act.wait_ge(full[t.bank], t.full_after[-1])
                act.activation(dst, tile_ap(t, n), ACT.Copy).then_inc(free[t.bank], 1)

            act.wait_ge(params, 16 * N_PARAMS)
            act.wait_ge(x_landed, 16)
            act.activation(cond_silu[:], cond[:], ACT.Silu).then_inc(cond_act, 1)
            act.wait_ge(lam_sum, 1)
            act.wait_ge(consts, 1)
            act.activation(inv_sum[:, 0, :], sumsq[:, 0:2], ACT.Exp).then_inc(lam_exp, 1)

            def signal(name, ins):
                ins.then_inc(S[name], 1)

            def norm(s):
                if s.x_updates:
                    act.wait_ge(S["x_updated"], s.x_updates)
                if s.topk_before:
                    act.wait_ge(S["topk_ready"], s.topk_before)
                act.wait_ge(S["mod_ready"], 1)
                src = ctx_x[:, s.src[1], :] if s.src[0] == "ctx" else x[:, s.src[1], :]
                dst = h_tile if s.dest == "h" else h2[:, s.dest[1], :]
                step(act.activation(dst, src, ACT.Square, accum_out=sumsq[:, 0:1]))
                signal("std_ready", act.activation(std[:, 0:1], sumsq[:, 0:1], ACT.Sqrt, bias=eps[:], scale=1.0 / D))
                t = s.tile
                act.wait_ge(full[t.bank], t.full_after[-1])
                dst = ht_all[:, s.out_t[1]] if s.out_t[0] == "all" else h_t
                step(act.activation(dst.rearrange("p k n -> p (k n)"), tile_ap(t, 1024), ACT.Copy))
                act.sem_inc(free[t.bank], 1)
                act.sem_inc(S["ht_ready"], 1)

            def heads(s):
                for n, tok in enumerate(s.tiles):
                    t = s.proj[n]
                    act.wait_ge(full[t.bank], t.full_after[0])
                    if n:
                        act.wait_ge(S["qk_rotated"], s.turned + n)
                    step(act.activation(qk_raw, tile_ap(t, 512), ACT.Copy))
                    act.sem_inc(free[t.bank], 1)
                    signal("qk_copied", act.activation(qk_sq, qk_raw, ACT.Square))
                    act.wait_ge(S["qk_summed"], s.summed + n + 1)
                    signal("std_ready", act.activation(std[:], sumsq[:], ACT.Sqrt, bias=eps[:], scale=1.0 / QK))
                    t = s.turn[n]
                    act.wait_ge(full[t.bank], t.full_after[0])
                    dst = k_t[:, :, tok * P:(tok + 1) * P] if s.name == "k" else q_t
                    step(act.activation(dst, tile_ap(t, 512).rearrange("p (h n) -> p h n", h=HEADS), ACT.Copy))
                    act.sem_inc(free[t.bank], 1)
                    act.sem_inc(S["qkt_ready"], 1)

            def values(s):
                for n, tok in enumerate(s.tiles):
                    t = s.proj[n]
                    act.wait_ge(full[t.bank], t.full_after[0])
                    ins = act.activation(v_all[:, tok, :], tile_ap(t, 512), ACT.Copy)
                    ins.then_inc(free[t.bank], 1)

            def gating(s):
                act.wait_ge(full[s.ut.bank], s.ut.full_after[0])
                step(act.activation(u_tile, tile_ap(s.ut, 512), ACT.Copy))
                act.sem_inc(free[s.ut.bank], 1)
                act.sem_inc(S["u_ready"], 1)
                act.wait_ge(S["var_ready"], s.var + 1)
                signal("std_ready", act.activation(std[:, 0:1], meanvar[:, 1:2], ACT.Sqrt, bias=eps[:]))

            def attend(s):
                def exps(h):
                    for c in range(2):
                        t = s.score[h][c]
                        act.wait_ge(full[t.bank], t.full_after[1])
                        act.wait_ge(S["max_ready"], s.max + 2 * h + c + 1)
                        step(act.activation(probs[h % 2][c], tile_ap(t, KEYS), ACT.Exp,
                                            bias=neg_peak[:, h % 2, c:c + 1], scale=SCALE,
                                            accum_out=expsum[:, h % 2, c:c + 1]))
                        act.sem_inc(free[t.bank], 1)
                        act.sem_inc(S["exp_ready"], 1)

                exps(0)
                for h in range(HEADS):
                    if h + 1 < HEADS:
                        exps(h + 1)
                    t = s.turn[h]
                    act.wait_ge(full[t.bank], t.full_after[0])
                    step(act.activation(probs_t.rearrange("p t n -> p (t n)"), tile_ap(t, KEYS), ACT.Copy))
                    act.sem_inc(free[t.bank], 1)
                    act.sem_inc(S["probst_ready"], 1)
                    t = s.out[h]
                    act.wait_ge(full[t.bank], t.full_after[0])
                    step(act.activation(o_tile[:, h * VD:(h + 1) * VD], tile_ap(t, VD), ACT.Copy))
                    act.sem_inc(free[t.bank], 1)
                    act.sem_inc(S["o_ready"], 1)
                act.wait_ge(S["o_summed"], s.ss + 1)
                signal("std_ready", act.activation(std[:, 0:HEADS], sumsq[:, 0:HEADS], ACT.Sqrt, bias=eps[:], scale=1.0 / VD))

            def project(s):
                if s.which == "even":
                    t = s.turn
                    act.wait_ge(full[t.bank], t.full_after[0])
                    step(act.activation(h_t.rearrange("p k n -> p (k n)"), tile_ap(t, 1024), ACT.Copy))
                    act.sem_inc(free[t.bank], 1)
                    act.sem_inc(S["left_ready"], 1)

            def conv_in(s):
                act.wait_ge(full[s.gate.bank], s.gate.full_after[1])
                if s.z:
                    act.wait_ge(S["z_ready"], s.z)
                step(act.activation(sig, tile_ap(s.gate, 1024), ACT.Sigmoid))
                act.sem_inc(free[s.gate.bank], 1)
                act.sem_inc(S["sig_ready"], 1)
                t = s.turn
                act.wait_ge(full[t.bank], t.full_after[0])
                step(act.activation(z_t[:, :, PAD + s.b * P:PAD + (s.b + 1) * P],
                                    tile_ap(t, 1024).rearrange("p (k n) -> p k n", k=KD), ACT.Copy))
                act.sem_inc(free[t.bank], 1)
                act.sem_inc(S["zt_ready"], 1)

            def conv(s):
                act.wait_ge(S["var_ready"], s.var + 1)
                signal("std_ready", act.activation(std[:, 0:1], meanvar[:, 1:2], ACT.Sqrt, bias=eps[:]))
                t = s.back
                act.wait_ge(full[t.bank], t.full_after[0])
                for k in range(KD):
                    ins = act.activation(cn_t[:, k, :], tile_ap(t, 1024)[:, k * P:(k + 1) * P], ACT.Silu,
                                         bias=conv_par[:, 2, k:k + 1], scale=conv_par[:, 1, k:k + 1])
                step(ins)
                act.sem_inc(free[t.bank], 1)
                act.sem_inc(S["left_ready"], 1)

            def select(s):
                for j in range(2):
                    t = s.q[j]
                    act.wait_ge(full[t.bank], t.full_after[1])
                    step(act.activation(pq_t[:, 8 * j:8 * j + 8, :].rearrange("p g n -> p (g n)"), tile_ap(t, 1024), ACT.Copy))
                    act.sem_inc(free[t.bank], 1)
                    act.sem_inc(S["pq_ready"], 1)
                for j in range(2):
                    t = s.s[j]
                    act.wait_ge(full[t.bank], t.full_after[1])
                    step(act.activation(scores[:, 8 * j:8 * j + 8, :].rearrange("p g n -> p (g n)"), tile_ap(t, 1024), ACT.Copy))
                    act.sem_inc(free[t.bank], 1)
                    act.sem_inc(S["scores_ready"], 1)
                act.wait_ge(S["cand_ready"], s.top + 1)
                bv = best_v[:].rearrange("p h n -> p (h n)")
                signal("gate_exp", act.activation(bv, bv, ACT.Exp))

            def gather(s):
                base = s.index * ITERS * NG
                with act.Fori(0, ITERS) as i:
                    for g in range(NG):
                        lo, hi = g * GROUP, (g + 1) * GROUP
                        act.wait_ge(dots_ready, i * NG + (base + g + 1))
                        act.activation(acts[:, lo:hi], dots[:, lo:hi], ACT.Gelu).then_inc(acts_ready, 1)

            for s in plan.stages:
                if s.kind != "ada":
                    {"norm": norm, "heads": heads, "values": values, "gating": gating, "attend": attend,
                     "project": project, "conv_in": conv_in, "conv": conv, "select": select, "gather": gather}[s.kind](s)

        @block.vector
        def _(dve):
            steps = [0]

            def issue(ins):
                steps[0] += 1
                ins.then_inc(dve_step, 1)

            def settle():
                dve.wait_ge(dve_step, steps[0])

            def step(ins):
                issue(ins)
                settle()

            def signal(name, ins):
                ins.then_inc(S[name], 1)

            def bc(ap, shape):
                return ap.to_broadcast(shape)

            def tile_ap(t, n):
                return psum[:, t.bank, 0:n]

            dve.memset(eps[:], EPS)
            dve.memset(ones_row[:], 1.0)
            dve.memset(zero_row[:], 0.0).then_inc(consts, 1)
            dve.wait_ge(params, 16 * N_PARAMS)
            lam_prod = qk_raw[:, 0:2 * QK].rearrange("p (a n) -> p a n", a=2)
            step(dve.tensor_tensor(lam_prod, lam_in[:, 0:4:2, :], lam_in[:, 1:4:2, :], ALU.mult))
            dve.tensor_reduce(sumsq[:, 0:2], lam_prod, AX.X, ALU.add).then_inc(lam_sum, 1)
            step(dve.tensor_scalar(subln[:], subln[:], 1.0 - LAM_INIT, None, ALU.mult))
            dve.wait_ge(lam_exp, 1)
            step(dve.scalar_tensor_tensor(out=neg_lam[:], in0=inv_sum[:, 0, 1:2], scalar=-LAM_INIT, in1=inv_sum[:, 0, 0:1],
                                     op0=ALU.add, op1=ALU.subtract))

            def ada(s):
                if s.layer == 0:
                    dve.wait_ge(cond_act, 1)
                for v in range(2):
                    for k in range(KD):
                        ins = dve.tensor_copy(cond_b[:, v, k, :], cond_silu[:, v, k:k + 1].to_broadcast([P, P]))
                        if (v, k) != (1, KD - 1):
                            issue(ins)
                signal("cond_ready", ins)
                for j, c, t, both in s.parts:
                    dve.wait_ge(full[t.bank], t.full_after[-1])
                    sec, half = j // 2, (j % 2) * COLS
                    plus = 1.0 if sec in (SC1, SC2) else 0.0
                    if both:
                        issue(dve.tensor_scalar(ctx_mod[:, sec, half:half + COLS], psum[:, t.bank, COLS:2 * COLS], plus, None, ALU.add))
                    issue(dve.tensor_scalar(mod[:, sec, half:half + COLS], psum[:, t.bank, 0:COLS], plus, None, ALU.add))
                    settle()
                    dve.sem_inc(free[t.bank], 1)
                dve.sem_inc(S["mod_ready"], 1)

            def norm(s):
                dve.wait_ge(S["std_ready"], s.std + 1)
                if s.mods == "ctx":
                    sh, sc = ctx_mod[:, 0, :], ctx_mod[:, 1, :]
                elif s.mods == "mix":
                    sh, sc = mod[:, SH1, :], mod[:, SC1, :]
                else:
                    sh, sc = mod[:, SH2, :], mod[:, SC2, :]
                src = ctx_x[:, s.src[1], :] if s.src[0] == "ctx" else x[:, s.src[1], :]
                dst = h_tile if s.dest == "h" else h2[:, s.dest[1], :]
                step(dve.reciprocal(rstd[:, 0:1], std[:, 0:1]))
                step(dve.scalar_tensor_tensor(out=dst, in0=src, scalar=rstd[:, 0:1], in1=sc, op0=ALU.mult, op1=ALU.mult))
                signal("h_ready", dve.tensor_tensor(dst, dst, sh, ALU.add))

            def heads(s):
                for n, tok in enumerate(s.tiles):
                    dve.wait_ge(S["qk_copied"], s.copied + n + 1)
                    v8 = qk_raw.rearrange("p (g n) -> p g n", n=QK)
                    signal("qk_summed", dve.tensor_reduce(sumsq[:], qk_sq.rearrange("p (g n) -> p g n", n=QK), AX.X, ALU.add))
                    dve.wait_ge(S["std_ready"], s.std + n + 1)
                    step(dve.reciprocal(rstd[:], std[:]))
                    step(dve.tensor_tensor(v8, v8, rstd[:, :, None].to_broadcast([P, 8, QK]), ALU.mult))
                    gain = gains[:, 0 if s.name == "q" else 1, None, :].to_broadcast([P, 8, QK])
                    rot = qk_rot.rearrange("p (g n) -> p g n", n=QK)
                    if n:
                        t = s.turn[n - 1]
                        dve.wait_ge(full[t.bank], t.full_after[0])
                    if tok < CTX // P:
                        signal("qk_rotated", dve.tensor_tensor(rot, v8, gain, ALU.mult))
                        continue
                    b = tok - CTX // P
                    step(dve.tensor_tensor(v8, v8, gain, ALU.mult))
                    issue(dve.tensor_tensor(rot, v8, rope_cos[:, b, None, :].to_broadcast([P, 8, QK]), ALU.mult))
                    halves = qk_raw.rearrange("p (g a r f) -> p g a r f", a=2, r=2, f=QK // 4)
                    other = qk_sq.rearrange("p (g a r f) -> p g a r f", a=2, r=2, f=QK // 4)
                    sines = rope_sin[:, b, :].rearrange("p (a r f) -> p a r f", a=2, r=2)
                    for r in range(2):
                        issue(dve.tensor_tensor(other[:, :, :, r, :], halves[:, :, :, 1 - r, :],
                                                sines[:, None, :, r, :].to_broadcast([P, 8, 2, QK // 4]), ALU.mult))
                    settle()
                    signal("qk_rotated", dve.tensor_tensor(qk_rot, qk_rot, qk_sq, ALU.add))

            def gating(s):
                t = s.vt
                dve.wait_ge(full[t.bank], t.full_after[0])
                step(dve.bn_stats(stats[:, 0, :], tile_ap(t, 512)))
                signal("var_ready", dve.bn_aggr(meanvar[:], stats[:, 0, :]))
                dve.wait_ge(S["std_ready"], s.std + 1)
                step(dve.reciprocal(rstd[:, 0:1], std[:, 0:1]))
                step(dve.tensor_scalar(vn_tile, tile_ap(t, 512), meanvar[:, 0:1], rstd[:, 0:1], ALU.subtract, ALU.mult))
                dve.sem_inc(free[t.bank], 1)
                step(dve.tensor_tensor(vn_tile, vn_tile, vn_gain[:, 0, :], ALU.mult))
                signal("vn_ready", dve.tensor_tensor(vn_tile, vn_tile, vn_gain[:, 1, :], ALU.add))
                dve.wait_ge(S["u_ready"], s.u_ready + 1)
                t = s.mt
                dve.wait_ge(full[t.bank], t.full_after[0])
                for g in range(GROUPS):
                    cols = slice(g * P, (g + 1) * P)
                    issue(dve.scalar_tensor_tensor(out=cat[:, HEADS * VD + g * P:HEADS * VD + (g + 1) * P],
                                                   in0=tile_ap(t, 512)[:, cols], scalar=sgu_bias[:, g:g + 1],
                                                   in1=u_tile[:, cols], op0=ALU.add, op1=ALU.mult))
                settle()
                dve.sem_inc(free[t.bank], 1)

            def attend(s):
                def peaks(h):
                    for c in range(2):
                        t = s.score[h][c]
                        dve.wait_ge(full[t.bank], t.full_after[1])
                        step(dve.tensor_reduce(peak[:, h % 2, c:c + 1], tile_ap(t, KEYS), AX.X, ALU.max))
                        signal("max_ready", dve.tensor_scalar(neg_peak[:, h % 2, c:c + 1], peak[:, h % 2, c:c + 1], -SCALE, None, ALU.mult))

                peaks(0)
                for h in range(HEADS):
                    e = h % 2
                    dve.wait_ge(S["exp_ready"], s.exp + 2 * h + 2)
                    step(dve.reciprocal(inv_sum[:, e, :], expsum[:, e, :]))
                    issue(dve.tensor_scalar(inv_sum[:, e, 1:2], inv_sum[:, e, 1:2], neg_lam[:], None, ALU.mult))
                    issue(dve.tensor_scalar(probs[e][0], probs[e][0], inv_sum[:, e, 0:1], None, ALU.mult))
                    settle()
                    signal("probs_ready", dve.scalar_tensor_tensor(
                        out=probs[e][0], in0=probs[e][1], scalar=inv_sum[:, e, 1:2], in1=probs[e][0],
                        op0=ALU.mult, op1=ALU.add))
                    if h + 1 < HEADS:
                        peaks(h + 1)
                dve.wait_ge(S["o_ready"], s.o + HEADS)
                step(dve.tensor_tensor(o_sq, o_tile, o_tile, ALU.mult))
                signal("o_summed", dve.tensor_reduce(sumsq[:, 0:HEADS], o_sq.rearrange("p (h n) -> p h n", h=HEADS), AX.X, ALU.add))
                dve.wait_ge(S["std_ready"], s.std + 1)
                step(dve.reciprocal(rstd[:, 0:HEADS], std[:, 0:HEADS]))
                o3 = o_tile.rearrange("p (h n) -> p h n", h=HEADS)
                step(dve.tensor_tensor(o3, o3, rstd[:, 0:HEADS, None].to_broadcast([P, HEADS, VD]), ALU.mult))
                signal("cat_ready", dve.tensor_tensor(cat[:, 0:HEADS * VD].rearrange("p (h n) -> p h n", h=HEADS), o3,
                                                      subln[:, None, :].to_broadcast([P, HEADS, VD]), ALU.mult))

            def project(s):
                t = s.tile
                dve.wait_ge(full[t.bank], t.full_after[1])
                step(dve.tensor_tensor(h_tile, tile_ap(t, 1024), mod[:, G1, :], ALU.mult))
                dve.sem_inc(free[t.bank], 1)
                signal("x_updated", dve.tensor_tensor(x[:, s.b, :], x[:, s.b, :], h_tile, ALU.add))

            def conv_in(s):
                if s.b == 0:
                    issue(dve.memset(z_t[:, :, 0:PAD], 0.0))
                    issue(dve.memset(z_t[:, :, PAD + SEQ:], 0.0))
                    settle()
                t = s.val
                dve.wait_ge(full[t.bank], t.full_after[1])
                dve.wait_ge(S["sig_ready"], s.sig + 1)
                step(dve.tensor_tensor(z_tile, tile_ap(t, 1024), sig, ALU.mult))
                dve.sem_inc(free[t.bank], 1)
                dve.sem_inc(S["z_ready"], 1)

            def conv(s):
                dve.wait_ge(S["zt_ready"], s.zt)
                na, nb = (TAPS + 1) // 2, TAPS // 2
                done_a, done_b = s.conv * KD * na, s.conv * KD * (nb + 1)
                with dve.Fori(0, KD) as k:
                    for w in range(TAPS):
                        window = z_t[:, bass.ds(k, 1), s.b * P + w:s.b * P + w + P]
                        a = acc[w % 2][:, bass.ds(k, 1), :]
                        tap = taps[:, bass.ds(k, 1), w]
                        mine, before, done, per = (tap_a, w // 2, done_a, na) if w % 2 == 0 else (tap_b, w // 2, done_b, nb + 1)
                        if before:
                            dve.wait_ge(mine, k * per + (done + before))
                        if w == 0:
                            dve.tensor_scalar(a, window, tap, conv_par[:, 0, bass.ds(k, 1)], ALU.mult, ALU.add).then_inc(mine, 1)
                        elif w == 1:
                            dve.tensor_scalar(a, window, tap, None, ALU.mult).then_inc(mine, 1)
                        else:
                            dve.scalar_tensor_tensor(out=a, in0=window, scalar=tap, in1=a, op0=ALU.mult, op1=ALU.add).then_inc(mine, 1)
                    dve.wait_ge(tap_a, k * na + (done_a + na))
                    dve.wait_ge(tap_b, k * (nb + 1) + (done_b + nb))
                    dve.tensor_tensor(acc[0][:, bass.ds(k, 1), :], acc[0][:, bass.ds(k, 1), :], acc[1][:, bass.ds(k, 1), :],
                                      ALU.add).then_inc(tap_b, 1)
                dve.wait_ge(tap_b, done_b + KD * (nb + 1))
                dve.sem_inc(S["conv_done"], 1)
                t = s.there
                dve.wait_ge(full[t.bank], t.full_after[0])
                issue(dve.bn_stats(stats[:, 0, :], tile_ap(t, 1024)[:, 0:512]))
                step(dve.bn_stats(stats[:, 1, :], tile_ap(t, 1024)[:, 512:1024]))
                signal("var_ready", dve.bn_aggr(meanvar[:], stats[:].rearrange("p a n -> p (a n)")))
                dve.wait_ge(S["std_ready"], s.std + 1)
                step(dve.reciprocal(rstd[:, 0:1], std[:, 0:1]))
                step(dve.tensor_scalar(cn_tile, tile_ap(t, 1024), meanvar[:, 0:1], rstd[:, 0:1], ALU.subtract, ALU.mult))
                dve.sem_inc(free[t.bank], 1)
                dve.sem_inc(S["cn_ready"], 1)

            def top16(values, where, scores_of, n):
                for g in range(n):
                    issue(dve.max(values[:, g, 0:8], scores_of(g)))
                settle()
                for g in range(n):
                    issue(dve.max_index(where[:, g, 0:8], values[:, g, 0:8], scores_of(g)))
                    issue(dve.match_replace(scores_of(g), values[:, g, 0:8], scores_of(g), LOW))
                settle()
                for g in range(n):
                    issue(dve.max(values[:, g, 8:16], scores_of(g)))
                settle()
                for g in range(n):
                    issue(dve.max_index(where[:, g, 8:16], values[:, g, 8:16], scores_of(g)))
                settle()

            def select(s):
                dve.wait_ge(S["scores_ready"], s.sc + 2)
                top16(top_v, top_i, lambda g: scores[:, g, :], 2 * PH)
                issue(dve.tensor_copy(top_f, top_i[:]))
                halves = top_v[:].rearrange("p (h two) n -> p h two n", two=2)
                step(dve.tensor_tensor(cand.rearrange("p h (a b) -> p h a b", a=TOPK),
                                       halves[:, :, 0, :, None].to_broadcast([P, PH, TOPK, TOPK]),
                                       halves[:, :, 1, None, :].to_broadcast([P, PH, TOPK, TOPK]), ALU.add))
                top16(best_v, best_p, lambda h: cand[:, h, :], PH)
                issue(dve.tensor_copy(gate_sum[:], best_v[:, :, 0]))
                pos = best_p[:].rearrange("p h n -> p (h n)")
                issue(dve.tensor_scalar(part_u[:, 0, :], pos, 4, None, ALU.logical_shift_right))
                issue(dve.tensor_scalar(part_u[:, 1, :], pos, TOPK - 1, None, ALU.bitwise_and))
                settle()
                issue(dve.tensor_copy(part_f, part_u))
                signal("cand_ready", dve.tensor_tensor(best_v[:], best_v[:], gate_sum[:, :, None].to_broadcast([P, PH, TOPK]), ALU.subtract))
                settle()
                numbers = top_f.rearrange("p (h two) n -> p h two n", two=2)
                for half in range(2):
                    step(dve.tensor_tensor(onehot, part_f[:, half, :, None].to_broadcast([P, SLOTS_PER_BLOCK, TOPK]),
                                           iota16[:, None, :].to_broadcast([P, SLOTS_PER_BLOCK, TOPK]), ALU.is_equal))
                    view = onehot.rearrange("p (h s) n -> p h s n", h=PH)
                    step(dve.tensor_tensor(view, view, numbers[:, :, half, None, :].to_broadcast([P, PH, TOPK, TOPK]), ALU.mult))
                    step(dve.tensor_reduce(part_f[:, half, :], onehot, AX.X, ALU.add))
                step(dve.scalar_tensor_tensor(out=part_f[:, 0, :], in0=part_f[:, 0, :], scalar=float(N_KEYS), in1=part_f[:, 1, :],
                                              op0=ALU.mult, op1=ALU.add))
                issue(dve.tensor_scalar(expert[:, s.b, :], part_f[:, 0, :], float(s.layer * N_EXPERTS), None, ALU.add))
                dve.wait_ge(S["gate_exp"], s.exp + 1)
                step(dve.tensor_reduce(gate_sum[:], best_v[:], AX.X, ALU.add))
                step(dve.reciprocal(gate_sum[:], gate_sum[:]))
                signal("topk_ready", dve.tensor_tensor(gate[:, s.b, :].rearrange("p (h n) -> p h n", h=PH), best_v[:],
                                                       gate_sum[:, :, None].to_broadcast([P, PH, TOPK]), ALU.mult))

            def gather(s):
                base = s.index * ITERS * NG
                dve.wait_ge(S["topk_ready"], s.topk)
                with dve.Fori(0, ITERS) as i:
                    for g in range(NG):
                        for k in range(g * GROUP, (g + 1) * GROUP):
                            dve.wait_ge(slot_landed[k], i * 16 + 16 * (s.index * ITERS + 1))
                            ins = dve.tensor_tensor_reduce(out=ring[:, k, 0:D], in0=ring[:, k, 0:D], in1=h2[:, s.b, :], scale=1.0,
                                                           scalar=0.0, op0=ALU.mult, op1=ALU.add, accum_out=dots[:, k:k + 1])
                        ins.then_inc(dots_ready, 1)
                        dve.wait_ge(acts_ready, i * NG + (base + g + 1))
                        for k in range(g * GROUP, (g + 1) * GROUP):
                            ins = dve.tensor_scalar(diag[:, k, :], ident[:], acts[:, k:k + 1],
                                                    gate[:, s.b, bass.ds(i * RING + k, 1)], ALU.mult, ALU.mult)
                        ins.then_inc(diag_ready, 1)
                dve.wait_ge(slots_free, base + ITERS * NG + NG)
                step(dve.tensor_tensor(h_tile, ffn_out, mod[:, G2, :], ALU.mult))
                signal("x_updated", dve.tensor_tensor(x[:, s.b, :], x[:, s.b, :], h_tile, ALU.add))

            for s in plan.stages:
                if s.kind != "values":
                    {"ada": ada, "norm": norm, "heads": heads, "gating": gating, "attend": attend, "project": project,
                     "conv_in": conv_in, "conv": conv, "select": select, "gather": gather}[s.kind](s)

        @block.tensor
        def _(pe):
            def claim(t):
                if t.frees_before:
                    pe.wait_ge(free[t.bank], t.frees_before)

            def turn(t, src, n):
                claim(t)
                for k in range(n):
                    ins = pe.transpose(psum[:, t.bank, k * P:(k + 1) * P], src[:, k * P:(k + 1) * P], ident[:])
                ins.then_inc(full[t.bank], 1)

            def linear(t, part, left, c):
                pe.wait_ge(landed[c.buf], c.landed)
                if part == 0:
                    claim(t)
                dst = psum[:, t.bank, part * COLS:(part + 1) * COLS]
                if c.bias is not None:
                    pe.matmul(dst, ones_row[:], weights[0:1, c.buf, KD, :], start=True, stop=False)
                for k in range(KD):
                    ins = pe.matmul(dst, left[:, k, :], weights[:, c.buf, k, :], start=k == 0 and c.bias is None, stop=k == KD - 1)
                ins.then_inc(full[t.bank], 1)

            def ada(s):
                pe.wait_ge(S["cond_ready"], s.cond + 1)
                for j, c, t, both in s.parts:
                    linear(t, 0, cond_b[:, 0], c)
                    if both:
                        linear(t, 1, cond_b[:, 1], c)

            def norm(s):
                pe.wait_ge(S["h_ready"], s.h + 1)
                turn(s.tile, h_tile if s.dest == "h" else h2[:, s.dest[1], :], KD)

            def left_of(name, tok):
                return ht_all[:, tok] if name == "k" else h_t

            def heads(s):
                pe.wait_ge(S["ht_ready"], s.ht)
                for n in range(len(s.tiles) + 1):
                    if n < len(s.tiles):
                        linear(s.proj[n], 0, left_of(s.name, s.tiles[n]), s.chunk)
                    if n:
                        pe.wait_ge(S["qk_rotated"], s.turned + n)
                        turn(s.turn[n - 1], qk_rot, HEADS)

            def values(s):
                for n, tok in enumerate(s.tiles):
                    linear(s.proj[n], 0, ht_all[:, tok], s.chunk)

            def gating(s):
                linear(s.ut, 0, h_t, s.u)
                linear(s.vt, 0, h_t, s.vg)
                pe.wait_ge(S["vn_ready"], s.vn + 1)
                claim(s.mt)
                for g in range(GROUPS):
                    ins = pe.matmul(psum[:, s.mt.bank, g * P:(g + 1) * P], sgu_t[:, g, :], vn_tile[:, g * P:(g + 1) * P],
                                    start=True, stop=True)
                ins.then_inc(full[s.mt.bank], 1)

            def attend(s):
                pe.wait_ge(S["qkt_ready"], s.qkt)

                def score(h):
                    for c in range(2):
                        t = s.score[h][c]
                        claim(t)
                        rows = slice(c * QK, (c + 1) * QK)
                        for lo, hi in ((0, COLS), (COLS, KEYS)):
                            pe.matmul(psum[:, t.bank, lo:hi], q_t[rows, h, :], k_t[rows, h, lo:hi], start=True, stop=True).then_inc(
                                full[t.bank], 1)

                score(0)
                for h in range(HEADS):
                    if h + 1 < HEADS:
                        score(h + 1)
                    pe.wait_ge(S["probs_ready"], s.mix + h + 1)
                    turn(s.turn[h], probs[h % 2][0], NT)
                    pe.wait_ge(S["probst_ready"], s.pt + h + 1)
                    t = s.out[h]
                    claim(t)
                    for kt in range(NT):
                        ins = pe.matmul(psum[:, t.bank, 0:VD], probs_t[:, kt, :], v_all[:, kt, h * VD:(h + 1) * VD],
                                        start=kt == 0, stop=kt == NT - 1)
                    ins.then_inc(full[t.bank], 1)

            def project(s):
                if s.which == "even":
                    pe.wait_ge(S["cat_ready"], s.cat)
                    turn(s.turn, cat, KD)
                    pe.wait_ge(S["left_ready"], s.left + 1)
                    left = h_t
                else:
                    pe.wait_ge(S["left_ready"], s.left_before)
                    left = cn_t
                for j in range(2):
                    linear(s.tile, j, left, s.chunks[j])

            def conv_in(s):
                pe.wait_ge(S["ht_ready"], s.ht)
                for j in range(4):
                    linear(s.gate if j < 2 else s.val, j % 2, h_t, s.chunks[j])
                pe.wait_ge(S["z_ready"], s.z + 1)
                turn(s.turn, z_tile, KD)

            def conv(s):
                pe.wait_ge(S["conv_done"], s.conv + 1)
                turn(s.there, acc[0].rearrange("p k n -> p (k n)"), KD)
                pe.wait_ge(S["cn_ready"], s.cn + 1)
                turn(s.back, cn_tile, KD)

            def select(s):
                pe.wait_ge(S["ht_ready"], s.ht)
                for j in range(4):
                    c, t = s.chunks[j], s.q[j // 2]
                    pe.wait_ge(landed[c.buf], c.landed)
                    if j % 2 == 0:
                        claim(t)
                    for g in range(4):
                        dst = psum[:, t.bank, (j % 2) * COLS + g * P:(j % 2) * COLS + (g + 1) * P]
                        for k in range(KD):
                            ins = pe.matmul(dst, weights[:, c.buf, k, g * P:(g + 1) * P], h_t[:, k, :], start=k == 0, stop=k == KD - 1)
                    ins.then_inc(full[t.bank], 1)
                c = s.keys
                pe.wait_ge(landed[c.buf], c.landed)
                keys = weights[:, c.buf, 0:KD, :].rearrange("p k n -> p (k n)")[:, s.layer * 2048:(s.layer + 1) * 2048]
                for j in range(2):
                    pe.wait_ge(S["pq_ready"], s.qt + j + 1)
                    t = s.s[j]
                    claim(t)
                    for g in range(8):
                        hp = 8 * j + g
                        ins = pe.matmul(psum[:, t.bank, g * P:(g + 1) * P], pq_t[:, hp, :], keys[:, hp * P:(hp + 1) * P],
                                        start=True, stop=True)
                        if g % 4 == 3:
                            ins.then_inc(full[t.bank], 1)

            def gather(s):
                base = s.index * ITERS * NG
                pe.wait_ge(S["x_updated"], s.x)
                for n in range(2):
                    pe.matmul(ffn_out[:, n * COLS:(n + 1) * COLS], zero_row[:], h2[0:1, s.b, 0:COLS], start=True, stop=True)
                with pe.Fori(0, ITERS) as i:
                    for g in range(NG):
                        pe.wait_ge(diag_ready, i * NG + (base + g + 1))
                        for k in range(g * GROUP, (g + 1) * GROUP):
                            for n in range(2):
                                ins = pe.matmul(ffn_out[:, n * COLS:(n + 1) * COLS], diag[:, k, :],
                                                ring[:, k, D + n * COLS:D + (n + 1) * COLS], start=False, stop=True,
                                                skip_group_check=True)
                        ins.then_inc(slots_free, 1)

            pe.sem_inc(slots_free, NG)
            pe.wait_ge(params, 16 * N_PARAMS)
            pe.wait_ge(consts, 1)
            for s in plan.stages:
                {"ada": ada, "norm": norm, "heads": heads, "values": values, "gating": gating, "attend": attend,
                 "project": project, "conv_in": conv_in, "conv": conv, "select": select, "gather": gather}[s.kind](s)


def layouts(np_, i):
    def chunked(w):
        return w.reshape(KD, P, -1, COLS).transpose(2, 1, 0, 3).reshape(-1, P, KD * COLS)

    f = np_.float32
    keys = i["peer_keys"].reshape(LAYERS, 2 * PH, N_KEYS, P).transpose(3, 0, 1, 2).reshape(1, P, 2 * 2048)
    chunks = np_.concatenate([
        chunked(i["ada_w"][0]), chunked(i["ada_w"][1]), chunked(i["ev_w_in"][0]), chunked(i["ev_w_out"][0]),
        chunked(i["od_pw1_w"][0]), chunked(i["od_pw2_w"][0]), chunked(i["peer_wq"][0]), chunked(i["peer_wq"][1]), keys])
    biases = np_.concatenate([i["ada_b"].reshape(-1, COLS), i["od_pw1_b"].reshape(-1, COLS), i["od_pw2_b"].reshape(-1, COLS)])
    n = np_.arange(SEQ)
    grid = np_.stack([n // 64, n % 64], 1).astype(f)
    inv = (10000.0 ** (-np_.arange(QK // 4, dtype=f) / (QK // 4))).astype(f)
    ang = (grid[:, :, None] * inv).astype(f)
    cos = np_.stack([np_.cos(ang)] * 2, 2).reshape(SEQ, QK).astype(f)
    sin = np_.stack([-np_.sin(ang), np_.sin(ang)], 2).reshape(SEQ, QK).astype(f)

    def blocks(a):
        return a.reshape(NB, P, -1).transpose(1, 0, 2)

    def columns(a):
        return a.reshape(-1, KD, P).transpose(2, 0, 1)

    return {
        "x": i["x"][0], "ctx": i["ctx"][0],
        "cond": columns(np_.stack([i["c"][0], i["c_ctx"]])),
        "ident": np_.eye(P, dtype=f),
        "iota16": np_.tile(np_.arange(TOPK, dtype=f), (P, 1)),
        "rope_cos": blocks(cos), "rope_sin": blocks(sin),
        "gains": np_.stack([i["ev_q_gain"][0], i["ev_k_gain"][0]]),
        "lam": i["ev_lam"][0], "subln": i["ev_subln_g"][0],
        "vn_gain": np_.stack([i["ev_vnorm_g"][0], i["ev_vnorm_b"][0]]),
        "sgu_t": i["ev_sgu_w"][0].transpose(2, 0, 1), "sgu_bias": i["ev_sgu_b"][0].T,
        "taps": i["od_dw_w"][0].reshape(TAPS, KD, P).transpose(2, 1, 0),
        "conv_par": columns(np_.stack([i["od_dw_b"][0], i["od_ln_g"][0], i["od_ln_b"][0]])),
        "chunks": chunks, "biases": biases,
        "experts": np_.concatenate([i["peer_down"], i["peer_up"]], axis=2).reshape(LAYERS * N_EXPERTS, 2 * D),
    }


def kernel(**inputs):
    import concourse.bacc as bacc
    from concourse.bass_utils import run_bass_kernel_spmd

    laid = layouts(np, {k: np.asarray(v) for k, v in inputs.items()})
    nc = bacc.Bacc("TRN2", target_bir_lowering=False, num_devices=1)
    arrays, aps = {}, {}
    for name, a in laid.items():
        a = np.ascontiguousarray(a)
        arrays[f"in_{name}"] = a
        aps[name] = nc.dram_tensor(f"in_{name}", a.shape, mybir.dt.from_np(a.dtype), kind="ExternalInput").ap()
    out = nc.dram_tensor("out_x", (SEQ, D), F32, kind="ExternalOutput").ap()
    trunk_kernel(nc, aps, out)
    r = run_bass_kernel_spmd(nc, [arrays], core_ids=[0])
    return np.asarray(r.results[0]["out_x"]).reshape(1, SEQ, D)
```

```python
from contextlib import ExitStack

import numpy as np

import concourse.bass as bass
from concourse import mybir

F32 = mybir.dt.float32
U32 = mybir.dt.uint32
ALU = mybir.AluOpType
ACT = mybir.ActivationFunctionType
AX = mybir.AxisListType

P = 128
D = 1024
KD = D // P
SEQ = 512
CTX = 256
NB = SEQ // P
NT = (SEQ + CTX) // P
LAYERS = 2
EPS = 1e-6
COLS = 512

HEADS = 4
QK = 64
VD = 128
KEYS = SEQ + CTX
LAM_INIT = 0.8 - 0.6
SCALE = QK ** -0.5
GROUPS = 4

TAPS = 31
PAD = TAPS // 2

N_KEYS = 128
PH = 8
TOPK = 16
SLOTS_PER_BLOCK = PH * TOPK
N_EXPERTS = N_KEYS * N_KEYS
LOW = -3.0e38

RING = 8
GROUP = 2
NG = RING // GROUP
ITERS = SLOTS_PER_BLOCK // RING

ADA_CH = [0, 12]
Q_CH, K_CH, V_CH, U_CH, VG_CH = 24, 25, 26, 27, 28
OUT_CH = 29
PW1_CH = 31
PW2_CH = 35
WQ_CH = [37, 41]
KEY_CH = 45
N_CHUNKS = 46
SH1, SC1, G1, SH2, SC2, G2 = range(6)


class Tile:

    def __init__(self, bank, frees_before, full_after):
        self.bank, self.frees_before, self.full_after = bank, frees_before, full_after


class Chunk:

    def __init__(self, source, buf, landed, cols):
        self.source, self.buf, self.landed, self.cols, self.last_use = source, buf, landed, cols, None


class Stage:

    def __init__(self, kind, layer=None, b=None, name=None, tiles=None, which=None, src=None, dest=None, out_t=None,
                 mods=None, parts=None, first=None, last=None, cost=(0,)):
        self.kind, self.layer, self.b, self.name, self.tiles, self.which = kind, layer, b, name, tiles, which
        self.src, self.dest, self.out_t, self.mods, self.parts = src, dest, out_t, mods, parts
        self.first, self.last = first, last
        self.cost = cost


class Plan:

    DUOS = 3
    BUFS = 2
    EARLY = 2

    def __init__(self):
        self.uses = [0] * (self.DUOS + 1)
        self.fulls = [0] * (self.DUOS + 1)
        self.n = 0
        self.chunks = []
        self.early_chunks = []
        self.landed = [0] * (self.BUFS + self.EARLY)
        self.counts = {}
        self.order = []

    def tile(self, parts=1, early=False):
        d = self.DUOS if early else self.n % self.DUOS
        self.n += not early
        t = Tile(d, self.uses[d], [self.fulls[d] + i + 1 for i in range(parts)])
        self.uses[d] += 1
        self.fulls[d] += parts
        return t

    def chunk(self, source, cols=(0, KD * COLS), early=False):
        line = self.early_chunks if early else self.chunks
        b = self.BUFS + len(line) % self.EARLY if early else len(line) % self.BUFS
        self.landed[b] += 16
        c = Chunk(source, b, self.landed[b], cols)
        line.append(c)
        return c

    def used(self, chunk, tile, part):
        chunk.last_use = (tile.bank, tile.full_after[part])

    def take(self, name, k=1):
        before = self.counts.get(name, 0)
        self.counts[name] = before + k
        return before

    def so_far(self, name):
        return self.counts.get(name, 0)

    def ada(self, layer, sections, first=False):
        early = layer == 0
        s = Stage("ada", layer=layer, parts=[], first=first, cost=(3.5, 3.5, 2) * len(sections))
        for sec in sections:
            chunks = [self.chunk(ADA_CH[layer] + 2 * sec + j, early=early) for j in range(2)]
            t = self.tile(2, early)
            for j in range(2):
                self.used(chunks[j], t, j)
            row = self.tile(early=early) if sec in (G1, G2) else None
            s.parts.append((sec, chunks, t, self.take("mod_ready"), row))
        s.rows = self.take("row_ready", sum(p[4] is not None for p in s.parts))
        return s

    def norm(self, src, dest, out_t, mods):
        s = Stage("norm", src=src, dest=dest, out_t=out_t, mods=mods, cost=(2, 4, 3) if dest else (2, 4))
        s.x_updates = self.so_far("x_updated")
        s.topk_before = self.so_far("topk_ready")
        s.mod = self.so_far("mod_ready")
        s.std = self.take("std_ready")
        s.h = self.take("h_ready")
        s.ht = self.take("ht_ready")
        s.tile = self.tile()
        if dest:
            s.back = self.tile()
            s.h2 = self.take("h2_ready")
        return s

    def heads(self, name, tiles, source):
        s = Stage("heads", name=name, tiles=tiles, cost=(3.6, 4) * len(tiles) + (2,))
        s.ht = self.so_far("ht_ready")
        s.chunk = self.chunk(source)
        s.proj, s.turn = [None] * len(tiles), [None] * len(tiles)
        for n in range(len(tiles) + 1):
            if n < len(tiles):
                s.proj[n] = self.tile()
            if n:
                s.turn[n - 1] = self.tile()
        self.used(s.chunk, s.proj[-1], 0)
        s.copied = self.take("qk_copied", len(tiles))
        s.summed = self.take("qk_summed", len(tiles))
        s.std = self.take("std_ready", len(tiles))
        s.turned = self.take("qk_rotated", len(tiles))
        s.done = self.take("qkt_ready", len(tiles))
        return s

    def values(self, tiles):
        s = Stage("values", tiles=tiles, cost=(3.6, 3.6) * len(tiles))
        s.ht = self.so_far("ht_ready")
        s.chunk = self.chunk(V_CH)
        s.proj = [self.tile() for _ in tiles]
        self.used(s.chunk, s.proj[-1], 0)
        s.done = self.take("v_ready", len(tiles))
        return s

    def gating(self, b):
        s = Stage("gating", b=b, cost=(3.6, 3.6, 3.6, 4, 3))
        s.ht = self.so_far("ht_ready")
        s.u, s.vg = self.chunk(U_CH), self.chunk(VG_CH)
        s.ut, s.vt, s.mt = self.tile(), self.tile(), self.tile()
        self.used(s.u, s.ut, 0)
        self.used(s.vg, s.vt, 0)
        s.u_ready = self.take("u_ready")
        s.var = self.take("var_ready")
        s.std = self.take("std_ready")
        s.vn = self.take("vn_ready")
        return s

    def attend(self, b):
        s = Stage("attend", b=b, cost=(8,) + (8, 2) * (HEADS - 1) + (2, 2, 4))
        s.qkt, s.v = self.so_far("qkt_ready"), self.so_far("v_ready")
        s.score, s.turn, s.out = [None] * HEADS, [None] * HEADS, [None] * HEADS
        s.score[0] = [self.tile(2), self.tile(2)]
        for h in range(HEADS):
            if h + 1 < HEADS:
                s.score[h + 1] = [self.tile(2), self.tile(2)]
            s.turn[h], s.out[h] = self.tile(), self.tile()
        s.max = self.take("max_ready", 2 * HEADS)
        s.exp = self.take("exp_ready", 2 * HEADS)
        s.mix = self.take("probs_ready", HEADS)
        s.pt = self.take("probst_ready", HEADS)
        s.o = self.take("o_ready", HEADS)
        s.ss = self.take("o_summed")
        s.std = self.take("std_ready")
        s.cat = self.take("cat_ready")
        return s

    def project(self, b, which):
        s = Stage("project", b=b, which=which, cost=(3, 3.6, 3.6, 3.6, 4) if which == "even" else (5, 3.6, 3.6, 4))
        s.rows = self.so_far("row_ready")
        if which == "even":
            s.cat = self.so_far("cat_ready")
            s.turn = self.tile()
        s.chunks = [self.chunk((OUT_CH if which == "even" else PW2_CH) + j) for j in range(2)]
        s.left_before = self.so_far("left_ready")
        s.left = self.take("left_ready") if which == "even" else None
        s.tile = self.tile(2)
        for j in range(2):
            self.used(s.chunks[j], s.tile, j)
        s.x = self.take("x_updated")
        return s

    def conv_in(self, b):
        s = Stage("conv_in", b=b, cost=(4.2,) * 8)
        s.ht = self.so_far("ht_ready")
        order = [2, 3, 0, 1]
        s.chunks = [self.chunk(PW1_CH + j) for j in order]
        s.gate, s.val = self.tile(2), self.tile(2)
        for j in range(4):
            self.used(s.chunks[j], s.gate if j < 2 else s.val, j % 2)
        s.sig = self.take("sig_ready")
        s.z = self.take("z_ready")
        return s

    def conv(self, b):
        s = Stage("conv", b=b, cost=(4.4,) * len(TAP_RUNS) + (5, 4))
        s.there, s.back = self.tile(), self.tile()
        s.conv = self.take("conv_done")
        s.var = self.take("var_ready")
        s.std = self.take("std_ready")
        s.cn = self.take("cn_ready")
        s.left = self.take("left_ready")
        return s

    def select(self, layer, b):
        s = Stage("select", layer=layer, b=b, cost=(4.2,) * 8 + (3, 3) + (4, 4, 4, 4, 5, 4, 3, 3, 4, 5, 3, 5, 5, 5, 5))
        s.ht = self.so_far("ht_ready")
        s.chunks = [self.chunk(WQ_CH[layer] + j) for j in range(4)]
        s.q = [self.tile(2), self.tile(2)]
        for j in range(4):
            self.used(s.chunks[j], s.q[j // 2], j % 2)
        s.keys = self.chunk(KEY_CH, (layer * 2048, (layer + 1) * 2048))
        s.s = [self.tile(2), self.tile(2)]
        self.used(s.keys, s.s[1], 1)
        s.qt = self.take("pq_ready", 2)
        s.sc = self.take("scores_ready", 2)
        s.top = self.take("cand_ready")
        s.exp = self.take("gate_exp")
        s.done = self.take("topk_ready")
        return s

    def gather(self, layer, b, first, last):
        s = Stage("gather", layer=layer, b=b, first=first, last=last)
        s.index = layer * NB + b
        return s

    def finish(self, layer, b):
        s = Stage("finish", layer=layer, b=b)
        s.index = layer * NB + b
        s.rows = self.so_far("row_ready")
        s.x = self.take("x_updated")
        return s

    def run(self, stage):
        for n in range(len(stage.cost)):
            self.order.append((stage, n))

    def beside(self, layer, b, makers):
        stages = [make() for make in makers]
        phases = [(s, n) for s in stages for n in range(len(s.cost))]
        weight = [s.cost[n] + 1.0 for s, n in phases]
        total, spent, at = sum(weight), 0.0, 0
        groups = ITERS * NG
        if not phases:
            self.run(self.gather(layer, b, 0, groups))
            groups = 0
        for i in range(groups):
            self.order.append((self.gather(layer, b, i, i + 1), 0))
            while at < len(phases) and spent + weight[at] / 2 < total * (i + 1) / (groups - 1):
                spent += weight[at]
                self.order.append(phases[at])
                at += 1
        assert at == len(phases)
        self.run(self.finish(layer, b))

    def later(self):
        order, held, beside = [], [], False
        for s, phase in self.order:
            if s.kind == "gather" and s.last - s.first > 1:
                order += held + [(s, phase)]
                held = []
            elif s.kind == "gather":
                order += [(s, phase)] + held
                held, beside = [], True
            elif beside:
                held.append((s, phase))
            else:
                order.append((s, phase))
        return order + held


TAP_RUNS = [(lo, lo + 2) for lo in range(1, TAPS, 2)]


def make_plan():
    p = Plan()

    def ffn_prep(layer, b):
        return [lambda: p.norm(("x", b), ("h2", b % 2), ("one", 0), (layer, SH2)), lambda: p.select(layer, b)]

    def even(b):
        return [lambda: p.norm(("x", b), None, ("one", 0), (0, SH1)), lambda: p.heads("q", [b + CTX // P], Q_CH),
                lambda: p.gating(b), lambda: p.attend(b), lambda: p.project(b, "even")] + ffn_prep(0, b)

    def pointwise(b):
        return [lambda: p.norm(("x", b), None, ("one", 0), (1, SH1)), lambda: p.conv_in(b)]

    def odd(b):
        return [lambda: p.conv(b), lambda: p.project(b, "odd")] + ffn_prep(1, b)

    p.run(p.ada(0, [SH1, SC1], first=True))
    for t in range(NT):
        ctx = t < CTX // P
        p.run(p.norm(("ctx", t) if ctx else ("x", t - CTX // P), None, ("all", t), "ctx" if ctx else (0, SH1)))
    rest = p.ada(0, [G1, SH2, SC2, G2])
    kv = [p.heads("k", list(range(NT)), K_CH), p.values(list(range(NT)))]
    kv = [(s, n) for s in kv for n in range(len(s.cost))]
    for n, item in enumerate(kv):
        p.order.append(item)
        if 3 <= n < 3 + len(rest.cost):
            p.order.append((rest, n - 3))
    for make in even(0):
        p.run(make())
    p.beside(0, 0, even(1) + [lambda: p.ada(1, [SH1, SC1])])
    p.beside(0, 1, even(2) + [lambda: p.ada(1, [SH2, SC2])])
    p.beside(0, 2, even(3) + [lambda: p.ada(1, [G1])] + pointwise(0))
    p.beside(0, 3, pointwise(1) + odd(0))
    p.beside(1, 0, [lambda: p.ada(1, [G2])] + pointwise(2) + odd(1))
    p.beside(1, 1, pointwise(3) + odd(2))
    p.beside(1, 2, odd(3))
    p.beside(1, 3, [])
    return p


def trunk_kernel(nc, A, out):
    plan = make_plan()
    with ExitStack() as ctx:
        def sb(name, shape, dt=F32):
            return ctx.enter_context(nc.sbuf_tensor(name, shape, dt))

        def sem(name):
            return ctx.enter_context(nc.semaphore(name))

        x = sb("x", [P, NB, D])
        mod = sb("mod", [P, LAYERS, 6, KD])
        ctx_mod = sb("ctx_mod", [P, 2, KD])
        ada_bias = sb("ada_bias", [P, LAYERS, 6, KD])
        g1_row = sb("g1_row", [P, D])
        g2_row = sb("g2_row", [P, D])
        ring = sb("ring", [P, RING, 2 * D])
        h2 = sb("h2", [P, 2, D])
        kept = sb("kept", [P, 6144])
        weights = sb("weights", [P, Plan.BUFS, KD, COLS])
        arena = sb("arena", [P, 8192])
        ident = sb("ident", [P, P])
        zero_row = sb("zero_row", [1, P])
        eps = sb("eps", [P, 1])
        iota16 = sb("iota16", [P, TOPK])
        cond = sb("cond", [P, 2, KD])
        cond_silu = sb("cond_silu", [P, 2, KD])
        rope_cos = sb("rope_cos", [P, NB, QK])
        rope_sin = sb("rope_sin", [P, NB, QK])
        gains = sb("gains", [P, 2, QK])
        subln = sb("subln", [P, VD])
        sgu_t = sb("sgu_t", [P, GROUPS, P])
        sgu_bias = sb("sgu_bias", [P, GROUPS])
        taps = sb("taps", [P, KD, TAPS])
        conv_par = sb("conv_par", [P, 4 + 2, KD])
        vn_gain = sb("vn_gain", [P, 2, COLS])
        neg_lam = sb("neg_lam", [P, 1])
        sumsq = sb("sumsq", [P, 8])
        std = sb("std", [P, 8])
        rstd = sb("rstd", [P, 8])
        stats = sb("stats", [P, 2, 6])
        meanvar = sb("meanvar", [P, 2])
        peak = sb("peak", [P, 2, 2])
        neg_peak = sb("neg_peak", [P, 2, 2])
        expsum = sb("expsum", [P, 2, 2])
        inv_sum = sb("inv_sum", [P, 2, 2])
        top_v = sb("top_v", [P, 2 * PH, TOPK])
        top_i = sb("top_i", [P, 2 * PH, TOPK], U32)
        best_v = sb("best_v", [P, PH, TOPK])
        best_p = sb("best_p", [P, PH, TOPK], U32)
        gate_sum = sb("gate_sum", [P, PH])
        expert = sb("expert", [P, 2, SLOTS_PER_BLOCK], U32)
        gate = sb("gate", [P, 2, SLOTS_PER_BLOCK])
        staged = sb("staged", [P, RING], U32)
        dots = sb("dots", [P, RING])
        acts = sb("acts", [P, RING])
        diag = sb("diag", [P, RING, P])
        psum = ctx.enter_context(nc.psum_tensor("psum", [P, 4, 2 * COLS], F32))
        ffn_out = psum[:, 3, :]

        store = ring[:].rearrange("p s n -> p (s n)")
        ht_all = store[:, 0:6144].rearrange("p (t k n) -> p t k n", t=NT, k=KD)
        ctx_x = store[:, 6144:8192].rearrange("p (t n) -> p t n", t=CTX // P)
        buffers = [weights[:, i] for i in range(Plan.BUFS)] + [
            store[:, 8192 + i * KD * COLS:8192 + (i + 1) * KD * COLS].rearrange("p (k n) -> p k n", k=KD) for i in range(Plan.EARLY)]
        k_t = kept[:, 0:3072].rearrange("p (h t) -> p h t", h=HEADS)
        v_all = kept[:, 3072:6144].rearrange("p (t n) -> p t n", t=NT)
        ZW = SEQ + 2 * PAD
        z_t = kept[:, 0:KD * ZW].rearrange("p (k t) -> p k t", k=KD)

        def at(start, n):
            return arena[:, start:start + n]

        h_tile = at(0, 1024)
        h_t = at(1024, 1024).rearrange("p (k n) -> p k n", k=KD)
        q_t = at(2048, 512).rearrange("p (h n) -> p h n", h=HEADS)
        qk_raw, qk_sq, qk_rot = at(2560, 512), at(3072, 512), at(3584, 512)
        u_tile, vn_tile = at(4096, 512), at(4608, 512)
        o_tile, o_sq = at(5120, 512), at(3584, 512)
        cat = at(5632, 1024)
        probs = [[at(0, KEYS), at(1024, KEYS)], [at(4096, KEYS), at(6656, KEYS)]]
        lam_in = at(2048, 4 * QK).rearrange("p (a n) -> p a n", a=4)
        probs_t = at(2560, 768).rearrange("p (t n) -> p t n", t=NT)
        pq_t = at(2048, 2048).rearrange("p (g n) -> p g n", g=2 * PH)
        scores = at(4096, 2048).rearrange("p (g n) -> p g n", g=2 * PH)
        cand = at(6144, 2048).rearrange("p (h n) -> p h n", h=PH)
        onehot = at(2048, 2048).rearrange("p (s n) -> p s n", n=TOPK)
        top_f = at(4096, 256).rearrange("p (g n) -> p g n", n=TOPK)
        part_u = at(4352, 256).bitcast(U32).rearrange("p (a n) -> p a n", a=2)
        part_f = at(4608, 256).rearrange("p (a n) -> p a n", a=2)
        sig = at(2048, 1024)
        pw1_bias = conv_par[:, 4:6, :]
        acc = at(4096, 1024).rearrange("p (k n) -> p k n", k=KD)
        cn_tile = at(6144, 1024)
        cn_t = at(7168, 1024).rearrange("p (k n) -> p k n", k=KD)

        params = sem("params_landed")
        x_landed = sem("x_landed")
        consts = sem("consts_ready")
        landed = [sem(f"chunk_landed{i}") for i in range(Plan.BUFS + Plan.EARLY)]
        full = [sem(f"psum_full{i}") for i in range(Plan.DUOS + 1)]
        free = [sem(f"psum_free{i}") for i in range(Plan.DUOS + 1)]
        act_step, dve_step = sem("act_step"), sem("dve_step")
        S = {n: sem(n) for n in (
            "raw_ready",
            "std_ready", "h_ready", "ht_ready", "h2_ready", "row_ready", "mod_ready", "qk_copied", "qk_summed", "qk_rotated",
            "qkt_ready", "v_ready", "u_ready", "var_ready", "vn_ready", "max_ready", "exp_ready",
            "probs_ready", "probst_ready", "o_ready", "o_summed", "cat_ready", "left_ready", "x_updated", "sig_ready",
            "z_ready", "conv_done", "cn_ready", "pq_ready", "scores_ready", "cand_ready",
            "gate_exp", "topk_ready")}
        lam_sum, lam_exp, cond_act = sem("lam_sum"), sem("lam_exp"), sem("cond_act")
        slot_landed = [sem(f"slot_landed{i}") for i in range(RING)]
        staged_ready, staged_seen = sem("staged_ready"), sem("staged_seen")
        dots_ready, acts_ready, diag_ready = sem("dots_ready"), sem("acts_ready"), sem("diag_ready")
        slots_free = sem("slots_free")
        taps_done = sem("taps_done")
        stored = sem("stored")
        sums_read = sem("sums_read")

        N_PARAMS = 15
        orders = {"pe": plan.order, "others": plan.later()}

        def run_phases(functions, order):
            running = {}
            for s, phase in orders[order]:
                if s.kind not in functions:
                    continue
                if phase == 0:
                    running[s.kind] = functions[s.kind](s)
                next(running[s.kind], None)

        block = ctx.enter_context(nc.Block())

        @block.sync
        def _(sp):
            sp.dma_start(cond[:], A["cond"]).then_inc(params, 16)
            sp.dma_start(ident[:], A["ident"]).then_inc(params, 16)

            def load_chunk(n):
                c = plan.chunks[n]
                if n >= Plan.BUFS:
                    sp.wait_ge(full[plan.chunks[n - Plan.BUFS].last_use[0]], plan.chunks[n - Plan.BUFS].last_use[1])
                lo, hi = c.cols
                sp.dma_start(buffers[c.buf].rearrange("p k n -> p (k n)")[:, 0:hi - lo],
                             A["chunks"][c.source, :, lo:hi]).then_inc(landed[c.buf], 16)

            load_chunk(0)
            load_chunk(1)
            sp.dma_start(ada_bias[:], A["ada_bias"]).then_inc(params, 16)
            sp.dma_start(iota16[:], A["iota16"]).then_inc(params, 16)
            sp.dma_start(rope_cos[:], A["rope_cos"]).then_inc(params, 16)
            sp.dma_start(rope_sin[:], A["rope_sin"]).then_inc(params, 16)
            sp.dma_start(gains[:], A["gains"].partition_broadcast(P)).then_inc(params, 16)
            sp.dma_start(lam_in[:], A["lam"].partition_broadcast(P)).then_inc(params, 16)
            sp.dma_start(subln[:], A["subln"].partition_broadcast(P)).then_inc(params, 16)
            sp.dma_start(vn_gain[:], A["vn_gain"].partition_broadcast(P)).then_inc(params, 16)
            sp.dma_start(sgu_t[:], A["sgu_t"]).then_inc(params, 16)
            sp.dma_start(sgu_bias[:], A["sgu_bias"]).then_inc(params, 16)
            sp.dma_start(taps[:], A["taps"]).then_inc(params, 16)
            sp.dma_start(conv_par[:], A["conv_par"]).then_inc(params, 16)
            sp.dma_start(ctx_x, A["ctx"].rearrange("(t p) n -> p t n", p=P)).then_inc(params, 16)
            sp.dma_start(x[:], A["x"].rearrange("(t p) n -> p t n", p=P)).then_inc(x_landed, 16)
            for n in range(2, len(plan.chunks)):
                load_chunk(n)
            n_out = 0
            for s, _ in plan.order:
                if s.kind == "finish" and s.layer == LAYERS - 1:
                    sp.wait_ge(S["x_updated"], s.x + 1)
                    sp.dma_start(out[s.b * P:(s.b + 1) * P, :], x[:, s.b, :]).then_inc(stored, 16)
                    n_out += 1
            sp.wait_ge(stored, 16 * n_out)

        @block.gpsimd
        def _(pool):
            for n, c in enumerate(plan.early_chunks):
                if n >= Plan.EARLY:
                    pool.wait_ge(full[plan.early_chunks[n - Plan.EARLY].last_use[0]], plan.early_chunks[n - Plan.EARLY].last_use[1])
                pool.dma_start(buffers[c.buf].rearrange("p k n -> p (k n)"), A["chunks"][c.source]).then_inc(landed[c.buf], 16)
            table = A["experts"]
            for s, _ in plan.order:
                if s.kind != "gather" or s.first:
                    continue
                base = s.index * ITERS * NG
                pool.wait_ge(S["topk_ready"], s.index + 1)
                with pool.Fori(0, ITERS) as i:
                    for g in range(NG):
                        pool.wait_ge(slots_free, i * NG + (base + g + 1))
                        pool.tensor_copy(staged[:, g * GROUP:(g + 1) * GROUP],
                                         expert[:, s.b % 2, bass.ds(i * RING + g * GROUP, GROUP)]).then_inc(staged_ready, 1)
                        pool.wait_ge(staged_ready, i * NG + (base + g + 1))
                        pool.sem_inc(staged_seen, 1)
                        for k in range(g * GROUP, (g + 1) * GROUP):
                            pool.indirect_dma_start(
                                out=ring[:, k, :], out_offset=None, in_=table,
                                in_offset=bass.IndirectOffsetOnAxis(ap=staged[:, k:k + 1], axis=0),
                            ).then_inc(slot_landed[k], 16)

        @block.scalar
        def _(act):
            steps = [0]

            def step(ins):
                steps[0] += 1
                ins.then_inc(act_step, 1)
                act.wait_ge(act_step, steps[0])

            def tile_ap(t, n):
                return psum[:, t.bank, 0:n]

            def await_tile(t, part=-1):
                act.wait_ge(full[t.bank], t.full_after[part])

            def evacuate(dst, t, src, name):
                await_tile(t)
                step(act.activation(dst, src, ACT.Copy))
                act.sem_inc(free[t.bank], 1)
                act.sem_inc(S[name], 1)

            act.wait_ge(params, 16 * N_PARAMS)
            act.wait_ge(x_landed, 16)
            act.activation(cond_silu[:], cond[:], ACT.Silu).then_inc(cond_act, 1)
            act.wait_ge(lam_sum, 1)
            act.activation(inv_sum[:, 0, :], sumsq[:, 0:2], ACT.Exp).then_inc(lam_exp, 1)
            act.wait_ge(lam_exp, 1)

            def signal(name, ins):
                ins.then_inc(S[name], 1)

            def ada(s):
                for sec, chunks, t, modded, row in s.parts:
                    yield
                    yield
                    if row is not None:
                        if sec == G2 and s.layer:
                            act.wait_ge(sums_read, s.layer * NB)
                        dst = g1_row[:] if sec == G1 else g2_row[:]
                        evacuate(dst, row, tile_ap(row, 1024), "row_ready")
                    yield

            def norm(s):
                if s.x_updates:
                    act.wait_ge(S["x_updated"], s.x_updates)
                if s.topk_before:
                    act.wait_ge(S["topk_ready"], s.topk_before)
                if s.h:
                    act.wait_ge(S["h_ready"], s.h)
                src = ctx_x[:, s.src[1], :] if s.src[0] == "ctx" else x[:, s.src[1], :]
                if s.h:
                    act.wait_ge(S["ht_ready"], s.ht)
                step(act.activation(h_tile, src, ACT.Square, accum_out=sumsq[:, 0:1]))
                signal("std_ready", act.activation(std[:, 0:1], sumsq[:, 0:1], ACT.Sqrt, bias=eps[:], scale=1.0 / D))
                yield
                await_tile(s.tile)
                act.wait_ge(S["mod_ready"], s.mod)
                dst = ht_all[:, s.out_t[1]] if s.out_t[0] == "all" else h_t
                for k in range(KD):
                    if s.mods == "ctx":
                        shift, scale = ctx_mod[:, 0, k:k + 1], ctx_mod[:, 1, k:k + 1]
                    else:
                        layer, sec = s.mods
                        shift, scale = mod[:, layer, sec, k:k + 1], mod[:, layer, sec + 1, k:k + 1]
                    ins = act.activation(dst[:, k, :], tile_ap(s.tile, 1024)[:, k * P:(k + 1) * P], ACT.Identity, bias=shift, scale=scale)
                step(ins)
                act.sem_inc(free[s.tile.bank], 1)
                act.sem_inc(S["ht_ready"], 1)
                yield
                if s.dest:
                    evacuate(h2[:, s.dest[1], :], s.back, tile_ap(s.back, 1024), "h2_ready")
                yield

            def heads(s):
                def turned(n):
                    tok = s.tiles[n]
                    dst = k_t[:, :, tok * P:(tok + 1) * P] if s.name == "k" else q_t
                    evacuate(dst, s.turn[n], tile_ap(s.turn[n], 512).rearrange("p (h n) -> p h n", h=HEADS), "qkt_ready")

                for n in range(len(s.tiles)):
                    yield
                    if n:
                        act.wait_ge(S["qk_rotated"], s.turned + n)
                    evacuate(qk_raw, s.proj[n], tile_ap(s.proj[n], 512), "raw_ready")
                    signal("qk_copied", act.activation(qk_sq, qk_raw, ACT.Square))
                    act.wait_ge(S["qk_summed"], s.summed + n + 1)
                    signal("std_ready", act.activation(std[:], sumsq[:], ACT.Sqrt, bias=eps[:], scale=1.0 / QK))
                    if n:
                        turned(n - 1)
                    yield
                turned(len(s.tiles) - 1)
                yield

            def values(s):
                for n, tok in enumerate(s.tiles):
                    yield
                    evacuate(v_all[:, tok, :], s.proj[n], tile_ap(s.proj[n], 512), "v_ready")
                    yield

            def gating(s):
                yield
                evacuate(u_tile, s.ut, tile_ap(s.ut, 512), "u_ready")
                yield
                yield
                act.wait_ge(S["var_ready"], s.var + 1)
                signal("std_ready", act.activation(std[:, 0:1], meanvar[:, 1:2], ACT.Sqrt, bias=eps[:]))
                yield

            def attend(s):
                def exps(h):
                    for c in range(2):
                        t = s.score[h][c]
                        await_tile(t)
                        act.wait_ge(S["max_ready"], s.max + 2 * h + c + 1)
                        step(act.activation(probs[h % 2][c], tile_ap(t, KEYS), ACT.Exp,
                                            bias=neg_peak[:, h % 2, c:c + 1], scale=SCALE,
                                            accum_out=expsum[:, h % 2, c:c + 1]))
                        act.sem_inc(free[t.bank], 1)
                        act.sem_inc(S["exp_ready"], 1)

                exps(0)
                yield
                for h in range(HEADS):
                    if h + 1 < HEADS:
                        exps(h + 1)
                    evacuate(probs_t.rearrange("p t n -> p (t n)"), s.turn[h], tile_ap(s.turn[h], KEYS), "probst_ready")
                    yield
                    evacuate(o_tile[:, h * VD:(h + 1) * VD], s.out[h], tile_ap(s.out[h], VD), "o_ready")
                    yield
                act.wait_ge(S["o_summed"], s.ss + 1)
                signal("std_ready", act.activation(std[:, 0:HEADS], sumsq[:, 0:HEADS], ACT.Sqrt, bias=eps[:], scale=1.0 / VD))
                yield

            def project(s):
                if s.which == "even":
                    evacuate(h_t.rearrange("p k n -> p (k n)"), s.turn, tile_ap(s.turn, 1024), "left_ready")
                yield

            def conv_in(s):
                for _ in range(3):
                    yield
                await_tile(s.gate)
                for k in range(KD):
                    ins = act.activation(sig[:, k * P:(k + 1) * P], tile_ap(s.gate, 1024)[:, k * P:(k + 1) * P], ACT.Sigmoid,
                                         bias=pw1_bias[:, 1, k:k + 1])
                step(ins)
                act.sem_inc(free[s.gate.bank], 1)
                act.sem_inc(S["sig_ready"], 1)
                yield

            def conv(s):
                for _ in TAP_RUNS:
                    yield
                act.wait_ge(S["var_ready"], s.var + 1)
                signal("std_ready", act.activation(std[:, 0:1], meanvar[:, 1:2], ACT.Sqrt, bias=eps[:]))
                yield
                t = s.back
                await_tile(t)
                for k in range(KD):
                    ins = act.activation(cn_t[:, k, :], tile_ap(t, 1024)[:, k * P:(k + 1) * P], ACT.Silu,
                                         bias=conv_par[:, 2, k:k + 1], scale=conv_par[:, 1, k:k + 1])
                step(ins)
                act.sem_inc(free[t.bank], 1)
                act.sem_inc(S["left_ready"], 1)
                yield

            def select(s):
                for j in range(4):
                    yield
                    if j % 2:
                        half = j // 2
                        evacuate(pq_t[:, 8 * half:8 * half + 8, :].rearrange("p g n -> p (g n)"), s.q[half],
                                 tile_ap(s.q[half], 1024), "pq_ready")
                    yield
                for half in range(2):
                    evacuate(scores[:, 8 * half:8 * half + 8, :].rearrange("p g n -> p (g n)"), s.s[half],
                             tile_ap(s.s[half], 1024), "scores_ready")
                    yield
                for n in range(12):
                    yield
                act.wait_ge(S["cand_ready"], s.top + 1)
                bv = best_v[:].rearrange("p h n -> p (h n)")
                signal("gate_exp", act.activation(bv, bv, ACT.Exp))
                yield

            def gather(s):
                base = s.index * ITERS * NG
                if s.last - s.first == 1:
                    lo = s.first % NG * GROUP
                    act.wait_ge(dots_ready, base + s.last)
                    act.activation(acts[:, lo:lo + GROUP], dots[:, lo:lo + GROUP], ACT.Gelu).then_inc(acts_ready, 1)
                else:
                    with act.Fori(s.first // NG, s.last // NG) as i:
                        for g in range(NG):
                            lo, hi = g * GROUP, (g + 1) * GROUP
                            act.wait_ge(dots_ready, i * NG + (base + g + 1))
                            act.activation(acts[:, lo:hi], dots[:, lo:hi], ACT.Gelu).then_inc(acts_ready, 1)
                yield

            run_phases({"ada": ada, "norm": norm, "heads": heads, "values": values, "gating": gating, "attend": attend,
                        "project": project, "conv_in": conv_in, "conv": conv, "select": select, "gather": gather}, "others")

        @block.vector
        def _(dve):
            steps = [0]

            def issue(ins):
                steps[0] += 1
                ins.then_inc(dve_step, 1)

            def settle():
                dve.wait_ge(dve_step, steps[0])

            def step(ins):
                issue(ins)
                settle()

            def signal(name, ins):
                ins.then_inc(S[name], 1)

            def bc(ap, shape):
                return ap.to_broadcast(shape)

            def tile_ap(t, n):
                return psum[:, t.bank, 0:n]

            dve.memset(eps[:], EPS)
            dve.memset(zero_row[:], 0.0).then_inc(consts, 1)
            dve.wait_ge(params, 16 * N_PARAMS)
            lam_prod = qk_raw[:, 0:2 * QK].rearrange("p (a n) -> p a n", a=2)
            step(dve.tensor_tensor(lam_prod, lam_in[:, 0:4:2, :], lam_in[:, 1:4:2, :], ALU.mult))
            dve.tensor_reduce(sumsq[:, 0:2], lam_prod, AX.X, ALU.add).then_inc(lam_sum, 1)
            step(dve.tensor_scalar(subln[:], subln[:], 1.0 - LAM_INIT, None, ALU.mult))
            dve.wait_ge(lam_exp, 1)
            step(dve.scalar_tensor_tensor(out=neg_lam[:], in0=inv_sum[:, 0, 1:2], scalar=-LAM_INIT, in1=inv_sum[:, 0, 0:1],
                                     op0=ALU.add, op1=ALU.subtract))

            def ada(s):
                for sec, chunks, t, modded, row in s.parts:
                    yield
                    dve.wait_ge(full[t.bank], t.full_after[-1])
                    plus = 1.0 if sec in (SC1, SC2) else 0.0
                    both = tile_ap(t, 2 * KD).rearrange("p (k c) -> p c k", c=2)
                    if s.layer == 0 and sec in (SH1, SC1):
                        issue(dve.scalar_tensor_tensor(out=ctx_mod[:, sec, :], in0=both[:, 1, :], scalar=plus,
                                                       in1=ada_bias[:, s.layer, sec, :], op0=ALU.add, op1=ALU.add))
                    issue(dve.scalar_tensor_tensor(out=mod[:, s.layer, sec, :], in0=both[:, 0, :], scalar=plus,
                                                   in1=ada_bias[:, s.layer, sec, :], op0=ALU.add, op1=ALU.add))
                    settle()
                    dve.sem_inc(free[t.bank], 1)
                    dve.sem_inc(S["mod_ready"], 1)
                    yield
                    yield

            def norm(s):
                dve.wait_ge(S["std_ready"], s.std + 1)
                src = ctx_x[:, s.src[1], :] if s.src[0] == "ctx" else x[:, s.src[1], :]
                step(dve.reciprocal(rstd[:, 0:1], std[:, 0:1]))
                signal("h_ready", dve.tensor_scalar(h_tile, src, rstd[:, 0:1], None, ALU.mult))
                yield

            def heads(s):
                for n, tok in enumerate(s.tiles):
                    yield
                    dve.wait_ge(S["qk_copied"], s.copied + n + 1)
                    v8 = qk_raw.rearrange("p (g n) -> p g n", n=QK)
                    signal("qk_summed", dve.tensor_reduce(sumsq[:], qk_sq.rearrange("p (g n) -> p g n", n=QK), AX.X, ALU.add))
                    dve.wait_ge(S["std_ready"], s.std + n + 1)
                    step(dve.reciprocal(rstd[:], std[:]))
                    step(dve.tensor_tensor(v8, v8, rstd[:, :, None].to_broadcast([P, 8, QK]), ALU.mult))
                    gain = gains[:, 0 if s.name == "q" else 1, None, :].to_broadcast([P, 8, QK])
                    rot = qk_rot.rearrange("p (g n) -> p g n", n=QK)
                    if n:
                        t = s.turn[n - 1]
                        dve.wait_ge(full[t.bank], t.full_after[0])
                    if tok < CTX // P:
                        signal("qk_rotated", dve.tensor_tensor(rot, v8, gain, ALU.mult))
                        yield
                        continue
                    b = tok - CTX // P
                    step(dve.tensor_tensor(v8, v8, gain, ALU.mult))
                    issue(dve.tensor_tensor(rot, v8, rope_cos[:, b, None, :].to_broadcast([P, 8, QK]), ALU.mult))
                    halves = qk_raw.rearrange("p (g a r f) -> p g a r f", a=2, r=2, f=QK // 4)
                    other = qk_sq.rearrange("p (g a r f) -> p g a r f", a=2, r=2, f=QK // 4)
                    sines = rope_sin[:, b, :].rearrange("p (a r f) -> p a r f", a=2, r=2)
                    for r in range(2):
                        issue(dve.tensor_tensor(other[:, :, :, r, :], halves[:, :, :, 1 - r, :],
                                                sines[:, None, :, r, :].to_broadcast([P, 8, 2, QK // 4]), ALU.mult))
                    settle()
                    signal("qk_rotated", dve.tensor_tensor(qk_rot, qk_rot, qk_sq, ALU.add))
                    yield
                yield

            def gating(s):
                for _ in range(3):
                    yield
                t = s.vt
                dve.wait_ge(full[t.bank], t.full_after[0])
                step(dve.bn_stats(stats[:, 0, :], tile_ap(t, 512)))
                signal("var_ready", dve.bn_aggr(meanvar[:], stats[:, 0, :]))
                dve.wait_ge(S["std_ready"], s.std + 1)
                step(dve.reciprocal(rstd[:, 0:1], std[:, 0:1]))
                step(dve.tensor_scalar(vn_tile, tile_ap(t, 512), meanvar[:, 0:1], rstd[:, 0:1], ALU.subtract, ALU.mult))
                dve.sem_inc(free[t.bank], 1)
                step(dve.tensor_tensor(vn_tile, vn_tile, vn_gain[:, 0, :], ALU.mult))
                signal("vn_ready", dve.tensor_tensor(vn_tile, vn_tile, vn_gain[:, 1, :], ALU.add))
                yield
                dve.wait_ge(S["u_ready"], s.u_ready + 1)
                t = s.mt
                dve.wait_ge(full[t.bank], t.full_after[0])
                for g in range(GROUPS):
                    cols = slice(g * P, (g + 1) * P)
                    issue(dve.scalar_tensor_tensor(out=cat[:, HEADS * VD + g * P:HEADS * VD + (g + 1) * P],
                                                   in0=tile_ap(t, 512)[:, cols], scalar=sgu_bias[:, g:g + 1],
                                                   in1=u_tile[:, cols], op0=ALU.add, op1=ALU.mult))
                settle()
                dve.sem_inc(free[t.bank], 1)
                yield

            def attend(s):
                def peaks(h):
                    for c in range(2):
                        t = s.score[h][c]
                        dve.wait_ge(full[t.bank], t.full_after[1])
                        step(dve.tensor_reduce(peak[:, h % 2, c:c + 1], tile_ap(t, KEYS), AX.X, ALU.max))
                        signal("max_ready", dve.tensor_scalar(neg_peak[:, h % 2, c:c + 1], peak[:, h % 2, c:c + 1], -SCALE, None, ALU.mult))

                def combine(h):
                    e = h % 2
                    dve.wait_ge(S["exp_ready"], s.exp + 2 * h + 2)
                    step(dve.reciprocal(inv_sum[:, e, :], expsum[:, e, :]))
                    issue(dve.tensor_scalar(inv_sum[:, e, 1:2], inv_sum[:, e, 1:2], neg_lam[:], None, ALU.mult))
                    issue(dve.tensor_scalar(probs[e][0], probs[e][0], inv_sum[:, e, 0:1], None, ALU.mult))
                    settle()
                    signal("probs_ready", dve.scalar_tensor_tensor(
                        out=probs[e][0], in0=probs[e][1], scalar=inv_sum[:, e, 1:2], in1=probs[e][0],
                        op0=ALU.mult, op1=ALU.add))

                peaks(0)
                combine(0)
                yield
                for h in range(HEADS):
                    if h + 1 < HEADS:
                        peaks(h + 1)
                        combine(h + 1)
                    yield
                    yield
                dve.wait_ge(S["o_ready"], s.o + HEADS)
                step(dve.tensor_tensor(o_sq, o_tile, o_tile, ALU.mult))
                signal("o_summed", dve.tensor_reduce(sumsq[:, 0:HEADS], o_sq.rearrange("p (h n) -> p h n", h=HEADS), AX.X, ALU.add))
                dve.wait_ge(S["std_ready"], s.std + 1)
                step(dve.reciprocal(rstd[:, 0:HEADS], std[:, 0:HEADS]))
                o3 = o_tile.rearrange("p (h n) -> p h n", h=HEADS)
                step(dve.tensor_tensor(o3, o3, rstd[:, 0:HEADS, None].to_broadcast([P, HEADS, VD]), ALU.mult))
                signal("cat_ready", dve.tensor_tensor(cat[:, 0:HEADS * VD].rearrange("p (h n) -> p h n", h=HEADS), o3,
                                                      subln[:, None, :].to_broadcast([P, HEADS, VD]), ALU.mult))
                yield

            def project(s):
                for _ in range(len(s.cost) - 1):
                    yield
                t = s.tile
                dve.wait_ge(full[t.bank], t.full_after[-1])
                dve.wait_ge(S["row_ready"], s.rows)
                step(dve.tensor_tensor(h_tile, tile_ap(t, 1024), g1_row[:], ALU.mult))
                dve.sem_inc(free[t.bank], 1)
                signal("x_updated", dve.tensor_tensor(x[:, s.b, :], x[:, s.b, :], h_tile, ALU.add))
                yield

            def conv_in(s):
                if s.b == 0:
                    dve.memset(z_t[:, :, 0:PAD], 0.0)
                    dve.memset(z_t[:, :, PAD + SEQ:], 0.0)
                for _ in range(7):
                    yield
                t = s.val
                dve.wait_ge(full[t.bank], t.full_after[-1])
                dve.wait_ge(S["sig_ready"], s.sig + 1)
                for k in range(KD):
                    cols = slice(k * P, (k + 1) * P)
                    issue(dve.scalar_tensor_tensor(out=z_t[:, k, PAD + s.b * P:PAD + (s.b + 1) * P], in0=tile_ap(t, 1024)[:, cols],
                                                   scalar=pw1_bias[:, 0, k:k + 1], in1=sig[:, cols], op0=ALU.add, op1=ALU.mult))
                settle()
                dve.sem_inc(free[t.bank], 1)
                dve.sem_inc(S["z_ready"], 1)
                yield

            def conv(s):
                base = s.conv * TAPS * KD
                for k in range(KD):
                    dve.tensor_scalar(acc[:, k, :], z_t[:, k, s.b * P:(s.b + 1) * P], taps[:, k, 0:1], conv_par[:, 0, k:k + 1],
                                      ALU.mult, ALU.add).then_inc(taps_done, 1)
                for lo, hi in TAP_RUNS:
                    for w in range(lo, hi):
                        dve.wait_ge(taps_done, base + w * KD)
                        for k in range(KD):
                            dve.scalar_tensor_tensor(out=acc[:, k, :], in0=z_t[:, k, w + s.b * P:w + (s.b + 1) * P],
                                                     scalar=taps[:, k, w:w + 1], in1=acc[:, k, :],
                                                     op0=ALU.mult, op1=ALU.add).then_inc(taps_done, 1)
                    if hi == TAPS:
                        dve.wait_ge(taps_done, base + TAPS * KD)
                        dve.sem_inc(S["conv_done"], 1)
                    yield
                t = s.there
                dve.wait_ge(full[t.bank], t.full_after[0])
                issue(dve.bn_stats(stats[:, 0, :], tile_ap(t, 1024)[:, 0:512]))
                step(dve.bn_stats(stats[:, 1, :], tile_ap(t, 1024)[:, 512:1024]))
                signal("var_ready", dve.bn_aggr(meanvar[:], stats[:].rearrange("p a n -> p (a n)")))
                dve.wait_ge(S["std_ready"], s.std + 1)
                step(dve.reciprocal(rstd[:, 0:1], std[:, 0:1]))
                step(dve.tensor_scalar(cn_tile, tile_ap(t, 1024), meanvar[:, 0:1], rstd[:, 0:1], ALU.subtract, ALU.mult))
                dve.sem_inc(free[t.bank], 1)
                dve.sem_inc(S["cn_ready"], 1)
                yield

            def top16(values, where, scores_of, n):
                for g in range(n):
                    issue(dve.max(values[:, g, 0:8], scores_of(g)))
                settle()
                yield
                for g in range(n):
                    issue(dve.max_index(where[:, g, 0:8], values[:, g, 0:8], scores_of(g)))
                    issue(dve.match_replace(scores_of(g), values[:, g, 0:8], scores_of(g), LOW))
                    if g == n // 2 - 1:
                        yield
                settle()
                yield
                for g in range(n):
                    issue(dve.max(values[:, g, 8:16], scores_of(g)))
                settle()
                yield
                for g in range(n):
                    issue(dve.max_index(where[:, g, 8:16], values[:, g, 8:16], scores_of(g)))
                settle()
                yield

            def select(s):
                for _ in range(10):
                    yield
                dve.wait_ge(S["scores_ready"], s.sc + 2)
                yield from top16(top_v, top_i, lambda g: scores[:, g, :], 2 * PH)
                issue(dve.tensor_copy(top_f, top_i[:]))
                halves = top_v[:].rearrange("p (h two) n -> p h two n", two=2)
                step(dve.tensor_tensor(cand.rearrange("p h (a b) -> p h a b", a=TOPK),
                                       halves[:, :, 0, :, None].to_broadcast([P, PH, TOPK, TOPK]),
                                       halves[:, :, 1, None, :].to_broadcast([P, PH, TOPK, TOPK]), ALU.add))
                yield from top16(best_v, best_p, lambda h: cand[:, h, :], PH)
                issue(dve.tensor_copy(gate_sum[:], best_v[:, :, 0]))
                pos = best_p[:].rearrange("p h n -> p (h n)")
                issue(dve.tensor_scalar(part_u[:, 0, :], pos, 4, None, ALU.logical_shift_right))
                issue(dve.tensor_scalar(part_u[:, 1, :], pos, TOPK - 1, None, ALU.bitwise_and))
                settle()
                issue(dve.tensor_copy(part_f, part_u))
                signal("cand_ready", dve.tensor_tensor(best_v[:], best_v[:], gate_sum[:, :, None].to_broadcast([P, PH, TOPK]), ALU.subtract))
                settle()
                yield
                numbers = top_f.rearrange("p (h two) n -> p h two n", two=2)
                for half in range(2):
                    step(dve.tensor_tensor(onehot, part_f[:, half, :, None].to_broadcast([P, SLOTS_PER_BLOCK, TOPK]),
                                           iota16[:, None, :].to_broadcast([P, SLOTS_PER_BLOCK, TOPK]), ALU.is_equal))
                    view = onehot.rearrange("p (h s) n -> p h s n", h=PH)
                    step(dve.tensor_tensor(view, view, numbers[:, :, half, None, :].to_broadcast([P, PH, TOPK, TOPK]), ALU.mult))
                    yield
                    step(dve.tensor_reduce(part_f[:, half, :], onehot, AX.X, ALU.add))
                    if half == 0:
                        yield
                step(dve.scalar_tensor_tensor(out=part_f[:, 0, :], in0=part_f[:, 0, :], scalar=float(N_KEYS), in1=part_f[:, 1, :],
                                              op0=ALU.mult, op1=ALU.add))
                issue(dve.tensor_scalar(expert[:, s.b % 2, :], part_f[:, 0, :], float(s.layer * N_EXPERTS), None, ALU.add))
                dve.wait_ge(S["gate_exp"], s.exp + 1)
                step(dve.tensor_reduce(gate_sum[:], best_v[:], AX.X, ALU.add))
                step(dve.reciprocal(gate_sum[:], gate_sum[:]))
                signal("topk_ready", dve.tensor_tensor(gate[:, s.b % 2, :].rearrange("p (h n) -> p h n", h=PH), best_v[:],
                                                       gate_sum[:, :, None].to_broadcast([P, PH, TOPK]), ALU.mult))

            def gather(s):
                base = s.index * ITERS * NG
                par = s.b % 2
                dve.wait_ge(S["topk_ready"], s.index + 1)
                dve.wait_ge(S["h2_ready"], s.index + 1)

                def dot(i, g):
                    for k in range(g * GROUP, (g + 1) * GROUP):
                        dve.wait_ge(slot_landed[k], i * 16 + 16 * (s.index * ITERS + 1))
                        ins = dve.tensor_tensor_reduce(out=ring[:, k, 0:D], in0=ring[:, k, 0:D], in1=h2[:, par, :], scale=1.0,
                                                       scalar=0.0, op0=ALU.mult, op1=ALU.add, accum_out=dots[:, k:k + 1])
                    ins.then_inc(dots_ready, 1)

                def slot(i, k):
                    return slice(i * RING + k, i * RING + k + 1) if isinstance(i, int) else bass.ds(i * RING + k, 1)

                def weigh(i, g):
                    dve.wait_ge(acts_ready, i * NG + (base + g + 1))
                    for k in range(g * GROUP, (g + 1) * GROUP):
                        ins = dve.tensor_scalar(diag[:, k, :], ident[:], acts[:, k:k + 1],
                                                gate[:, par, slot(i, k)], ALU.mult, ALU.mult)
                    ins.then_inc(diag_ready, 1)

                if s.last - s.first == 1:
                    i, g = s.first // NG, s.first % NG
                    dot(i, g)
                    if s.first:
                        weigh((s.first - 1) // NG, (s.first - 1) % NG)
                    if s.last == ITERS * NG:
                        weigh(i, g)
                else:
                    with dve.Fori(s.first // NG, s.last // NG) as i:
                        for g in range(NG):
                            dot(i, g)
                            if g:
                                weigh(i, g - 1)
                        weigh(i, NG - 1)
                yield

            def finish(s):
                dve.wait_ge(slots_free, (s.index + 1) * ITERS * NG + NG)
                dve.wait_ge(S["row_ready"], s.rows)
                product = h2[:, s.b % 2, :]
                step(dve.tensor_tensor(product, ffn_out, g2_row[:], ALU.mult))
                dve.sem_inc(sums_read, 1)
                signal("x_updated", dve.tensor_tensor(x[:, s.b, :], x[:, s.b, :], product, ALU.add))
                yield

            run_phases({"ada": ada, "norm": norm, "heads": heads, "gating": gating, "attend": attend, "project": project,
                        "conv_in": conv_in, "conv": conv, "select": select, "gather": gather, "finish": finish}, "others")

        @block.tensor
        def _(pe):
            def claim(t):
                if t.frees_before:
                    pe.wait_ge(free[t.bank], t.frees_before)

            def turn(t, src, n):
                claim(t)
                for k in range(n):
                    ins = pe.transpose(psum[:, t.bank, k * P:(k + 1) * P], src[:, k * P:(k + 1) * P], ident[:])
                ins.then_inc(full[t.bank], 1)

            def rows(dst, column, start, stop):
                for k in range(KD):
                    ins = pe.matmul(dst[:, k * P:(k + 1) * P], column(k).to_broadcast([P, P]), ident[:], start=start and k % 4 == 0,
                                    stop=stop, skip_group_check=True)
                return ins

            def linear(t, part, left, c, begin=True):
                pe.wait_ge(landed[c.buf], c.landed)
                if part == 0 and begin:
                    claim(t)
                dst = psum[:, t.bank, part * COLS:(part + 1) * COLS]
                for k in range(KD):
                    if k == KD // 2:
                        yield
                    ins = pe.matmul(dst, left[:, k, :], buffers[c.buf][:, k, :], start=k == 0 and begin, stop=k == KD - 1,
                                    skip_group_check=not begin)
                ins.then_inc(full[t.bank], 1)

            def linear_t(t, part, right, c):
                pe.wait_ge(landed[c.buf], c.landed)
                if part == 0:
                    claim(t)
                for g in range(COLS // P):
                    if g == 2:
                        yield
                    dst = psum[:, t.bank, part * COLS + g * P:part * COLS + (g + 1) * P]
                    for k in range(KD):
                        ins = pe.matmul(dst, buffers[c.buf][:, k, g * P:(g + 1) * P], right[:, k, :], start=k == 0, stop=k == KD - 1)
                ins.then_inc(full[t.bank], 1)

            def ada(s):
                if s.first:
                    pe.wait_ge(cond_act, 1)
                for sec, chunks, t, modded, row in s.parts:
                    for j in range(2):
                        c = chunks[j]
                        pe.wait_ge(landed[c.buf], c.landed)
                        if j == 0:
                            claim(t)
                        for g in range(COLS // P):
                            col = 2 * (j * (COLS // P) + g)
                            for k in range(KD):
                                ins = pe.matmul(psum[:, t.bank, col:col + 2], buffers[c.buf][:, k, g * P:(g + 1) * P],
                                                cond_silu[:, :, k], start=k == 0, stop=k == KD - 1)
                        ins.then_inc(full[t.bank], 1)
                        yield
                    if row is not None:
                        pe.wait_ge(S["mod_ready"], modded + 1)
                        claim(row)
                        rows(tile_of(row), lambda k: mod[:, s.layer, sec, k:k + 1], True, True).then_inc(full[row.bank], 1)
                    yield

            def tile_of(t):
                return psum[:, t.bank, :]

            def norm(s):
                yield
                pe.wait_ge(S["h_ready"], s.h + 1)
                turn(s.tile, h_tile, KD)
                yield
                if s.dest:
                    pe.wait_ge(S["ht_ready"], s.ht + 1)
                    turn(s.back, h_t.rearrange("p k n -> p (k n)"), KD)
                yield

            def heads(s):
                def turned(n):
                    pe.wait_ge(S["qk_rotated"], s.turned + n + 1)
                    turn(s.turn[n], qk_rot, HEADS)

                pe.wait_ge(S["ht_ready"], s.ht)
                for n in range(len(s.tiles)):
                    yield from linear(s.proj[n], 0, ht_all[:, s.tiles[n]] if s.name == "k" else h_t, s.chunk)
                    if n:
                        turned(n - 1)
                    yield
                turned(len(s.tiles) - 1)
                yield

            def values(s):
                for n, tok in enumerate(s.tiles):
                    yield from linear(s.proj[n], 0, ht_all[:, tok], s.chunk)
                    yield

            def gating(s):
                yield from linear(s.ut, 0, h_t, s.u)
                yield
                yield from linear(s.vt, 0, h_t, s.vg)
                yield
                pe.wait_ge(S["vn_ready"], s.vn + 1)
                claim(s.mt)
                for g in range(GROUPS):
                    ins = pe.matmul(psum[:, s.mt.bank, g * P:(g + 1) * P], sgu_t[:, g, :], vn_tile[:, g * P:(g + 1) * P],
                                    start=True, stop=True)
                ins.then_inc(full[s.mt.bank], 1)
                yield

            def attend(s):
                pe.wait_ge(S["qkt_ready"], s.qkt)
                pe.wait_ge(S["v_ready"], s.v)

                def score(h):
                    for c in range(2):
                        t = s.score[h][c]
                        claim(t)
                        r = slice(c * QK, (c + 1) * QK)
                        for lo, hi in ((0, COLS), (COLS, KEYS)):
                            pe.matmul(psum[:, t.bank, lo:hi], q_t[r, h, :], k_t[r, h, lo:hi], start=True, stop=True).then_inc(
                                full[t.bank], 1)

                score(0)
                yield
                for h in range(HEADS):
                    if h + 1 < HEADS:
                        score(h + 1)
                    pe.wait_ge(S["probs_ready"], s.mix + h + 1)
                    turn(s.turn[h], probs[h % 2][0], NT)
                    yield
                    pe.wait_ge(S["probst_ready"], s.pt + h + 1)
                    t = s.out[h]
                    claim(t)
                    for kt in range(NT):
                        ins = pe.matmul(psum[:, t.bank, 0:VD], probs_t[:, kt, :], v_all[:, kt, h * VD:(h + 1) * VD],
                                        start=kt == 0, stop=kt == NT - 1)
                    ins.then_inc(full[t.bank], 1)
                    yield

            def project(s):
                if s.which == "even":
                    pe.wait_ge(S["cat_ready"], s.cat)
                    turn(s.turn, cat, KD)
                    yield
                    pe.wait_ge(S["left_ready"], s.left + 1)
                    left = h_t
                else:
                    pe.wait_ge(S["left_ready"], s.left_before)
                    left = cn_t
                    claim(s.tile)
                    rows(tile_of(s.tile), lambda k: conv_par[:, 3, k:k + 1], True, False)
                for j in range(2):
                    yield from linear(s.tile, j, left, s.chunks[j], begin=s.which == "even")
                    yield

            def conv_in(s):
                pe.wait_ge(S["ht_ready"], s.ht)
                for j in range(4):
                    yield from linear_t(s.gate if j < 2 else s.val, j % 2, h_t, s.chunks[j])
                    yield

            def conv(s):
                for _ in TAP_RUNS:
                    yield
                pe.wait_ge(S["conv_done"], s.conv + 1)
                turn(s.there, acc.rearrange("p k n -> p (k n)"), KD)
                yield
                pe.wait_ge(S["cn_ready"], s.cn + 1)
                turn(s.back, cn_tile, KD)
                yield

            def select(s):
                pe.wait_ge(S["ht_ready"], s.ht)
                for j in range(4):
                    yield from linear_t(s.q[j // 2], j % 2, h_t, s.chunks[j])
                    yield
                c = s.keys
                pe.wait_ge(landed[c.buf], c.landed)
                keys = buffers[c.buf].rearrange("p k n -> p (k n)")
                for j in range(2):
                    pe.wait_ge(S["pq_ready"], s.qt + j + 1)
                    t = s.s[j]
                    claim(t)
                    for g in range(8):
                        hp = 8 * j + g
                        ins = pe.matmul(psum[:, t.bank, g * P:(g + 1) * P], pq_t[:, hp, :], keys[:, hp * P:(hp + 1) * P],
                                        start=True, stop=True)
                        if g % 4 == 3:
                            ins.then_inc(full[t.bank], 1)
                    yield

            def gather(s):
                base = s.index * ITERS * NG
                if s.first == 0:
                    if s.index:
                        pe.wait_ge(sums_read, s.index)
                    pe.wait_ge(S["h2_ready"], s.index + 1)
                    for n in range(2):
                        pe.matmul(ffn_out[:, n * COLS:(n + 1) * COLS], zero_row[:], h2[0:1, s.b % 2, 0:COLS], start=True, stop=True)
                def add_up(i, g):
                    pe.wait_ge(diag_ready, i * NG + (base + g + 1))
                    for k in range(g * GROUP, (g + 1) * GROUP):
                        for n in range(2):
                            ins = pe.matmul(ffn_out[:, n * COLS:(n + 1) * COLS], diag[:, k, :],
                                            ring[:, k, D + n * COLS:D + (n + 1) * COLS], start=False, stop=True,
                                            skip_group_check=True)
                    ins.then_inc(slots_free, 1)

                if s.last - s.first == 1:
                    add_up(s.first // NG, s.first % NG)
                else:
                    with pe.Fori(s.first // NG, s.last // NG) as i:
                        for g in range(NG):
                            add_up(i, g)
                yield

            pe.sem_inc(slots_free, NG)
            pe.wait_ge(params, 16 * N_PARAMS)
            pe.wait_ge(consts, 1)
            run_phases({"ada": ada, "norm": norm, "heads": heads, "values": values, "gating": gating, "attend": attend,
                        "project": project, "conv_in": conv_in, "conv": conv, "select": select, "gather": gather}, "pe")


def layouts(np_, i):
    def chunked(w):
        return w.reshape(KD, P, -1, COLS).transpose(2, 1, 0, 3).reshape(-1, P, KD * COLS)

    f = np_.float32
    keys = i["peer_keys"].reshape(LAYERS, 2 * PH, N_KEYS, P).transpose(3, 0, 1, 2).reshape(1, P, 2 * 2048)
    chunks = np_.concatenate([
        chunked(i["ada_w"][0]), chunked(i["ada_w"][1]), chunked(i["ev_w_in"][0]), chunked(i["ev_w_out"][0]),
        chunked(i["od_pw1_w"][0]), chunked(i["od_pw2_w"][0]), chunked(i["peer_wq"][0]), chunked(i["peer_wq"][1]), keys])
    n = np_.arange(SEQ)
    grid = np_.stack([n // 64, n % 64], 1).astype(f)
    inv = (10000.0 ** (-np_.arange(QK // 4, dtype=f) / (QK // 4))).astype(f)
    ang = (grid[:, :, None] * inv).astype(f)
    cos = np_.stack([np_.cos(ang)] * 2, 2).reshape(SEQ, QK).astype(f)
    sin = np_.stack([-np_.sin(ang), np_.sin(ang)], 2).reshape(SEQ, QK).astype(f)

    def blocks(a):
        return a.reshape(NB, P, -1).transpose(1, 0, 2)

    def columns(a):
        return a.reshape(-1, KD, P).transpose(2, 0, 1)

    return {
        "x": i["x"][0], "ctx": i["ctx"][0],
        "cond": columns(np_.stack([i["c"][0], i["c_ctx"]])),
        "ident": np_.eye(P, dtype=f),
        "iota16": np_.tile(np_.arange(TOPK, dtype=f), (P, 1)),
        "rope_cos": blocks(cos), "rope_sin": blocks(sin),
        "gains": np_.stack([i["ev_q_gain"][0], i["ev_k_gain"][0]]),
        "lam": i["ev_lam"][0], "subln": i["ev_subln_g"][0],
        "vn_gain": np_.stack([i["ev_vnorm_g"][0], i["ev_vnorm_b"][0]]),
        "sgu_t": i["ev_sgu_w"][0].transpose(2, 0, 1), "sgu_bias": i["ev_sgu_b"][0].T,
        "taps": i["od_dw_w"][0].reshape(TAPS, KD, P).transpose(2, 1, 0),
        "conv_par": columns(np_.concatenate([i["od_dw_b"][0], i["od_ln_g"][0], i["od_ln_b"][0], i["od_pw2_b"][0], i["od_pw1_b"][0]])),
        "ada_bias": columns(i["ada_b"]).reshape(P, LAYERS, 6, KD),
        "chunks": chunks,
        "experts": np_.concatenate([i["peer_down"], i["peer_up"]], axis=2).reshape(LAYERS * N_EXPERTS, 2 * D),
    }


def kernel(**inputs):
    import concourse.bacc as bacc
    from concourse.bass_utils import run_bass_kernel_spmd

    laid = layouts(np, {k: np.asarray(v) for k, v in inputs.items()})
    nc = bacc.Bacc("TRN2", target_bir_lowering=False, num_devices=1)
    arrays, aps = {}, {}
    for name, a in laid.items():
        a = np.ascontiguousarray(a)
        arrays[f"in_{name}"] = a
        aps[name] = nc.dram_tensor(f"in_{name}", a.shape, mybir.dt.from_np(a.dtype), kind="ExternalInput").ap()
    out = nc.dram_tensor("out_x", (SEQ, D), F32, kind="ExternalOutput").ap()
    trunk_kernel(nc, aps, out)
    r = run_bass_kernel_spmd(nc, [arrays], core_ids=[0])
    return np.asarray(r.results[0]["out_x"]).reshape(1, SEQ, D)
```

```python
from contextlib import ExitStack

import numpy as np

import concourse.bass as bass
from concourse import mybir

F32 = mybir.dt.float32
U32 = mybir.dt.uint32
ALU = mybir.AluOpType
ACT = mybir.ActivationFunctionType
AX = mybir.AxisListType

P = 128
D = 1024
KD = D // P
SEQ = 512
CTX = 256
NB = SEQ // P
NT = (SEQ + CTX) // P
LAYERS = 2
EPS = 1e-6
COLS = 512

HEADS = 4
QK = 64
VD = 128
KEYS = SEQ + CTX
LAM_INIT = 0.8 - 0.6
SCALE = QK ** -0.5
GROUPS = 4

TAPS = 31
PAD = TAPS // 2

N_KEYS = 128
PH = 8
TOPK = 16
SLOTS_PER_BLOCK = PH * TOPK
N_EXPERTS = N_KEYS * N_KEYS
LOW = -3.0e38

RING = 8
GROUP = 2
NG = RING // GROUP
ITERS = SLOTS_PER_BLOCK // RING

ADA_CH = [0, 12]
Q_CH, K_CH, V_CH, U_CH, VG_CH = 24, 25, 26, 27, 28
OUT_CH = 29
PW1_CH = 31
PW2_CH = 35
WQ_CH = [37, 41]
KEY_CH = 45
N_CHUNKS = 46
SH1, SC1, G1, SH2, SC2, G2 = range(6)


class Tile:

    def __init__(self, bank, frees_before, full_after):
        self.bank, self.frees_before, self.full_after = bank, frees_before, full_after


class Chunk:

    def __init__(self, source, buf, landed, cols):
        self.source, self.buf, self.landed, self.cols, self.last_use = source, buf, landed, cols, None


class Stage:

    def __init__(self, kind, layer=None, b=None, name=None, tiles=None, which=None, src=None, dest=None, out_t=None,
                 mods=None, parts=None, first=None, last=None, cost=(0,)):
        self.kind, self.layer, self.b, self.name, self.tiles, self.which = kind, layer, b, name, tiles, which
        self.src, self.dest, self.out_t, self.mods, self.parts = src, dest, out_t, mods, parts
        self.first, self.last = first, last
        self.cost = cost


class Plan:

    DUOS = 3
    BUFS = 2
    EARLY = 2

    def __init__(self):
        self.uses = [0] * (self.DUOS + 1)
        self.fulls = [0] * (self.DUOS + 1)
        self.n = 0
        self.chunks = []
        self.early_chunks = []
        self.landed = [0] * (self.BUFS + self.EARLY)
        self.counts = {}
        self.order = []
        self.mod_counts = {}

    def tile(self, parts=1, early=False):
        d = self.DUOS if early else self.n % self.DUOS
        self.n += not early
        t = Tile(d, self.uses[d], [self.fulls[d] + i + 1 for i in range(parts)])
        self.uses[d] += 1
        self.fulls[d] += parts
        return t

    def chunk(self, source, cols=(0, KD * COLS), early=False):
        line = self.early_chunks if early else self.chunks
        b = self.BUFS + len(line) % self.EARLY if early else len(line) % self.BUFS
        self.landed[b] += 16
        c = Chunk(source, b, self.landed[b], cols)
        line.append(c)
        return c

    def used(self, chunk, tile, part):
        chunk.last_use = (tile.bank, tile.full_after[part])

    def take(self, name, k=1):
        before = self.counts.get(name, 0)
        self.counts[name] = before + k
        return before

    def so_far(self, name):
        return self.counts.get(name, 0)

    def ada(self, layer, sections):
        s = Stage("ada", layer=layer, parts=[], cost=(7, 7, 2) * len(sections))
        for sec in sections:
            chunks = [self.chunk(ADA_CH[layer] + 2 * sec + j, early=sec == SH1) for j in range(2)]
            line = self.tile(2, early=True)
            for j in range(2):
                self.used(chunks[j], line, j)
            s.parts.append((sec, chunks, line, self.tile(early=True), self.take("mod_ready")))
            self.mod_counts[layer, sec] = self.so_far("mod_ready")
        return s

    def side_ada(self, sections):
        s = Stage("side_ada", parts=[], cost=(1,) * (4 * len(sections) + 5))
        for layer, sec in sections:
            chunks = [self.chunk(ADA_CH[layer] + 2 * sec + j, early=True) for j in range(2)]
            for c in chunks:
                self.take("acc_ready")
                c.last_use = ("acc_ready", self.so_far("acc_ready"))
            s.parts.append((layer, sec, chunks, self.tile(2, early=True), sec in (G1, G2) and layer == 0))
            self.take("row_ready" if s.parts[-1][-1] else "mod_ready")
            self.mod_counts[layer, sec] = self.so_far("mod_ready")
        return s

    def gate_row(self, layer, sec):
        s = Stage("gate_row", layer=layer, which=sec, cost=(2,))
        s.tile = self.tile()
        s.mods = self.mod_counts[layer, sec]
        self.take("row_ready")
        return s

    def front_norms(self):
        s = Stage("front_norms", cost=(2, 12))
        s.std = self.take("std_ready")
        s.h = self.take("h_ready", NT)
        s.tile = [self.tile() for _ in range(NT)]
        self.take("ht_ready", NT)
        return s

    def norm(self, src, dest, out_t, mods):
        s = Stage("norm", src=src, dest=dest, out_t=out_t, mods=mods, cost=(2, 4, 3) if dest else (2, 4))
        s.x_updates = self.so_far("x_updated")
        s.topk_before = self.so_far("topk_ready")
        s.mod = max(self.mod_counts[mods], self.mod_counts[mods[0], mods[1] + 1])
        s.std = self.take("std_ready")
        s.h = self.take("h_ready")
        s.ht = self.take("ht_ready")
        s.tile = self.tile()
        if dest:
            s.back = self.tile()
            s.h2 = self.take("h2_ready")
        return s

    def heads(self, name, tiles, source, beside=None):
        s = Stage("heads", name=name, tiles=tiles, cost=(3.6, 4) * len(tiles) + (2,))
        s.ht = self.so_far("ht_ready")
        s.chunk = self.chunk(source)
        s.proj, s.turn = [None] * len(tiles), [None] * len(tiles)
        for n in range(len(tiles) + 1):
            if n < len(tiles):
                s.proj[n] = self.tile()
            if n:
                s.turn[n - 1] = self.tile()
            if n < len(tiles) and beside:
                beside.proj[n] = self.tile()
        self.used(s.chunk, s.proj[-1], 0)
        s.copied = self.take("qk_copied", len(tiles))
        s.summed = self.take("qk_summed", len(tiles))
        s.std = self.take("std_ready", len(tiles))
        s.turned = self.take("qk_rotated", len(tiles))
        s.done = self.take("qkt_ready", len(tiles))
        return s

    def keys_and_values(self, tiles):
        v = Stage("values", tiles=tiles, cost=(3.6, 3.6) * len(tiles))
        v.proj = [None] * len(tiles)
        k = self.heads("k", tiles, K_CH, v)
        v.chunk = self.chunk(V_CH)
        self.used(v.chunk, v.proj[-1], 0)
        self.take("v_ready", len(tiles))
        return k, v

    def gating(self, b):
        s = Stage("gating", b=b, cost=(3.6, 3.6, 3.6, 4, 3))
        s.ht = self.so_far("ht_ready")
        s.u, s.vg = self.chunk(U_CH), self.chunk(VG_CH)
        s.ut, s.vt, s.mt = self.tile(), self.tile(), self.tile()
        self.used(s.u, s.ut, 0)
        self.used(s.vg, s.vt, 0)
        s.u_ready = self.take("u_ready")
        s.var = self.take("var_ready")
        s.std = self.take("std_ready")
        s.vn = self.take("vn_ready")
        return s

    def attend(self, b):
        s = Stage("attend", b=b, cost=(8,) + (8, 2) * (HEADS - 1) + (2, 2, 4))
        s.qkt, s.v = self.so_far("qkt_ready"), self.so_far("v_ready")
        s.score, s.turn, s.out = [None] * HEADS, [None] * HEADS, [None] * HEADS
        s.score[0] = [self.tile(2), self.tile(2)]
        for h in range(HEADS):
            if h + 1 < HEADS:
                s.score[h + 1] = [self.tile(2), self.tile(2)]
            s.turn[h], s.out[h] = self.tile(), self.tile()
        s.max = self.take("max_ready", 2 * HEADS)
        s.exp = self.take("exp_ready", 2 * HEADS)
        s.mix = self.take("probs_ready", HEADS)
        s.pt = self.take("probst_ready", HEADS)
        s.o = self.take("o_ready", HEADS)
        s.ss = self.take("o_summed")
        s.std = self.take("std_ready")
        s.cat = self.take("cat_ready")
        return s

    def project(self, b, which):
        s = Stage("project", b=b, which=which, cost=(3, 3.6, 3.6, 3.6, 4) if which == "even" else (5, 3.6, 3.6, 4))
        s.rows = self.so_far("row_ready")
        if which == "even":
            s.cat = self.so_far("cat_ready")
            s.turn = self.tile()
        s.chunks = [self.chunk((OUT_CH if which == "even" else PW2_CH) + j) for j in range(2)]
        s.left_before = self.so_far("left_ready")
        s.left = self.take("left_ready") if which == "even" else None
        s.tile = self.tile(2)
        for j in range(2):
            self.used(s.chunks[j], s.tile, j)
        s.x = self.take("x_updated")
        return s

    def conv_in(self, b):
        s = Stage("conv_in", b=b, cost=(3.8,) * 16)
        s.ht = self.so_far("ht_ready")
        s.chunks = [self.chunk(PW1_CH + j) for j in (2, 0, 3, 1)]
        s.out = [self.tile() for _ in range(4)]
        for j in range(4):
            self.used(s.chunks[j], s.out[j], 0)
        s.sig = self.take("sig_ready", 2)
        s.z = self.take("z_ready", 2)
        return s

    def conv(self, b):
        s = Stage("conv", b=b, cost=(5.4,) * len(TAP_RUNS) + (5, 4))
        s.there, s.back = self.tile(), self.tile()
        s.conv = self.take("conv_done")
        s.var = self.take("var_ready")
        s.std = self.take("std_ready")
        s.cn = self.take("cn_ready")
        s.left = self.take("left_ready")
        return s

    def select(self, layer, b):
        s = Stage("select", layer=layer, b=b, cost=(4.2,) * 4 + (3,) + SELECT_COST * 2)
        s.ht = self.so_far("ht_ready")
        s.chunks, s.keys, s.q, s.s = [], [], [], []
        for half in range(2):
            wq = [self.chunk(WQ_CH[layer] + 2 * half + j) for j in range(2)]
            s.chunks += wq
            s.keys.append(self.chunk(KEY_CH, (layer * 2048 + half * 1024, layer * 2048 + (half + 1) * 1024)))
            s.q.append(self.tile(2))
            for j in range(2):
                self.used(wq[j], s.q[half], j)
            s.s.append(self.tile(2))
            self.used(s.keys[half], s.s[half], 1)
        s.qt = self.take("pq_ready", 2)
        s.sc = self.take("scores_ready", 2)
        s.top = self.take("cand_ready", 2)
        s.exp = self.take("gate_exp", 2)
        s.done = self.take("topk_ready", 2)
        return s

    def gather(self, layer, b, first, last):
        s = Stage("gather", layer=layer, b=b, first=first, last=last)
        s.index = layer * NB + b
        return s

    def finish(self, layer, b):
        s = Stage("finish", layer=layer, b=b)
        s.index = layer * NB + b
        s.rows = self.so_far("row_ready")
        s.x = self.take("x_updated")
        return s

    def run(self, stage):
        for n in range(len(stage.cost)):
            self.order.append((stage, n))

    def beside(self, layer, b, makers, begun=()):
        phases = list(begun) + phases_of(makers)
        weight = [s.cost[n] + 1.0 for s, n in phases]
        total, spent, at = sum(weight), 0.0, 0
        groups = ITERS * NG
        if not phases:
            self.run(self.gather(layer, b, 0, groups))
            groups = 0
        for i in range(groups):
            self.order.append((self.gather(layer, b, i, i + 1), 0))
            while at < len(phases) and spent + weight[at] / 2 < total * (i + 1) / (groups - AHEAD[layer]):
                spent += weight[at]
                self.order.append(phases[at])
                at += 1
        assert at == len(phases)
        self.run(self.finish(layer, b))

    def later(self):
        order, held, beside = [], [], False
        for s, phase in self.order:
            if s.kind == "gather" and s.last - s.first > 1:
                order += held + [(s, phase)]
                held = []
            elif s.kind == "gather":
                order += [(s, phase)] + held
                held, beside = [], True
            elif beside:
                held.append((s, phase))
            else:
                order.append((s, phase))
        return order + held


AHEAD = (6, 4)
SELECT_COST = (5, 5, 5, 4, 4, 4, 3)
ROOM = {"norm": (0, 0, 0), "gating": (1.5, 1.5, 1, 0, 0), "attend": (0,) * 10, "project": (0.5, 1.5, 1.5, 1, 0),
        "select": (2.5, 2.5, 2.5, 2.5) + (0,) * 15}
WITH_KV = 21
TAP_RUNS = [(lo, lo + 2) for lo in range(1, TAPS, 2)]


def phases_of(makers):
    stages = [make() for make in makers]
    phases = [(s, n) for s in stages for n in range(len(s.cost))]
    for late, n, after, m in (("heads", 2, "gating", 1), ("gating", 4, "attend", 0)):
        moved = [item for item in phases if (item[0].kind, item[1]) == (late, n)]
        if moved:
            phases.remove(moved[0])
            at = [(s.kind, k) for s, k in phases].index((after, m))
            phases.insert(at + 1, moved[0])
    return phases


def spread(p, phases, side):
    room = [ROOM[s.kind][n] if s.kind in ROOM else 1 for s, n in phases]
    done, so_far = 0, 0.0
    for item, r in zip(phases, room):
        p.order.append(item)
        so_far += r
        while done < len(side) and done < round(len(side) * so_far / sum(room), 6):
            p.order.append(side[done])
            done += 1


def make_plan():
    p = Plan()

    def ffn_prep(layer, b):
        return [lambda: p.norm(("x", b), ("h2", b % 2), ("one", 0), (layer, SH2)), lambda: p.select(layer, b)]

    def even(b):
        return [lambda: p.norm(("x", b), None, ("one", 0), (0, SH1)), lambda: p.heads("q", [b + CTX // P], Q_CH),
                lambda: p.gating(b), lambda: p.attend(b), lambda: p.project(b, "even")] + ffn_prep(0, b)

    def pointwise(b):
        return [lambda: p.norm(("x", b), None, ("pair", 0), (1, SH1)), lambda: p.norm(("x", b + 1), None, ("pair", 1), (1, SH1)),
                lambda: p.conv_in(b)]

    def odd(b):
        return [lambda: p.conv(b), lambda: p.project(b, "odd")] + ffn_prep(1, b)

    first, norms = p.ada(0, [SH1, SC1]), p.front_norms()
    p.order += [(first, 0), (first, 1), (first, 2), (norms, 0), (first, 3), (first, 4), (first, 5), (norms, 1)]
    p.run(Stage("lam"))
    k, v = p.keys_and_values(list(range(NT)))
    rest = p.side_ada([(0, G1), (0, G2), (0, SH2), (0, SC2), (1, SH1), (1, SC1), (1, G1), (1, SH2), (1, SC2), (1, G2)])
    kv = [item for n in range(NT) for item in ((k, 2 * n), (k, 2 * n + 1), (v, 2 * n), (v, 2 * n + 1))] + [(k, 2 * NT)]
    first_block = phases_of(even(0))
    side = [(rest, n) for n in range(len(rest.cost))]
    spread(p, kv, side[:WITH_KV])
    spread(p, first_block[:-10], side[WITH_KV:])
    p.order += first_block[-10:-7]
    p.beside(0, 0, even(1), first_block[-7:])
    p.beside(0, 1, even(2))
    p.beside(0, 2, even(3) + pointwise(0))
    p.beside(0, 3, [lambda: p.gate_row(1, G1)] + odd(0))
    p.beside(1, 0, pointwise(2) + [lambda: p.gate_row(1, G2)] + odd(1))
    p.beside(1, 1, odd(2))
    p.beside(1, 2, odd(3))
    p.beside(1, 3, [])
    return p


def trunk_kernel(nc, A, out):
    plan = make_plan()
    with ExitStack() as ctx:
        def sb(name, shape, dt=F32):
            return ctx.enter_context(nc.sbuf_tensor(name, shape, dt))

        def sem(name):
            return ctx.enter_context(nc.semaphore(name))

        x = sb("x", [P, NB, D])
        mod = sb("mod", [P, LAYERS, 6, KD])
        ctx_mod = sb("ctx_mod", [P, 2, KD])
        ada_bias = sb("ada_bias", [P, LAYERS, 6, KD])
        g1_row = sb("g1_row", [P, D])
        g2_row = sb("g2_row", [P, D])
        ring = sb("ring", [P, RING, 2 * D])
        h2 = sb("h2", [P, 2, D])
        kept = sb("kept", [P, 6144])
        weights = sb("weights", [P, Plan.BUFS, KD, COLS])
        arena = sb("arena", [P, 8192])
        ident = sb("ident", [P, P])
        zero_row = sb("zero_row", [1, P])
        ones = sb("ones", [P, P])
        eps = sb("eps", [P, 1])
        iota16 = sb("iota16", [P, TOPK])
        cond = sb("cond", [P, 2, KD])
        cond_silu = sb("cond_silu", [P, 2, KD])
        rope_cos = sb("rope_cos", [P, NB, QK])
        rope_sin = sb("rope_sin", [P, NB, QK])
        gains = sb("gains", [P, 2, QK])
        subln = sb("subln", [P, VD])
        sgu_t = sb("sgu_t", [P, GROUPS, P])
        sgu_bias = sb("sgu_bias", [P, GROUPS])
        taps = sb("taps", [P, KD, TAPS])
        conv_par = sb("conv_par", [P, 4 + 2, KD])
        vn_gain = sb("vn_gain", [P, 2, COLS])
        neg_lam = sb("neg_lam", [P, 1])
        sumsq = sb("sumsq", [P, 8])
        std = sb("std", [P, 8])
        rstd = sb("rstd", [P, 8])
        stats = sb("stats", [P, 2, 6])
        meanvar = sb("meanvar", [P, 2])
        peak = sb("peak", [P, 2, 2])
        neg_peak = sb("neg_peak", [P, 2, 2])
        expsum = sb("expsum", [P, 2, 2])
        inv_sum = sb("inv_sum", [P, 2, 2])
        top_v = sb("top_v", [P, 2 * PH, TOPK])
        top_i = sb("top_i", [P, 2 * PH, TOPK], U32)
        best_v = sb("best_v", [P, PH, TOPK])
        best_p = sb("best_p", [P, PH, TOPK], U32)
        gate_sum = sb("gate_sum", [P, PH])
        expert = sb("expert", [P, 2, SLOTS_PER_BLOCK], U32)
        gate = sb("gate", [P, 2, SLOTS_PER_BLOCK])
        staged = sb("staged", [P, RING], U32)
        dots = sb("dots", [P, RING])
        acts = sb("acts", [P, RING])
        diag = sb("diag", [P, RING, P])
        psum = ctx.enter_context(nc.psum_tensor("psum", [P, 4, 2 * COLS], F32))
        ffn_out = psum[:, 3, :]

        store = ring[:].rearrange("p s n -> p (s n)")
        ht_all = store[:, 0:6144].rearrange("p (t k n) -> p t k n", t=NT, k=KD)
        ctx_x = store[:, 6144:8192].rearrange("p (t n) -> p t n", t=CTX // P)
        buffers = [weights[:, i] for i in range(Plan.BUFS)] + [
            store[:, 8192 + i * KD * COLS:8192 + (i + 1) * KD * COLS].rearrange("p (k n) -> p k n", k=KD) for i in range(Plan.EARLY)]
        k_t = kept[:, 0:3072].rearrange("p (h t) -> p h t", h=HEADS)
        v_all = kept[:, 3072:6144].rearrange("p (t n) -> p t n", t=NT)
        ZW = SEQ + 2 * PAD
        z_t = kept[:, 0:KD * ZW].rearrange("p (k t) -> p k t", k=KD)

        def at(start, n):
            return arena[:, start:start + n]

        h_tile = at(0, 1024)
        front_h = [at(t * D, D) for t in range(NT)]
        mod_line = h2[0:2, 1, :]
        diag_rows = diag[:].rearrange("p s n -> p (s n)")
        mod_acc = [h2[:, 1, 0:COLS], h2[:, 1, COLS:D], diag_rows[:, 0:COLS], diag_rows[:, COLS:D]]
        h_t = at(1024, 1024).rearrange("p (k n) -> p k n", k=KD)
        q_t = at(2048, 512).rearrange("p (h n) -> p h n", h=HEADS)
        qk_raw, qk_sq, qk_rot = at(2560, 512), at(3072, 512), at(3584, 512)
        u_tile, vn_tile = at(4096, 512), at(4608, 512)
        o_tile, o_sq = at(5120, 512), at(3584, 512)
        cat = at(5632, 1024)
        probs = [[at(0, KEYS), at(1024, KEYS)], [at(4096, KEYS), at(6656, KEYS)]]
        lam_in = at(6144, 4 * QK).rearrange("p (a n) -> p a n", a=4)
        probs_t = at(2560, 768).rearrange("p (t n) -> p t n", t=NT)
        pq_t = at(2048, 2048).rearrange("p (g n) -> p g n", g=2 * PH)
        scores = at(4096, 2048).rearrange("p (g n) -> p g n", g=2 * PH)
        cand = at(6144, 2048).rearrange("p (h n) -> p h n", h=PH)
        onehot = at(2048, 1024).rearrange("p (s n) -> p s n", n=TOPK)
        top_f = at(4096, 256).rearrange("p (g n) -> p g n", n=TOPK)
        part_u = at(4352, 256).bitcast(U32).rearrange("p (a n) -> p a n", a=2)
        part_f = at(4608, 256).rearrange("p (a n) -> p a n", a=2)
        h_pair = at(1024, 2048).rearrange("p (k n) -> p k n", k=KD)
        sig = at(3072, 1024)
        pw1_bias = conv_par[:, 4:6, :]
        acc = at(4096, 1024).rearrange("p (k n) -> p k n", k=KD)
        cn_tile = at(6144, 1024)
        cn_t = at(7168, 1024).rearrange("p (k n) -> p k n", k=KD)

        params = sem("params_landed")
        cond_landed, first_params = sem("cond_landed"), sem("first_params_landed")
        x_landed = sem("x_landed")
        consts = sem("consts_ready")
        landed = [sem(f"chunk_landed{i}") for i in range(Plan.BUFS + Plan.EARLY)]
        full = [sem(f"psum_full{i}") for i in range(Plan.DUOS + 1)]
        free = [sem(f"psum_free{i}") for i in range(Plan.DUOS + 1)]
        act_step, dve_step = sem("act_step"), sem("dve_step")
        S = {n: sem(n) for n in (
            "raw_ready", "line_ready", "acc_ready",
            "std_ready", "h_ready", "ht_ready", "h2_ready", "row_ready", "mod_ready", "qk_copied", "qk_summed", "qk_rotated",
            "qkt_ready", "v_ready", "u_ready", "var_ready", "vn_ready", "max_ready", "exp_ready",
            "probs_ready", "probst_ready", "o_ready", "o_summed", "cat_ready", "left_ready", "x_updated", "sig_ready",
            "z_ready", "conv_done", "cn_ready", "pq_ready", "scores_ready", "cand_ready",
            "gate_exp", "topk_ready")}
        lam_sum, lam_exp, cond_act = sem("lam_sum"), sem("lam_exp"), sem("cond_act")
        slot_landed = [sem(f"slot_landed{i}") for i in range(RING)]
        staged_ready, staged_seen = sem("staged_ready"), sem("staged_seen")
        dots_ready, acts_ready, diag_ready = sem("dots_ready"), sem("acts_ready"), sem("diag_ready")
        slots_free = sem("slots_free")
        taps_done = sem("taps_done")
        stored = sem("stored")
        sums_read = sem("sums_read")

        N_PARAMS = 11
        orders = {"pe": plan.order, "others": plan.later()}

        def run_phases(functions, order):
            running = {}
            for s, phase in orders[order]:
                if s.kind not in functions:
                    continue
                if phase == 0:
                    running[s.kind] = functions[s.kind](s)
                next(running[s.kind], None)

        block = ctx.enter_context(nc.Block())

        @block.sync
        def _(sp):
            sp.dma_start(cond[:], A["cond"]).then_inc(cond_landed, 16)
            sp.dma_start(ident[:], A["ident"]).then_inc(first_params, 16)
            sp.dma_start(ada_bias[:], A["ada_bias"]).then_inc(first_params, 16)
            def load_chunk(n):
                c = plan.chunks[n]
                if n >= Plan.BUFS:
                    sp.wait_ge(full[plan.chunks[n - Plan.BUFS].last_use[0]], plan.chunks[n - Plan.BUFS].last_use[1])
                lo, hi = c.cols
                sp.dma_start(buffers[c.buf].rearrange("p k n -> p (k n)")[:, 0:hi - lo],
                             A["chunks"][c.source, :, lo:hi]).then_inc(landed[c.buf], 16)

            load_chunk(0)
            load_chunk(1)
            sp.dma_start(ctx_x, A["ctx"].rearrange("(t p) n -> p t n", p=P)).then_inc(x_landed, 16)
            sp.dma_start(x[:], A["x"].rearrange("(t p) n -> p t n", p=P)).then_inc(x_landed, 16)
            sp.dma_start(iota16[:], A["iota16"]).then_inc(params, 16)
            sp.dma_start(rope_cos[:], A["rope_cos"]).then_inc(params, 16)
            sp.dma_start(rope_sin[:], A["rope_sin"]).then_inc(params, 16)
            sp.dma_start(gains[:], A["gains"].partition_broadcast(P)).then_inc(params, 16)
            sp.dma_start(lam_in[:], A["lam"].partition_broadcast(P)).then_inc(params, 16)
            sp.dma_start(subln[:], A["subln"].partition_broadcast(P)).then_inc(params, 16)
            sp.dma_start(vn_gain[:], A["vn_gain"].partition_broadcast(P)).then_inc(params, 16)
            sp.dma_start(sgu_t[:], A["sgu_t"]).then_inc(params, 16)
            sp.dma_start(sgu_bias[:], A["sgu_bias"]).then_inc(params, 16)
            sp.dma_start(taps[:], A["taps"]).then_inc(params, 16)
            sp.dma_start(conv_par[:], A["conv_par"]).then_inc(params, 16)
            for n in range(2, len(plan.chunks)):
                load_chunk(n)
            n_out = 0
            for s, _ in plan.order:
                if s.kind == "finish" and s.layer == LAYERS - 1:
                    sp.wait_ge(S["x_updated"], s.x + 1)
                    sp.dma_start(out[s.b * P:(s.b + 1) * P, :], x[:, s.b, :]).then_inc(stored, 16)
                    n_out += 1
            sp.wait_ge(stored, 16 * n_out)

        @block.gpsimd
        def _(pool):
            for n, c in enumerate(plan.early_chunks):
                if n >= Plan.EARLY:
                    used = plan.early_chunks[n - Plan.EARLY].last_use
                    pool.wait_ge(S["acc_ready"] if used[0] == "acc_ready" else full[used[0]], used[1])
                pool.dma_start(buffers[c.buf].rearrange("p k n -> p (k n)"), A["chunks"][c.source]).then_inc(landed[c.buf], 16)
            pool.wait_ge(S["acc_ready"], plan.so_far("acc_ready"))
            table = A["experts"]

            def gathers(base, par, lo, hi):
                with pool.Fori(lo, hi) as i:
                    for g in range(NG):
                        pool.wait_ge(slots_free, i * NG + (base + g + 1))
                        pool.tensor_copy(staged[:, g * GROUP:(g + 1) * GROUP],
                                         expert[:, par, bass.ds(i * RING + g * GROUP, GROUP)]).then_inc(staged_ready, 1)
                        pool.wait_ge(staged_ready, i * NG + (base + g + 1))
                        pool.sem_inc(staged_seen, 1)
                        for k in range(g * GROUP, (g + 1) * GROUP):
                            pool.indirect_dma_start(
                                out=ring[:, k, :], out_offset=None, in_=table,
                                in_offset=bass.IndirectOffsetOnAxis(ap=staged[:, k:k + 1], axis=0),
                            ).then_inc(slot_landed[k], 16)

            for s, _ in plan.order:
                if s.kind != "gather" or s.first:
                    continue
                base = s.index * ITERS * NG
                for half in range(2):
                    pool.wait_ge(S["topk_ready"], 2 * s.index + half + 1)
                    gathers(base, s.b % 2, half * ITERS // 2, (half + 1) * ITERS // 2)

        @block.scalar
        def _(act):
            steps = [0]

            def step(ins):
                steps[0] += 1
                ins.then_inc(act_step, 1)
                act.wait_ge(act_step, steps[0])

            def tile_ap(t, n):
                return psum[:, t.bank, 0:n]

            def await_tile(t, part=-1):
                act.wait_ge(full[t.bank], t.full_after[part])

            def evacuate(dst, t, src, name):
                await_tile(t)
                step(act.activation(dst, src, ACT.Copy))
                act.sem_inc(free[t.bank], 1)
                act.sem_inc(S[name], 1)

            act.wait_ge(cond_landed, 16)
            act.activation(cond_silu[:], cond[:], ACT.Silu).then_inc(cond_act, 1)

            def signal(name, ins):
                ins.then_inc(S[name], 1)

            def ada(s):
                for sec, chunks, line, column, modded in s.parts:
                    yield
                    if modded:
                        act.wait_ge(S["mod_ready"], modded)
                    evacuate(mod_line, line, psum[0:2, line.bank, :], "line_ready")
                    yield
                    yield

            def side_ada(s):
                for _ in range(5):
                    yield
                for layer, sec, chunks, t, is_row in s.parts:
                    yield
                    yield
                    if is_row:
                        evacuate(g1_row[:] if sec == G1 else g2_row[:], t, tile_ap(t, D), "row_ready")
                    yield
                    yield

            def front_norms(s):
                act.wait_ge(x_landed, 32)
                act.wait_ge(consts, 3)
                for t in range(NT):
                    src = ctx_x[:, t, :] if t < CTX // P else x[:, t - CTX // P, :]
                    ins = act.activation(front_h[t], src, ACT.Square, accum_out=sumsq[:, t:t + 1])
                step(ins)
                signal("std_ready", act.activation(std[:, 0:NT], sumsq[:, 0:NT], ACT.Sqrt, bias=eps[:], scale=1.0 / D))
                yield
                act.wait_ge(S["mod_ready"], 2)
                for t in range(0, NT, 2):
                    await_tile(s.tile[t])
                    shift, scale = (ctx_mod[:, SH1], ctx_mod[:, SC1]) if t < CTX // P else (mod[:, 0, SH1], mod[:, 0, SC1])
                    for k in range(KD):
                        ins = act.activation(ht_all[:, t, k, :], tile_ap(s.tile[t], D)[:, k * P:(k + 1) * P], ACT.Identity,
                                             bias=shift[:, k:k + 1], scale=scale[:, k:k + 1])
                    step(ins)
                    act.sem_inc(free[s.tile[t].bank], 1)
                    act.sem_inc(S["ht_ready"], 1)
                yield

            def lam(s):
                act.wait_ge(params, 16 * N_PARAMS)
                act.wait_ge(lam_sum, 1)
                act.activation(inv_sum[:, 0, :], sumsq[:, 0:2], ACT.Exp).then_inc(lam_exp, 1)
                act.wait_ge(lam_exp, 1)
                yield

            def gate_row(s):
                if s.which == G2:
                    act.wait_ge(sums_read, s.layer * NB)
                evacuate(g1_row[:] if s.which == G1 else g2_row[:], s.tile, tile_ap(s.tile, 1024), "row_ready")
                yield

            def norm(s):
                if s.x_updates:
                    act.wait_ge(S["x_updated"], s.x_updates)
                if s.topk_before:
                    act.wait_ge(S["topk_ready"], s.topk_before)
                if s.h:
                    act.wait_ge(S["h_ready"], s.h)
                src = x[:, s.src[1], :]
                if s.h:
                    act.wait_ge(S["ht_ready"], s.ht)
                step(act.activation(h_tile, src, ACT.Square, accum_out=sumsq[:, 0:1]))
                signal("std_ready", act.activation(std[:, 0:1], sumsq[:, 0:1], ACT.Sqrt, bias=eps[:], scale=1.0 / D))
                yield
                await_tile(s.tile)
                act.wait_ge(S["mod_ready"], s.mod)
                if s.out_t[0] == "pair":
                    dst = h_pair[:, :, s.out_t[1] * P:(s.out_t[1] + 1) * P]
                else:
                    dst = h_t
                layer, sec = s.mods
                for k in range(KD):
                    shift, scale = mod[:, layer, sec, k:k + 1], mod[:, layer, sec + 1, k:k + 1]
                    ins = act.activation(dst[:, k, :], tile_ap(s.tile, 1024)[:, k * P:(k + 1) * P], ACT.Identity, bias=shift, scale=scale)
                step(ins)
                act.sem_inc(free[s.tile.bank], 1)
                act.sem_inc(S["ht_ready"], 1)
                yield
                if s.dest:
                    evacuate(h2[:, s.dest[1], :], s.back, tile_ap(s.back, 1024), "h2_ready")
                yield

            def heads(s):
                def turned(n):
                    tok = s.tiles[n]
                    dst = k_t[:, :, tok * P:(tok + 1) * P] if s.name == "k" else q_t
                    evacuate(dst, s.turn[n], tile_ap(s.turn[n], 512).rearrange("p (h n) -> p h n", h=HEADS), "qkt_ready")

                for n in range(len(s.tiles)):
                    yield
                    if n:
                        act.wait_ge(S["qk_rotated"], s.turned + n)
                    evacuate(qk_raw, s.proj[n], tile_ap(s.proj[n], 512), "raw_ready")
                    signal("qk_copied", act.activation(qk_sq, qk_raw, ACT.Square))
                    act.wait_ge(S["qk_summed"], s.summed + n + 1)
                    signal("std_ready", act.activation(std[:], sumsq[:], ACT.Sqrt, bias=eps[:], scale=1.0 / QK))
                    if n:
                        turned(n - 1)
                    yield
                turned(len(s.tiles) - 1)
                yield

            def values(s):
                for n, tok in enumerate(s.tiles):
                    yield
                    evacuate(v_all[:, tok, :], s.proj[n], tile_ap(s.proj[n], 512), "v_ready")
                    yield

            def gating(s):
                yield
                evacuate(u_tile, s.ut, tile_ap(s.ut, 512), "u_ready")
                yield
                yield
                act.wait_ge(S["var_ready"], s.var + 1)
                signal("std_ready", act.activation(std[:, 0:1], meanvar[:, 1:2], ACT.Sqrt, bias=eps[:]))
                yield

            def attend(s):
                def exps(h):
                    for c in range(2):
                        t = s.score[h][c]
                        await_tile(t)
                        act.wait_ge(S["max_ready"], s.max + 2 * h + c + 1)
                        step(act.activation(probs[h % 2][c], tile_ap(t, KEYS), ACT.Exp,
                                            bias=neg_peak[:, h % 2, c:c + 1], scale=SCALE,
                                            accum_out=expsum[:, h % 2, c:c + 1]))
                        act.sem_inc(free[t.bank], 1)
                        act.sem_inc(S["exp_ready"], 1)

                exps(0)
                yield
                for h in range(HEADS):
                    if h + 1 < HEADS:
                        exps(h + 1)
                    evacuate(probs_t.rearrange("p t n -> p (t n)"), s.turn[h], tile_ap(s.turn[h], KEYS), "probst_ready")
                    yield
                    evacuate(o_tile[:, h * VD:(h + 1) * VD], s.out[h], tile_ap(s.out[h], VD), "o_ready")
                    yield
                act.wait_ge(S["o_summed"], s.ss + 1)
                signal("std_ready", act.activation(std[:, 0:HEADS], sumsq[:, 0:HEADS], ACT.Sqrt, bias=eps[:], scale=1.0 / VD))
                yield

            def project(s):
                if s.which == "even":
                    evacuate(h_t.rearrange("p k n -> p (k n)"), s.turn, tile_ap(s.turn, 1024), "left_ready")
                yield

            def conv_in(s):
                for j in range(4):
                    for _ in range(3):
                        yield
                    if j % 2 == 0:
                        t = s.out[j]
                        await_tile(t)
                        if j:
                            act.wait_ge(S["z_ready"], s.z + 1)
                        for g in range(4):
                            ins = act.activation(sig[:, 2 * g * P:2 * (g + 1) * P], tile_ap(t, 1024)[:, 2 * g * P:2 * (g + 1) * P],
                                                 ACT.Sigmoid, bias=pw1_bias[:, 1, 2 * j + g:2 * j + g + 1])
                        step(ins)
                        act.sem_inc(free[t.bank], 1)
                        act.sem_inc(S["sig_ready"], 1)
                    yield

            def conv(s):
                for _ in TAP_RUNS:
                    yield
                act.wait_ge(S["var_ready"], s.var + 1)
                signal("std_ready", act.activation(std[:, 0:1], meanvar[:, 1:2], ACT.Sqrt, bias=eps[:]))
                yield
                t = s.back
                await_tile(t)
                for k in range(KD):
                    ins = act.activation(cn_t[:, k, :], tile_ap(t, 1024)[:, k * P:(k + 1) * P], ACT.Silu,
                                         bias=conv_par[:, 2, k:k + 1], scale=conv_par[:, 1, k:k + 1])
                step(ins)
                act.sem_inc(free[t.bank], 1)
                act.sem_inc(S["left_ready"], 1)
                yield

            def select(s):
                def exponent(half):
                    act.wait_ge(S["cand_ready"], s.top + half + 1)
                    bv = best_v[:, 4 * half:4 * half + 4, :]
                    signal("gate_exp", act.activation(bv, bv, ACT.Exp))

                for half in range(2):
                    yield
                    yield
                    yield
                    evacuate(pq_t[:, 8 * half:8 * half + 8, :].rearrange("p g n -> p (g n)"), s.q[half], tile_ap(s.q[half], 1024), "pq_ready")
                    yield
                    if half:
                        exponent(0)
                    evacuate(scores[:, 8 * half:8 * half + 8, :].rearrange("p g n -> p (g n)"), s.s[half], tile_ap(s.s[half], 1024),
                             "scores_ready")
                    yield
                for _ in range(6):
                    yield
                exponent(1)
                yield

            def gather(s):
                base = s.index * ITERS * NG
                if s.last - s.first == 1:
                    lo = s.first % NG * GROUP
                    act.wait_ge(dots_ready, base + s.last)
                    act.activation(acts[:, lo:lo + GROUP], dots[:, lo:lo + GROUP], ACT.Gelu).then_inc(acts_ready, 1)
                else:
                    with act.Fori(s.first // NG, s.last // NG) as i:
                        for g in range(NG):
                            lo, hi = g * GROUP, (g + 1) * GROUP
                            act.wait_ge(dots_ready, i * NG + (base + g + 1))
                            act.activation(acts[:, lo:hi], dots[:, lo:hi], ACT.Gelu).then_inc(acts_ready, 1)
                yield

            run_phases({"ada": ada, "side_ada": side_ada, "front_norms": front_norms, "lam": lam, "norm": norm, "heads": heads, "values": values, "gate_row": gate_row, "gating": gating, "attend": attend,
                        "project": project, "conv_in": conv_in, "conv": conv, "select": select, "gather": gather}, "others")

        @block.vector
        def _(dve):
            steps = [0]

            def issue(ins):
                steps[0] += 1
                ins.then_inc(dve_step, 1)

            def settle():
                dve.wait_ge(dve_step, steps[0])

            def step(ins):
                issue(ins)
                settle()

            def signal(name, ins):
                ins.then_inc(S[name], 1)

            def bc(ap, shape):
                return ap.to_broadcast(shape)

            def tile_ap(t, n):
                return psum[:, t.bank, 0:n]

            dve.memset(eps[:], EPS).then_inc(consts, 1)
            dve.memset(zero_row[:], 0.0).then_inc(consts, 1)
            dve.memset(ones[:], 1.0).then_inc(consts, 1)
            dve.wait_ge(first_params, 32)

            def front_norms(s):
                dve.wait_ge(S["std_ready"], s.std + 1)
                step(dve.reciprocal(rstd[:, 0:NT], std[:, 0:NT]))
                for t in range(NT):
                    src = ctx_x[:, t, :] if t < CTX // P else x[:, t - CTX // P, :]
                    signal("h_ready", dve.tensor_scalar(front_h[t], src, rstd[:, t:t + 1], None, ALU.mult))
                yield
                for t in range(1, NT, 2):
                    tile = s.tile[t]
                    dve.wait_ge(full[tile.bank], tile.full_after[0])
                    shift, scale = (ctx_mod[:, SH1], ctx_mod[:, SC1]) if t < CTX // P else (mod[:, 0, SH1], mod[:, 0, SC1])
                    for k in range(KD):
                        issue(dve.tensor_scalar(ht_all[:, t, k, :], tile_ap(tile, D)[:, k * P:(k + 1) * P], scale[:, k:k + 1],
                                                shift[:, k:k + 1], ALU.mult, ALU.add))
                    settle()
                    dve.sem_inc(free[tile.bank], 1)
                    dve.sem_inc(S["ht_ready"], 1)
                yield

            def lam(s):
                dve.wait_ge(params, 16 * N_PARAMS)
                dve.wait_ge(S["ht_ready"], NT)
                lam_prod = qk_raw[:, 0:2 * QK].rearrange("p (a n) -> p a n", a=2)
                step(dve.tensor_tensor(lam_prod, lam_in[:, 0:4:2, :], lam_in[:, 1:4:2, :], ALU.mult))
                dve.tensor_reduce(sumsq[:, 0:2], lam_prod, AX.X, ALU.add).then_inc(lam_sum, 1)
                step(dve.tensor_scalar(subln[:], subln[:], 1.0 - LAM_INIT, None, ALU.mult))
                dve.wait_ge(lam_exp, 1)
                step(dve.scalar_tensor_tensor(out=neg_lam[:], in0=inv_sum[:, 0, 1:2], scalar=-LAM_INIT, in1=inv_sum[:, 0, 0:1],
                                              op0=ALU.add, op1=ALU.subtract))
                yield

            def ada(s):
                for sec, chunks, line, column, modded in s.parts:
                    yield
                    yield
                    dve.wait_ge(full[column.bank], column.full_after[-1])
                    both = tile_ap(column, 2 * KD).rearrange("p (k c) -> p c k", c=2)
                    for dst, c in ((ctx_mod[:, sec, :], 1), (mod[:, s.layer, sec, :], 0)):
                        issue(dve.scalar_tensor_tensor(out=dst, in0=both[:, c, :], scalar=1.0 if sec == SC1 else 0.0,
                                                       in1=ada_bias[:, s.layer, sec, :], op0=ALU.add, op1=ALU.add))
                    settle()
                    dve.sem_inc(free[column.bank], 1)
                    dve.sem_inc(S["mod_ready"], 1)
                    yield

            def side_ada(s):
                def columns(layer, sec, chunks, t, is_row):
                    if is_row:
                        return
                    dve.wait_ge(full[t.bank], t.full_after[-1])
                    step(dve.scalar_tensor_tensor(out=mod[:, layer, sec, :], in0=tile_ap(t, 2 * KD)[:, 0:2 * KD:2],
                                                  scalar=1.0 if sec in (SC1, SC2) else 0.0, in1=ada_bias[:, layer, sec, :],
                                                  op0=ALU.add, op1=ALU.add))
                    dve.sem_inc(free[t.bank], 1)
                    dve.sem_inc(S["mod_ready"], 1)

                for p, (layer, sec, chunks, t, is_row) in enumerate(s.parts):
                    if p >= 2:
                        columns(*s.parts[p - 2])
                    for j in range(2):
                        c, acc_j = chunks[j], mod_acc[2 * (p % 2) + j]
                        dve.wait_ge(landed[c.buf], c.landed)
                        if p >= 2:
                            before = s.parts[p - 2][3]
                            dve.wait_ge(full[before.bank], before.full_after[j])
                        for k in range(KD):
                            weight, scale = buffers[c.buf][:, k, :], cond_silu[:, 0, k:k + 1]
                            if k == 0:
                                ins = dve.tensor_scalar(acc_j, weight, scale, None, ALU.mult)
                            else:
                                ins = dve.scalar_tensor_tensor(out=acc_j, in0=weight, scalar=scale, in1=acc_j,
                                                               op0=ALU.mult, op1=ALU.add)
                            step(ins)
                            if k == KD // 2 - 1:
                                yield
                        dve.sem_inc(S["acc_ready"], 1)
                        yield
                columns(*s.parts[-2])
                for _ in range(4):
                    yield
                columns(*s.parts[-1])
                yield

            def norm(s):
                dve.wait_ge(S["std_ready"], s.std + 1)
                src = x[:, s.src[1], :]
                step(dve.reciprocal(rstd[:, 0:1], std[:, 0:1]))
                signal("h_ready", dve.tensor_scalar(h_tile, src, rstd[:, 0:1], None, ALU.mult))
                yield

            def heads(s):
                for n, tok in enumerate(s.tiles):
                    yield
                    dve.wait_ge(S["qk_copied"], s.copied + n + 1)
                    v8 = qk_raw.rearrange("p (g n) -> p g n", n=QK)
                    signal("qk_summed", dve.tensor_reduce(sumsq[:], qk_sq.rearrange("p (g n) -> p g n", n=QK), AX.X, ALU.add))
                    dve.wait_ge(S["std_ready"], s.std + n + 1)
                    step(dve.reciprocal(rstd[:], std[:]))
                    step(dve.tensor_tensor(v8, v8, rstd[:, :, None].to_broadcast([P, 8, QK]), ALU.mult))
                    gain = gains[:, 0 if s.name == "q" else 1, None, :].to_broadcast([P, 8, QK])
                    rot = qk_rot.rearrange("p (g n) -> p g n", n=QK)
                    if n:
                        t = s.turn[n - 1]
                        dve.wait_ge(full[t.bank], t.full_after[0])
                    if tok < CTX // P:
                        signal("qk_rotated", dve.tensor_tensor(rot, v8, gain, ALU.mult))
                        yield
                        continue
                    b = tok - CTX // P
                    step(dve.tensor_tensor(v8, v8, gain, ALU.mult))
                    issue(dve.tensor_tensor(rot, v8, rope_cos[:, b, None, :].to_broadcast([P, 8, QK]), ALU.mult))
                    halves = qk_raw.rearrange("p (g a r f) -> p g a r f", a=2, r=2, f=QK // 4)
                    other = qk_sq.rearrange("p (g a r f) -> p g a r f", a=2, r=2, f=QK // 4)
                    sines = rope_sin[:, b, :].rearrange("p (a r f) -> p a r f", a=2, r=2)
                    for r in range(2):
                        issue(dve.tensor_tensor(other[:, :, :, r, :], halves[:, :, :, 1 - r, :],
                                                sines[:, None, :, r, :].to_broadcast([P, 8, 2, QK // 4]), ALU.mult))
                    settle()
                    signal("qk_rotated", dve.tensor_tensor(qk_rot, qk_rot, qk_sq, ALU.add))
                    yield
                yield

            def gating(s):
                for _ in range(3):
                    yield
                t = s.vt
                dve.wait_ge(full[t.bank], t.full_after[0])
                step(dve.bn_stats(stats[:, 0, :], tile_ap(t, 512)))
                signal("var_ready", dve.bn_aggr(meanvar[:], stats[:, 0, :]))
                dve.wait_ge(S["std_ready"], s.std + 1)
                step(dve.reciprocal(rstd[:, 0:1], std[:, 0:1]))
                step(dve.tensor_scalar(vn_tile, tile_ap(t, 512), meanvar[:, 0:1], rstd[:, 0:1], ALU.subtract, ALU.mult))
                dve.sem_inc(free[t.bank], 1)
                step(dve.tensor_tensor(vn_tile, vn_tile, vn_gain[:, 0, :], ALU.mult))
                signal("vn_ready", dve.tensor_tensor(vn_tile, vn_tile, vn_gain[:, 1, :], ALU.add))
                yield
                dve.wait_ge(S["u_ready"], s.u_ready + 1)
                t = s.mt
                dve.wait_ge(full[t.bank], t.full_after[0])
                for g in range(GROUPS):
                    cols = slice(g * P, (g + 1) * P)
                    issue(dve.scalar_tensor_tensor(out=cat[:, HEADS * VD + g * P:HEADS * VD + (g + 1) * P],
                                                   in0=tile_ap(t, 512)[:, cols], scalar=sgu_bias[:, g:g + 1],
                                                   in1=u_tile[:, cols], op0=ALU.add, op1=ALU.mult))
                settle()
                dve.sem_inc(free[t.bank], 1)
                yield

            def attend(s):
                def peaks(h):
                    for c in range(2):
                        t = s.score[h][c]
                        dve.wait_ge(full[t.bank], t.full_after[1])
                        step(dve.tensor_reduce(peak[:, h % 2, c:c + 1], tile_ap(t, KEYS), AX.X, ALU.max))
                        signal("max_ready", dve.tensor_scalar(neg_peak[:, h % 2, c:c + 1], peak[:, h % 2, c:c + 1], -SCALE, None, ALU.mult))

                def combine(h):
                    e = h % 2
                    dve.wait_ge(S["exp_ready"], s.exp + 2 * h + 2)
                    step(dve.reciprocal(inv_sum[:, e, :], expsum[:, e, :]))
                    issue(dve.tensor_scalar(inv_sum[:, e, 1:2], inv_sum[:, e, 1:2], neg_lam[:], None, ALU.mult))
                    issue(dve.tensor_scalar(probs[e][0], probs[e][0], inv_sum[:, e, 0:1], None, ALU.mult))
                    settle()
                    signal("probs_ready", dve.scalar_tensor_tensor(
                        out=probs[e][0], in0=probs[e][1], scalar=inv_sum[:, e, 1:2], in1=probs[e][0],
                        op0=ALU.mult, op1=ALU.add))

                peaks(0)
                combine(0)
                yield
                for h in range(HEADS):
                    if h + 1 < HEADS:
                        peaks(h + 1)
                        combine(h + 1)
                    yield
                    yield
                dve.wait_ge(S["o_ready"], s.o + HEADS)
                step(dve.tensor_tensor(o_sq, o_tile, o_tile, ALU.mult))
                signal("o_summed", dve.tensor_reduce(sumsq[:, 0:HEADS], o_sq.rearrange("p (h n) -> p h n", h=HEADS), AX.X, ALU.add))
                dve.wait_ge(S["std_ready"], s.std + 1)
                step(dve.reciprocal(rstd[:, 0:HEADS], std[:, 0:HEADS]))
                o3 = o_tile.rearrange("p (h n) -> p h n", h=HEADS)
                step(dve.tensor_tensor(o3, o3, rstd[:, 0:HEADS, None].to_broadcast([P, HEADS, VD]), ALU.mult))
                signal("cat_ready", dve.tensor_tensor(cat[:, 0:HEADS * VD].rearrange("p (h n) -> p h n", h=HEADS), o3,
                                                      subln[:, None, :].to_broadcast([P, HEADS, VD]), ALU.mult))
                yield

            def project(s):
                for _ in range(len(s.cost) - 1):
                    yield
                t = s.tile
                dve.wait_ge(full[t.bank], t.full_after[-1])
                dve.wait_ge(S["row_ready"], s.rows)
                step(dve.tensor_tensor(h_tile, tile_ap(t, 1024), g1_row[:], ALU.mult))
                dve.sem_inc(free[t.bank], 1)
                signal("x_updated", dve.tensor_tensor(x[:, s.b, :], x[:, s.b, :], h_tile, ALU.add))
                yield

            def conv_in(s):
                if s.b == 0:
                    dve.memset(z_t[:, :, 0:PAD], 0.0)
                    dve.memset(z_t[:, :, PAD + SEQ:], 0.0)
                for j in range(4):
                    for _ in range(3):
                        yield
                    if j % 2:
                        t = s.out[j]
                        dve.wait_ge(full[t.bank], t.full_after[0])
                        dve.wait_ge(S["sig_ready"], s.sig + j // 2 + 1)
                        for g in range(4):
                            k, cols = 4 * (j // 2) + g, slice(2 * g * P, 2 * (g + 1) * P)
                            issue(dve.scalar_tensor_tensor(out=z_t[:, k, PAD + s.b * P:PAD + (s.b + 2) * P],
                                                           in0=tile_ap(t, 1024)[:, cols], scalar=pw1_bias[:, 0, k:k + 1],
                                                           in1=sig[:, cols], op0=ALU.add, op1=ALU.mult))
                        settle()
                        dve.sem_inc(free[t.bank], 1)
                        dve.sem_inc(S["z_ready"], 1)
                    yield

            def conv(s):
                base = s.conv * TAPS * KD
                for k in range(KD):
                    dve.tensor_scalar(acc[:, k, :], z_t[:, k, s.b * P:(s.b + 1) * P], taps[:, k, 0:1], conv_par[:, 0, k:k + 1],
                                      ALU.mult, ALU.add).then_inc(taps_done, 1)
                for lo, hi in TAP_RUNS:
                    for w in range(lo, hi):
                        dve.wait_ge(taps_done, base + w * KD)
                        for k in range(KD):
                            dve.scalar_tensor_tensor(out=acc[:, k, :], in0=z_t[:, k, w + s.b * P:w + (s.b + 1) * P],
                                                     scalar=taps[:, k, w:w + 1], in1=acc[:, k, :],
                                                     op0=ALU.mult, op1=ALU.add).then_inc(taps_done, 1)
                    if hi == TAPS:
                        dve.wait_ge(taps_done, base + TAPS * KD)
                        dve.sem_inc(S["conv_done"], 1)
                    yield
                t = s.there
                dve.wait_ge(full[t.bank], t.full_after[0])
                issue(dve.bn_stats(stats[:, 0, :], tile_ap(t, 1024)[:, 0:512]))
                step(dve.bn_stats(stats[:, 1, :], tile_ap(t, 1024)[:, 512:1024]))
                signal("var_ready", dve.bn_aggr(meanvar[:], stats[:].rearrange("p a n -> p (a n)")))
                dve.wait_ge(S["std_ready"], s.std + 1)
                step(dve.reciprocal(rstd[:, 0:1], std[:, 0:1]))
                step(dve.tensor_scalar(cn_tile, tile_ap(t, 1024), meanvar[:, 0:1], rstd[:, 0:1], ALU.subtract, ALU.mult))
                dve.sem_inc(free[t.bank], 1)
                dve.sem_inc(S["cn_ready"], 1)
                yield

            def best8(values, where, row_of, rows):
                for g in rows:
                    issue(dve.max(values[:, g, 0:8], row_of(g)))
                settle()
                for g in rows:
                    issue(dve.max_index(where[:, g, 0:8], values[:, g, 0:8], row_of(g)))
                    issue(dve.match_replace(row_of(g), values[:, g, 0:8], row_of(g), LOW))
                settle()

            def next8(values, where, row_of, rows):
                for g in rows:
                    issue(dve.max(values[:, g, 8:16], row_of(g)))
                settle()
                for g in rows:
                    issue(dve.max_index(where[:, g, 8:16], values[:, g, 8:16], row_of(g)))
                settle()

            def select(s):
                def pairs(half):
                    sides = top_v[:, 8 * half:8 * half + 8, :].rearrange("p (h two) n -> p h two n", two=2)
                    issue(dve.tensor_copy(top_f[:, 8 * half:8 * half + 8, :], top_i[:, 8 * half:8 * half + 8, :]))
                    step(dve.tensor_tensor(cand[:, 4 * half:4 * half + 4, :].rearrange("p h (a b) -> p h a b", a=TOPK),
                                           sides[:, :, 0, :, None].to_broadcast([P, PH // 2, TOPK, TOPK]),
                                           sides[:, :, 1, None, :].to_broadcast([P, PH // 2, TOPK, TOPK]), ALU.add))

                def shares(half):
                    heads, slots = slice(4 * half, 4 * half + 4), slice(64 * half, 64 * half + 64)
                    issue(dve.tensor_copy(gate_sum[:, heads], best_v[:, heads, 0]))
                    pos = best_p[:, heads, :].rearrange("p h n -> p (h n)")
                    issue(dve.tensor_scalar(part_u[:, 0, slots], pos, 4, None, ALU.logical_shift_right))
                    issue(dve.tensor_scalar(part_u[:, 1, slots], pos, TOPK - 1, None, ALU.bitwise_and))
                    settle()
                    issue(dve.tensor_copy(part_f[:, :, slots], part_u[:, :, slots]))
                    signal("cand_ready", dve.tensor_tensor(best_v[:, heads, :], best_v[:, heads, :],
                                                           gate_sum[:, heads, None].to_broadcast([P, PH // 2, TOPK]), ALU.subtract))
                    settle()

                def numbers(half, side):
                    slots, hot = slice(64 * half, 64 * half + 64), onehot
                    step(dve.tensor_tensor(hot, part_f[:, side, slots, None].to_broadcast([P, 64, TOPK]),
                                           iota16[:, None, :].to_broadcast([P, 64, TOPK]), ALU.is_equal))
                    view = hot.rearrange("p (h s) n -> p h s n", h=PH // 2)
                    listed = top_f[:, 8 * half:8 * half + 8, :].rearrange("p (h two) n -> p h two n", two=2)[:, :, side, None, :]
                    step(dve.tensor_tensor(view, view, listed.to_broadcast([P, PH // 2, TOPK, TOPK]), ALU.mult))
                    step(dve.tensor_reduce(part_f[:, side, slots], hot, AX.X, ALU.add))

                def combine(half):
                    heads, slots = slice(4 * half, 4 * half + 4), slice(64 * half, 64 * half + 64)
                    step(dve.scalar_tensor_tensor(out=part_f[:, 0, slots], in0=part_f[:, 0, slots], scalar=float(N_KEYS),
                                                  in1=part_f[:, 1, slots], op0=ALU.mult, op1=ALU.add))
                    issue(dve.tensor_scalar(expert[:, s.b % 2, slots], part_f[:, 0, slots], float(s.layer * N_EXPERTS), None, ALU.add))
                    dve.wait_ge(S["gate_exp"], s.exp + half + 1)
                    step(dve.tensor_reduce(gate_sum[:, heads], best_v[:, heads, :], AX.X, ALU.add))
                    step(dve.reciprocal(gate_sum[:, heads], gate_sum[:, heads]))
                    issue(dve.tensor_tensor(gate[:, s.b % 2, slots].rearrange("p (h n) -> p h n", h=PH // 2), best_v[:, heads, :],
                                            gate_sum[:, heads, None].to_broadcast([P, PH // 2, TOPK]), ALU.mult))
                    settle()

                for _ in range(5):
                    yield
                for half in range(2):
                    if half:
                        yield
                    dve.wait_ge(S["scores_ready"], s.sc + half + 1)
                    lists, heads = range(8 * half, 8 * half + 8), range(4 * half, 4 * half + 4)
                    best8(top_v, top_i, lambda g: scores[:, g, :], lists)
                    yield
                    next8(top_v, top_i, lambda g: scores[:, g, :], lists)
                    pairs(half)
                    yield
                    best8(best_v, best_p, lambda h: cand[:, h, :], heads)
                    yield
                    next8(best_v, best_p, lambda h: cand[:, h, :], heads)
                    shares(half)
                    for side in range(2):
                        yield
                        numbers(half, side)
                    yield
                    combine(half)
                    dve.sem_inc(S["topk_ready"], 1)
                yield

            def gather(s):
                base = s.index * ITERS * NG
                par = s.b % 2
                dve.wait_ge(S["topk_ready"], 2 * s.index + (1 if s.last <= ITERS * NG // 2 else 2))
                dve.wait_ge(S["h2_ready"], s.index + 1)

                def dot(i, g):
                    for k in range(g * GROUP, (g + 1) * GROUP):
                        dve.wait_ge(slot_landed[k], i * 16 + 16 * (s.index * ITERS + 1))
                        ins = dve.tensor_tensor_reduce(out=ring[:, k, 0:D], in0=ring[:, k, 0:D], in1=h2[:, par, :], scale=1.0,
                                                       scalar=0.0, op0=ALU.mult, op1=ALU.add, accum_out=dots[:, k:k + 1])
                    ins.then_inc(dots_ready, 1)

                def slot(i, k):
                    return slice(i * RING + k, i * RING + k + 1) if isinstance(i, int) else bass.ds(i * RING + k, 1)

                def weigh(i, g):
                    dve.wait_ge(acts_ready, i * NG + (base + g + 1))
                    for k in range(g * GROUP, (g + 1) * GROUP):
                        ins = dve.tensor_scalar(diag[:, k, :], ident[:], acts[:, k:k + 1],
                                                gate[:, par, slot(i, k)], ALU.mult, ALU.mult)
                    ins.then_inc(diag_ready, 1)

                if s.last - s.first == 1:
                    i, g = s.first // NG, s.first % NG
                    dot(i, g)
                    weigh(i, g)
                else:
                    with dve.Fori(s.first // NG, s.last // NG) as i:
                        for g in range(NG):
                            dot(i, g)
                            if g:
                                weigh(i, g - 1)
                        weigh(i, NG - 1)
                yield

            def finish(s):
                dve.wait_ge(slots_free, (s.index + 1) * ITERS * NG + NG)
                dve.wait_ge(S["row_ready"], s.rows)
                product = h2[:, s.b % 2, :]
                step(dve.tensor_tensor(product, ffn_out, g2_row[:], ALU.mult))
                dve.sem_inc(sums_read, 1)
                signal("x_updated", dve.tensor_tensor(x[:, s.b, :], x[:, s.b, :], product, ALU.add))
                yield

            run_phases({"ada": ada, "side_ada": side_ada, "front_norms": front_norms, "lam": lam, "norm": norm, "heads": heads, "gating": gating, "attend": attend, "project": project,
                        "conv_in": conv_in, "conv": conv, "select": select, "gather": gather, "finish": finish}, "others")

        @block.tensor
        def _(pe):
            def claim(t):
                if t.frees_before:
                    pe.wait_ge(free[t.bank], t.frees_before)

            def turn(t, src, n):
                claim(t)
                for k in range(n):
                    ins = pe.transpose(psum[:, t.bank, k * P:(k + 1) * P], src[:, k * P:(k + 1) * P], ident[:])
                ins.then_inc(full[t.bank], 1)

            def rows(dst, column, start, stop):
                for k in range(KD):
                    ins = pe.matmul(dst[:, k * P:(k + 1) * P], column(k).to_broadcast([P, P]), ident[:], start=start and k % 4 == 0,
                                    stop=stop, skip_group_check=True)
                return ins

            def linear(t, part, left, c, begin=True):
                pe.wait_ge(landed[c.buf], c.landed)
                if part == 0 and begin:
                    claim(t)
                dst = psum[:, t.bank, part * COLS:(part + 1) * COLS]
                for k in range(KD):
                    if k == KD // 2:
                        yield
                    ins = pe.matmul(dst, left[:, k, :], buffers[c.buf][:, k, :], start=k == 0 and begin, stop=k == KD - 1,
                                    skip_group_check=not begin)
                ins.then_inc(full[t.bank], 1)

            def linear_t(t, part, right, c):
                pe.wait_ge(landed[c.buf], c.landed)
                if part == 0:
                    claim(t)
                for g in range(COLS // P):
                    if g == 2:
                        yield
                    dst = psum[:, t.bank, part * COLS + g * P:part * COLS + (g + 1) * P]
                    for k in range(KD):
                        ins = pe.matmul(dst, buffers[c.buf][:, k, g * P:(g + 1) * P], right[:, k, :], start=k == 0, stop=k == KD - 1)
                ins.then_inc(full[t.bank], 1)

            def ada(s):
                pe.wait_ge(cond_act, 1)
                for sec, chunks, line, column, modded in s.parts:
                    for j in range(2):
                        c = chunks[j]
                        pe.wait_ge(landed[c.buf], c.landed)
                        if j == 0:
                            claim(line)
                        for k in range(KD):
                            ins = pe.matmul(psum[0:2, line.bank, j * COLS:(j + 1) * COLS], cond_silu[:, :, k], buffers[c.buf][:, k, :],
                                            start=k == 0, stop=k == KD - 1)
                        ins.then_inc(full[line.bank], 1)
                        yield
                    pe.wait_ge(S["line_ready"], modded + 1)
                    claim(column)
                    for k in range(KD):
                        ins = pe.matmul(psum[:, column.bank, 2 * k:2 * k + 2], mod_line[:, k * P:(k + 1) * P], ident[0:2, 0:2],
                                        start=True, stop=True)
                    ins.then_inc(full[column.bank], 1)
                    yield

            def side_ada(s):
                for _ in range(5):
                    yield
                n = s.parts[0][2][0].last_use[1]
                for p, (layer, sec, chunks, t, is_row) in enumerate(s.parts):
                    for j in range(2):
                        acc_j = mod_acc[2 * (p % 2) + j]
                        pe.wait_ge(S["acc_ready"], n)
                        n += 1
                        if j == 0:
                            claim(t)
                            if is_row:
                                rows(tile_of(t), lambda k: ada_bias[:, layer, sec, k:k + 1], True, False)
                        if is_row:
                            ins = pe.matmul(psum[:, t.bank, j * COLS:(j + 1) * COLS], ones[:], acc_j, start=False, stop=True,
                                            skip_group_check=True)
                        else:
                            for g in range(COLS // P):
                                col = 2 * (j * (COLS // P) + g)
                                ins = pe.matmul(psum[:, t.bank, col:col + 2], acc_j[:, g * P:(g + 1) * P], ones[:, 0:2],
                                                start=True, stop=True)
                        ins.then_inc(full[t.bank], 1)
                        yield
                        yield

            def front_norms(s):
                yield
                for t in range(NT):
                    pe.wait_ge(S["h_ready"], s.h + t + 1)
                    turn(s.tile[t], front_h[t], KD)
                yield

            def lam(s):
                pe.wait_ge(params, 16 * N_PARAMS)
                yield

            def gate_row(s):
                pe.wait_ge(S["mod_ready"], s.mods)
                claim(s.tile)
                rows(tile_of(s.tile), lambda k: mod[:, s.layer, s.which, k:k + 1], True, True).then_inc(full[s.tile.bank], 1)
                yield

            def tile_of(t):
                return psum[:, t.bank, :]

            def norm(s):
                yield
                pe.wait_ge(S["h_ready"], s.h + 1)
                turn(s.tile, h_tile, KD)
                yield
                if s.dest:
                    pe.wait_ge(S["ht_ready"], s.ht + 1)
                    turn(s.back, h_t.rearrange("p k n -> p (k n)"), KD)
                yield

            def heads(s):
                def turned(n):
                    pe.wait_ge(S["qk_rotated"], s.turned + n + 1)
                    turn(s.turn[n], qk_rot, HEADS)

                pe.wait_ge(S["ht_ready"], s.ht)
                for n in range(len(s.tiles)):
                    yield from linear(s.proj[n], 0, ht_all[:, s.tiles[n]] if s.name == "k" else h_t, s.chunk)
                    if n:
                        turned(n - 1)
                    yield
                turned(len(s.tiles) - 1)
                yield

            def values(s):
                for n, tok in enumerate(s.tiles):
                    yield from linear(s.proj[n], 0, ht_all[:, tok], s.chunk)
                    yield

            def gating(s):
                yield from linear(s.ut, 0, h_t, s.u)
                yield
                yield from linear(s.vt, 0, h_t, s.vg)
                yield
                pe.wait_ge(S["vn_ready"], s.vn + 1)
                claim(s.mt)
                for g in range(GROUPS):
                    ins = pe.matmul(psum[:, s.mt.bank, g * P:(g + 1) * P], sgu_t[:, g, :], vn_tile[:, g * P:(g + 1) * P],
                                    start=True, stop=True)
                ins.then_inc(full[s.mt.bank], 1)
                yield

            def attend(s):
                pe.wait_ge(S["qkt_ready"], s.qkt)
                pe.wait_ge(S["v_ready"], s.v)

                def score(h):
                    for c in range(2):
                        t = s.score[h][c]
                        claim(t)
                        r = slice(c * QK, (c + 1) * QK)
                        for lo, hi in ((0, COLS), (COLS, KEYS)):
                            pe.matmul(psum[:, t.bank, lo:hi], q_t[r, h, :], k_t[r, h, lo:hi], start=True, stop=True).then_inc(
                                full[t.bank], 1)

                score(0)
                yield
                for h in range(HEADS):
                    if h + 1 < HEADS:
                        score(h + 1)
                    pe.wait_ge(S["probs_ready"], s.mix + h + 1)
                    turn(s.turn[h], probs[h % 2][0], NT)
                    yield
                    pe.wait_ge(S["probst_ready"], s.pt + h + 1)
                    t = s.out[h]
                    claim(t)
                    for kt in range(NT):
                        ins = pe.matmul(psum[:, t.bank, 0:VD], probs_t[:, kt, :], v_all[:, kt, h * VD:(h + 1) * VD],
                                        start=kt == 0, stop=kt == NT - 1)
                    ins.then_inc(full[t.bank], 1)
                    yield

            def project(s):
                if s.which == "even":
                    pe.wait_ge(S["cat_ready"], s.cat)
                    turn(s.turn, cat, KD)
                    yield
                    pe.wait_ge(S["left_ready"], s.left + 1)
                    left = h_t
                else:
                    pe.wait_ge(S["left_ready"], s.left_before)
                    left = cn_t
                    claim(s.tile)
                    rows(tile_of(s.tile), lambda k: conv_par[:, 3, k:k + 1], True, False)
                for j in range(2):
                    yield from linear(s.tile, j, left, s.chunks[j], begin=s.which == "even")
                    yield

            def conv_in(s):
                pe.wait_ge(S["ht_ready"], s.ht)
                for j in range(4):
                    c, t = s.chunks[j], s.out[j]
                    pe.wait_ge(landed[c.buf], c.landed)
                    claim(t)
                    for g in range(COLS // P):
                        for k in range(KD):
                            ins = pe.matmul(psum[:, t.bank, 2 * g * P:2 * (g + 1) * P], buffers[c.buf][:, k, g * P:(g + 1) * P],
                                            h_pair[:, k, :], start=k == 0, stop=k == KD - 1)
                        if g == COLS // P - 1:
                            ins.then_inc(full[t.bank], 1)
                        yield

            def conv(s):
                for _ in TAP_RUNS:
                    yield
                pe.wait_ge(S["conv_done"], s.conv + 1)
                turn(s.there, acc.rearrange("p k n -> p (k n)"), KD)
                yield
                pe.wait_ge(S["cn_ready"], s.cn + 1)
                turn(s.back, cn_tile, KD)
                yield

            def select(s):
                pe.wait_ge(S["ht_ready"], s.ht)
                for half in range(2):
                    for j in range(2):
                        yield from linear_t(s.q[half], j, h_t, s.chunks[2 * half + j])
                        yield
                    c = s.keys[half]
                    pe.wait_ge(landed[c.buf], c.landed)
                    keys = buffers[c.buf].rearrange("p k n -> p (k n)")
                    pe.wait_ge(S["pq_ready"], s.qt + half + 1)
                    t = s.s[half]
                    claim(t)
                    for g in range(8):
                        ins = pe.matmul(psum[:, t.bank, g * P:(g + 1) * P], pq_t[:, 8 * half + g, :], keys[:, g * P:(g + 1) * P],
                                        start=True, stop=True)
                        if g % 4 == 3:
                            ins.then_inc(full[t.bank], 1)
                    yield

            def gather(s):
                base = s.index * ITERS * NG
                if s.first == 0:
                    if s.index:
                        pe.wait_ge(sums_read, s.index)
                    else:
                        pe.wait_ge(free[Plan.DUOS], plan.uses[Plan.DUOS])
                    pe.wait_ge(S["h2_ready"], s.index + 1)
                    for n in range(2):
                        pe.matmul(ffn_out[:, n * COLS:(n + 1) * COLS], zero_row[:], h2[0:1, s.b % 2, 0:COLS], start=True, stop=True)
                def add_up(i, g):
                    pe.wait_ge(diag_ready, i * NG + (base + g + 1))
                    for k in range(g * GROUP, (g + 1) * GROUP):
                        for n in range(2):
                            ins = pe.matmul(ffn_out[:, n * COLS:(n + 1) * COLS], diag[:, k, :],
                                            ring[:, k, D + n * COLS:D + (n + 1) * COLS], start=False, stop=True,
                                            skip_group_check=True)
                    ins.then_inc(slots_free, 1)

                if s.last - s.first == 1:
                    add_up(s.first // NG, s.first % NG)
                else:
                    with pe.Fori(s.first // NG, s.last // NG) as i:
                        for g in range(NG):
                            add_up(i, g)
                yield

            pe.sem_inc(slots_free, NG)
            pe.wait_ge(first_params, 32)
            pe.wait_ge(consts, 3)
            run_phases({"ada": ada, "side_ada": side_ada, "front_norms": front_norms, "lam": lam, "norm": norm, "heads": heads, "values": values, "gate_row": gate_row, "gating": gating, "attend": attend,
                        "project": project, "conv_in": conv_in, "conv": conv, "select": select, "gather": gather}, "pe")


def layouts(np_, i):
    def chunked(w):
        return w.reshape(KD, P, -1, COLS).transpose(2, 1, 0, 3).reshape(-1, P, KD * COLS)

    f = np_.float32
    keys = i["peer_keys"].reshape(LAYERS, 2 * PH, N_KEYS, P).transpose(3, 0, 1, 2).reshape(1, P, 2 * 2048)
    chunks = np_.concatenate([
        chunked(i["ada_w"][0]), chunked(i["ada_w"][1]), chunked(i["ev_w_in"][0]), chunked(i["ev_w_out"][0]),
        chunked(i["od_pw1_w"][0]), chunked(i["od_pw2_w"][0]), chunked(i["peer_wq"][0]), chunked(i["peer_wq"][1]), keys])
    n = np_.arange(SEQ)
    grid = np_.stack([n // 64, n % 64], 1).astype(f)
    inv = (10000.0 ** (-np_.arange(QK // 4, dtype=f) / (QK // 4))).astype(f)
    ang = (grid[:, :, None] * inv).astype(f)
    cos = np_.stack([np_.cos(ang)] * 2, 2).reshape(SEQ, QK).astype(f)
    sin = np_.stack([-np_.sin(ang), np_.sin(ang)], 2).reshape(SEQ, QK).astype(f)

    def blocks(a):
        return a.reshape(NB, P, -1).transpose(1, 0, 2)

    def columns(a):
        return a.reshape(-1, KD, P).transpose(2, 0, 1)

    return {
        "x": i["x"][0], "ctx": i["ctx"][0],
        "cond": columns(np_.stack([i["c"][0], i["c_ctx"]])),
        "ident": np_.eye(P, dtype=f),
        "iota16": np_.tile(np_.arange(TOPK, dtype=f), (P, 1)),
        "rope_cos": blocks(cos), "rope_sin": blocks(sin),
        "gains": np_.stack([i["ev_q_gain"][0], i["ev_k_gain"][0]]),
        "lam": i["ev_lam"][0], "subln": i["ev_subln_g"][0],
        "vn_gain": np_.stack([i["ev_vnorm_g"][0], i["ev_vnorm_b"][0]]),
        "sgu_t": i["ev_sgu_w"][0].transpose(2, 0, 1), "sgu_bias": i["ev_sgu_b"][0].T,
        "taps": i["od_dw_w"][0].reshape(TAPS, KD, P).transpose(2, 1, 0),
        "conv_par": columns(np_.concatenate([i["od_dw_b"][0], i["od_ln_g"][0], i["od_ln_b"][0], i["od_pw2_b"][0], i["od_pw1_b"][0]])),
        "ada_bias": columns(i["ada_b"]).reshape(P, LAYERS, 6, KD),
        "chunks": chunks,
        "experts": np_.concatenate([i["peer_down"], i["peer_up"]], axis=2).reshape(LAYERS * N_EXPERTS, 2 * D),
    }


def kernel(**inputs):
    import concourse.bacc as bacc
    from concourse.bass_utils import run_bass_kernel_spmd

    laid = layouts(np, {k: np.asarray(v) for k, v in inputs.items()})
    nc = bacc.Bacc("TRN2", target_bir_lowering=False, num_devices=1)
    arrays, aps = {}, {}
    for name, a in laid.items():
        a = np.ascontiguousarray(a)
        arrays[f"in_{name}"] = a
        aps[name] = nc.dram_tensor(f"in_{name}", a.shape, mybir.dt.from_np(a.dtype), kind="ExternalInput").ap()
    out = nc.dram_tensor("out_x", (SEQ, D), F32, kind="ExternalOutput").ap()
    trunk_kernel(nc, aps, out)
    r = run_bass_kernel_spmd(nc, [arrays], core_ids=[0])
    return np.asarray(r.results[0]["out_x"]).reshape(1, SEQ, D)
```
